# Optimizing a Trainium2 kernel written in Bass

```python
import jax, jax.numpy as jnp
from jax import lax
import numpy as np

D_MODEL = 1024
BATCH = 1
SEQ = 2048
DEPTH = 2

GRID_W = 64
CTX_LEN = 256
N_EVEN = (DEPTH + 1) // 2
N_ODD = DEPTH // 2
NORM_EPS = 1e-6

MLA_HEADS = 8
QK_NOPE = 64
QK_ROPE = 32
QK_HEAD = QK_NOPE + QK_ROPE
V_HEAD = 64
Q_LORA = 384
KV_LORA = 256
ROPE_FREQS = QK_ROPE // 4
ROPE_BASE = 10000.0
Q_BLOCK = 128
MLA_WIDTH = MLA_HEADS * V_HEAD
FNET_GROUPS = 4
FNET_GROUP_DIM = 128
FNET_WIDTH = FNET_GROUPS * FNET_GROUP_DIM
EVEN_WIDTH = MLA_WIDTH + FNET_WIDTH
E_KR0 = KV_LORA
E_Q0 = KV_LORA + QK_ROPE
E_F0 = E_Q0 + Q_LORA
E_G0 = E_F0 + FNET_WIDTH
EVEN_IN = E_G0 + EVEN_WIDTH
RWKV_HEAD = 64
RWKV_WIDTH = D_MODEL
RWKV_HEADS = RWKV_WIDTH // RWKV_HEAD
DECAY_LORA = 64
AAA_LORA = 64
N_DIR = 2
GN_EPS = 64e-5
SHIFT_W = 3
O_V0 = RWKV_WIDTH
O_WD0 = 2 * RWKV_WIDTH
O_AD0 = O_WD0 + N_DIR * DECAY_LORA
O_R0 = O_AD0 + N_DIR * AAA_LORA
STATE_CH = O_R0
CONV_CH = O_R0 + RWKV_WIDTH
ODD_IN = CONV_CH + RWKV_WIDTH

kernel_name = 'hybrid_mla_fnet_rwkv7_dit'

def rms_norm(x, g):
    x32 = x.astype(jnp.float32)
    y = x32 * lax.rsqrt(jnp.mean(x32 * x32, axis=-1, keepdims=True) + NORM_EPS)
    return (y * g.astype(jnp.float32)).astype(x.dtype)

def ada_chunks(cond, w, b, n):
    m = jax.nn.silu(cond) @ w[:, :n * D_MODEL] + b[:n * D_MODEL]
    return [m[..., i * D_MODEL:(i + 1) * D_MODEL] for i in range(n)]

def axial_rope(rows):
    row = jnp.repeat(jnp.arange(rows, dtype=jnp.float32), GRID_W)
    col = jnp.tile(jnp.arange(GRID_W, dtype=jnp.float32), rows)
    inv = 1.0 / (ROPE_BASE ** (jnp.arange(ROPE_FREQS, dtype=jnp.float32) / ROPE_FREQS))
    ang = jnp.stack([row[:, None] * inv, col[:, None] * inv], axis=1)
    return jnp.cos(ang), jnp.sin(ang)

def apply_rope_tail(x, cos, sin):
    b, t, h, _ = x.shape
    xp = x[..., QK_NOPE:].reshape(b, t, h, 2, 2, ROPE_FREQS)
    x1, x2 = xp[..., 0, :], xp[..., 1, :]
    cs = cos[None, :, None].astype(x.dtype)
    sn = sin[None, :, None].astype(x.dtype)
    rot = jnp.stack([x1 * cs - x2 * sn, x2 * cs + x1 * sn], axis=-2).reshape(b, t, h, QK_ROPE)
    return jnp.concatenate([x[..., :QK_NOPE], rot], axis=-1)

def mla_kv(u, kv_norm, w_ukv, k_head_norm, rope):
    b, t, _ = u.shape
    ckv = rms_norm(u[..., :KV_LORA], kv_norm)
    kv = (ckv @ w_ukv).reshape(b, t, MLA_HEADS, QK_NOPE + V_HEAD)
    k_pe = jnp.broadcast_to(u[..., E_KR0:E_Q0][:, :, None, :], (b, t, MLA_HEADS, QK_ROPE))
    k = rms_norm(jnp.concatenate([kv[..., :QK_NOPE], k_pe], axis=-1), k_head_norm)
    if rope is not None:
        k = apply_rope_tail(k, *rope)
    return k, kv[..., QK_NOPE:]

def mla_q(u, q_norm, w_uq, q_head_norm, rope):
    b, t, _ = u.shape
    cq = rms_norm(u[..., E_Q0:E_F0], q_norm)
    q = rms_norm((cq @ w_uq).reshape(b, t, MLA_HEADS, QK_HEAD), q_head_norm)
    if rope is not None:
        q = apply_rope_tail(q, *rope)
    return q

def attend_context(q, k, v):
    b, t, h, _ = q.shape
    s = jnp.einsum('bqhe,bkhe->bhqk', q, k).astype(jnp.float32) * (QK_HEAD ** -0.5)
    p = jax.nn.softmax(s, axis=-1).astype(v.dtype)
    return jnp.einsum('bhqk,bkhd->bqhd', p, v).reshape(b, t, h * V_HEAD)

def attend_latent(q, k_lat, v_lat, k_ctx, v_ctx):
    b, n, h, _ = q.shape
    nb = n // Q_BLOCK
    qb = q.reshape(b, nb, Q_BLOCK, h, QK_HEAD).transpose(1, 0, 3, 2, 4)
    kl = k_lat.transpose(0, 2, 1, 3)
    vl = v_lat.transpose(0, 2, 1, 3)
    kc = k_ctx.transpose(0, 2, 1, 3)
    vc = v_ctx.transpose(0, 2, 1, 3)

    def one_block(qi):
        s = jnp.concatenate([jnp.einsum('bhqe,bhke->bhqk', qi, kl),
                             jnp.einsum('bhqe,bhke->bhqk', qi, kc)], axis=-1)
        p = jax.nn.softmax(s.astype(jnp.float32) * (QK_HEAD ** -0.5), axis=-1).astype(vl.dtype)
        return (jnp.einsum('bhqk,bhkd->bhqd', p[..., :n], vl)
                + jnp.einsum('bhqk,bhkd->bhqd', p[..., n:], vc))

    o = lax.map(one_block, qb)
    return o.transpose(1, 0, 3, 2, 4).reshape(b, n, h * V_HEAD)

def fourier_mix(u, w_fnet):
    b, t, _ = u.shape
    ug = u.reshape(b, t, FNET_GROUPS, FNET_GROUP_DIM).astype(jnp.float32)
    f = jnp.fft.fft2(ug, axes=(1, 3), norm='ortho').real.astype(u.dtype)
    return jnp.einsum('btgc,gcd->btgd', f, w_fnet).reshape(b, t, FNET_WIDTH)

def even_mixer(h_lat, h_ctx, rope, need_ctx, w_in, kv_norm, q_norm, w_uq, w_ukv,
               q_head_norm, k_head_norm, w_fnet, w_out):
    u_lat = h_lat @ w_in
    u_ctx = h_ctx @ (w_in if need_ctx else w_in[:, :E_Q0])
    k_c, v_c = mla_kv(u_ctx, kv_norm, w_ukv, k_head_norm, None)
    k_l, v_l = mla_kv(u_lat, kv_norm, w_ukv, k_head_norm, rope)
    q_l = mla_q(u_lat, q_norm, w_uq, q_head_norm, rope)

    def merge(o, u):
        mix = jnp.concatenate([o, fourier_mix(u[..., E_F0:E_G0], w_fnet)], axis=-1)
        return (mix * jax.nn.silu(u[..., E_G0:])) @ w_out

    y_lat = merge(attend_latent(q_l, k_l, v_l, k_c, v_c), u_lat)
    y_ctx = None
    if need_ctx:
        q_c = mla_q(u_ctx, q_norm, w_uq, q_head_norm, None)
        y_ctx = merge(attend_context(q_c, k_c, v_c), u_ctx)
    return y_lat, y_ctx

def token_shift(z, w):
    zp = jnp.pad(z, ((0, 0), (1, 1), (0, 0)))
    return w[0] * zp[:, :-2] + w[1] * z + w[2] * zp[:, 2:]

def rwkv_scan(w, k, v, kk, a, r, s0, reverse):
    seqs = [jnp.moveaxis(t_, 1, 0) for t_ in (w, k, v, kk, a)]
    if r is not None:
        seqs.append(jnp.moveaxis(r, 1, 0))

    def step(s, inp):
        w_t, k_t, v_t, kk_t, a_t = inp[:5]
        sa = jnp.einsum('bhvk,bhk->bhv', s, kk_t)
        s = (s * w_t[:, :, None, :]
             - sa[..., None] * (kk_t * a_t)[:, :, None, :]
             + v_t[..., None] * k_t[:, :, None, :])
        y = jnp.einsum('bhvk,bhk->bhv', s, inp[5]) if len(inp) > 5 else None
        return s, y

    s_fin, ys = lax.scan(step, s0, tuple(seqs), reverse=reverse)
    return s_fin, (None if r is None else jnp.moveaxis(ys, 0, 1))

def head_group_norm(y, w, b):
    bsz, t, _, _ = y.shape
    mu = jnp.mean(y, axis=-1, keepdims=True)
    var = jnp.mean(jnp.square(y - mu), axis=-1, keepdims=True)
    yn = ((y - mu) * lax.rsqrt(var + GN_EPS)).reshape(bsz, t, RWKV_WIDTH)
    return yn * w + b

def rwkv_time_mix(z, gate, s0, w0, w2, a0, a2, k_k, k_a, r_k, gn_w, gn_b, w_out, with_out):
    b, t, _ = z.shape
    heads = lambda a_: a_.reshape(b, t, RWKV_HEADS, RWKV_HEAD)
    z32 = z.astype(jnp.float32)
    k = z32[..., :O_V0]
    v = heads(z32[..., O_V0:O_WD0])
    wd = z32[..., O_WD0:O_AD0].reshape(b, t, N_DIR, DECAY_LORA)
    ad = z32[..., O_AD0:STATE_CH].reshape(b, t, N_DIR, AAA_LORA)
    w_raw = w0 + jnp.einsum('btzr,zrc->btzc', jnp.tanh(wd), w2)
    decay = jnp.exp(-jnp.exp(-jax.nn.softplus(-w_raw) - 0.5))
    a = jax.nn.sigmoid(a0 + jnp.einsum('btzr,zrc->btzc', ad, a2))
    kk = heads(k * k_k)
    kk = kk / jnp.maximum(jnp.sqrt(jnp.sum(kk * kk, axis=-1, keepdims=True)), 1e-12)
    k_dir = k[:, :, None, :] * (1.0 + (a - 1.0) * k_a)
    r = heads(z32[..., O_R0:CONV_CH]) if with_out else None
    finals, outs, bonuses = [], [], []
    for d in range(N_DIR):
        kd = heads(k_dir[:, :, d])
        s_fin, ys = rwkv_scan(heads(decay[:, :, d]), kd, v, kk, heads(a[:, :, d]), r, s0[d], d == 1)
        finals.append(s_fin)
        if with_out:
            outs.append(ys)
            bonuses.append(jnp.sum(r * kd * r_k, axis=-1, keepdims=True) * v)
    if not with_out:
        return None, finals
    o = head_group_norm(outs[0] + outs[1], gn_w, gn_b) + (bonuses[0] + bonuses[1]).reshape(b, t, RWKV_WIDTH)
    return (o.astype(gate.dtype) * jax.nn.silu(gate)) @ w_out, finals

def odd_mixer(h_lat, h_ctx, need_ctx, w_in, shift_w, w0, w2, a0, a2, k_k, k_a, r_k, gn_w, gn_b, w_out):
    bsz = h_ctx.shape[0]
    s_zero = jnp.zeros((bsz, RWKV_HEADS, RWKV_HEAD, RWKV_HEAD), jnp.float32)
    if need_ctx:
        u_ctx = h_ctx @ w_in
        y_ctx, s_ctx = rwkv_time_mix(token_shift(u_ctx[..., :CONV_CH], shift_w), u_ctx[..., CONV_CH:],
                                     (s_zero, s_zero), w0, w2, a0, a2, k_k, k_a, r_k, gn_w, gn_b, w_out, True)
    else:
        u_ctx = h_ctx @ w_in[:, :STATE_CH]
        y_ctx, s_ctx = rwkv_time_mix(token_shift(u_ctx, shift_w[:, :STATE_CH]), None,
                                     (s_zero, s_zero), w0, w2, a0, a2, k_k, k_a, r_k, gn_w, gn_b, w_out, False)
    u_lat = h_lat @ w_in
    y_lat, _ = rwkv_time_mix(token_shift(u_lat[..., :CONV_CH], shift_w), u_lat[..., CONV_CH:],
                             s_ctx, w0, w2, a0, a2, k_k, k_a, r_k, gn_w, gn_b, w_out, True)
    return y_lat, y_ctx

def setup_inputs(seed: int = 0) -> dict:
    key = jax.random.key(seed)
    ks = iter(list(jax.random.split(key, 40)))
    nrm = lambda shape, scale: jax.random.normal(next(ks), shape, jnp.float32) * scale
    D = D_MODEL
    W = RWKV_WIDTH
    return {
        'x': nrm((BATCH, SEQ, D), 1.0),
        'c': nrm((BATCH, D), 1.0),
        'ctx': nrm((BATCH, CTX_LEN, D), 1.0),
        'c_ctx': nrm((D,), 1.0),
        'ada_w': nrm((DEPTH, D, 3 * D), 0.5 * D ** -0.5),
        'ada_b': nrm((DEPTH, 3 * D), 0.02),
        'norm_g': 1.0 + nrm((DEPTH, D), 0.02),
        'e_w_in': nrm((N_EVEN, D, EVEN_IN), D ** -0.5),
        'e_kv_norm': 1.0 + nrm((N_EVEN, KV_LORA), 0.02),
        'e_q_norm': 1.0 + nrm((N_EVEN, Q_LORA), 0.02),
        'e_w_uq': nrm((N_EVEN, Q_LORA, MLA_HEADS * QK_HEAD), Q_LORA ** -0.5),
        'e_w_ukv': nrm((N_EVEN, KV_LORA, MLA_HEADS * (QK_NOPE + V_HEAD)), KV_LORA ** -0.5),
        'e_q_head_norm': 1.0 + nrm((N_EVEN, QK_HEAD), 0.02),
        'e_k_head_norm': 1.0 + nrm((N_EVEN, QK_HEAD), 0.02),
        'e_w_fnet': nrm((N_EVEN, FNET_GROUPS, FNET_GROUP_DIM, FNET_GROUP_DIM), FNET_GROUP_DIM ** -0.5),
        'e_w_out': nrm((N_EVEN, EVEN_WIDTH, D), EVEN_WIDTH ** -0.5),
        'o_w_in': nrm((N_ODD, D, ODD_IN), D ** -0.5),
        'o_shift_w': jnp.array([0.3, 1.0, 0.3], jnp.float32)[None, :, None] + nrm((N_ODD, SHIFT_W, CONV_CH), 0.05),
        'o_w0': jnp.linspace(-5.0, -1.0, W, dtype=jnp.float32)[None, None, :] + nrm((N_ODD, N_DIR, W), 0.3),
        'o_w2': nrm((N_ODD, N_DIR, DECAY_LORA, W), 0.1 * DECAY_LORA ** -0.5),
        'o_a0': nrm((N_ODD, N_DIR, W), 0.1),
        'o_a2': nrm((N_ODD, N_DIR, AAA_LORA, W), AAA_LORA ** -0.5),
        'o_k_k': 0.85 + nrm((N_ODD, W), 0.02),
        'o_k_a': 1.0 + nrm((N_ODD, W), 0.02),
        'o_r_k': nrm((N_ODD, RWKV_HEADS, RWKV_HEAD), 0.1),
        'o_gn_w': 1.0 + nrm((N_ODD, W), 0.02),
        'o_gn_b': nrm((N_ODD, W), 0.02),
        'o_w_out': nrm((N_ODD, W, D), W ** -0.5),
    }

def reference(x, c, ctx, c_ctx, ada_w, ada_b, norm_g, e_w_in, e_kv_norm, e_q_norm, e_w_uq, e_w_ukv,
              e_q_head_norm, e_k_head_norm, e_w_fnet, e_w_out, o_w_in, o_shift_w, o_w0, o_w2, o_a0,
              o_a2, o_k_k, o_k_a, o_r_k, o_gn_w, o_gn_b, o_w_out):
    rows = x.shape[1] // GRID_W
    rope = axial_rope(rows)
    cond_lat = c[:, None, :]
    cond_ctx = c_ctx[None, None, :]
    for layer in range(DEPTH):
        need_ctx = layer < DEPTH - 1
        shift_l, scale_l, gate_l = ada_chunks(cond_lat, ada_w[layer], ada_b[layer], 3)
        mod_c = ada_chunks(cond_ctx, ada_w[layer], ada_b[layer], 3 if need_ctx else 2)
        h_lat = rms_norm(x, norm_g[layer]) * (1.0 + scale_l) + shift_l
        h_ctx = rms_norm(ctx, norm_g[layer]) * (1.0 + mod_c[1]) + mod_c[0]
        j = layer // 2
        if layer % 2 == 0:
            y_lat, y_ctx = even_mixer(h_lat, h_ctx, rope, need_ctx, e_w_in[j], e_kv_norm[j], e_q_norm[j],
                                      e_w_uq[j], e_w_ukv[j], e_q_head_norm[j], e_k_head_norm[j],
                                      e_w_fnet[j], e_w_out[j])
        else:
            y_lat, y_ctx = odd_mixer(h_lat, h_ctx, need_ctx, o_w_in[j], o_shift_w[j], o_w0[j], o_w2[j],
                                     o_a0[j], o_a2[j], o_k_k[j], o_k_a[j], o_r_k[j], o_gn_w[j],
                                     o_gn_b[j], o_w_out[j])
        x = x + gate_l * y_lat
        if need_ctx:
            ctx = ctx + mod_c[2] * y_ctx
    return x


_drawn_inputs = setup_inputs


def setup_inputs(seed=0):
    import zlib

    import numpy as np

    out = dict(_drawn_inputs(seed))
    spreads = {}
    factors = {'ctx': 3.198,
     'c_ctx': 4.871,
     'norm_g': 4.021,
     'e_kv_norm': 8.0,
     'e_q_norm': 8.0,
     'e_w_uq': 5.604,
     'e_q_head_norm': 8.0,
     'e_k_head_norm': 8.0,
     'o_w2': 64.0,
     'o_a0': 5.751,
     'o_k_k': 58.776,
     'o_k_a': 5.524,
     'o_gn_w': 64.0,
     'o_gn_b': 64.0,
     'o_w0': 5.186}
    for name, (base, spread) in spreads.items():
        noise = np.random.default_rng([zlib.crc32(name.encode()), seed]).standard_normal(out[name].shape)
        drawn = base * np.exp(spread * noise) if base else spread * noise
        out[name] = __import__('jax').numpy.asarray(drawn.astype(out[name].dtype))
    for name, factor in factors.items():
        out[name] = (out[name] * factor).astype(out[name].dtype)
    return out
```

```python
from contextlib import ExitStack

import numpy as np

import concourse.bass as bass
from concourse import mybir

F32 = mybir.dt.float32
BF16 = mybir.dt.bfloat16
I32 = mybir.dt.int32
ALU = mybir.AluOpType
ACT = mybir.ActivationFunctionType
AX = mybir.AxisListType

P = 128
D = 1024
SEQ = 2048
CTX = 256
T = CTX + SEQ
NT = T // P
NC_CTX = CTX // P
KD = D // P
EPS = 1e-6

HEADS = 8
NOPE = 64
ROPE = 32
QK = NOPE + ROPE
VH = 64
QL = 384
KVL = 256
KVQ = KVL + ROPE + QL
FG = 4
FD = 128
FW = FG * FD
GW = HEADS * VH + FW
E_Q0 = KVL + ROPE
E_F0 = E_Q0 + QL
E_G0 = E_F0 + FW
EVEN_IN = E_G0 + GW
GRID_W = 64
N2 = SEQ // P


def constant_tables():
    k = np.arange(P)
    ang = 2 * np.pi * np.outer(k, k) / FD
    norm = 1.0 / np.sqrt(SEQ * FD)
    chan = np.stack([np.cos(ang), np.sin(ang)], 1) * norm
    n1, k1 = np.arange(P), np.arange(P)
    t = np.arange(N2)[None, :, None] + N2 * n1[:, None, None]
    a1 = 2 * np.pi * (t * k1[None, None, :] % SEQ) / SEQ
    step1 = np.stack([np.cos(a1), np.sin(a1), -np.sin(a1)], 2)
    a2 = 2 * np.pi * np.outer(np.arange(N2), np.arange(N2)) / N2
    eye8 = np.eye(P // N2)
    step2 = np.stack([np.kron(np.cos(a2), eye8), -np.kron(np.sin(a2), eye8)], 1)
    tc = np.arange(CTX)
    ac = 2 * np.pi * np.outer(tc, tc) / CTX
    up = np.sqrt(SEQ / CTX)
    ctxdft = np.stack([np.cos(ac) * up, -np.sin(ac) * up], 1)
    ctxdft = ctxdft.reshape(CTX // P, P, 2, CTX).transpose(1, 0, 2, 3)
    nf = ROPE // 4
    pos = np.arange(SEQ)
    inv = 1.0 / (10000.0 ** (np.arange(nf) / nf))
    angle = np.stack([(pos // GRID_W)[:, None] * inv, (pos % GRID_W)[:, None] * inv], 1)
    cos = np.concatenate([np.ones((CTX, 2, nf)), np.cos(angle)])
    sin = np.concatenate([np.zeros((CTX, 2, nf)), np.sin(angle)])
    rope = np.concatenate([np.stack([cos, cos], 2).reshape(T, -1), np.stack([-sin, sin], 2).reshape(T, -1)], 1)
    f = np.float32
    return {
        "ident": np.eye(P, dtype=f), "chan": chan.astype(f), "step1": step1.astype(f), "step2": step2.astype(f),
        "ctxdft": ctxdft.astype(f), "rope": rope.astype(f),
    } | rwkv_tables()


HP = 64
C = 64
GT = 256
NG = T // GT
NCH = GT // C
PAIRS = D // P
KAPPA = float(np.exp(-0.5))
GN_EPS = 64e-5
SHIFT_ROWS = 3
O_WD0 = 2 * D
O_AD0 = O_WD0 + P
O_R0 = O_AD0 + P
O_G0 = O_R0 + D


def rwkv_tables():
    s = np.arange(P)
    head = s // C
    same = head[:, None] == head[None, :]
    si, ti = s[:, None] % C, s[None, :] % C
    out = {}
    masks = []
    for before in (si < ti, si > ti):
        masks.append(np.stack([same & before, same & (before | (si == ti))], 1))
    out["tri"] = np.stack(masks, 1).astype(np.float32)
    lev = []
    for order in (0, 1):
        for b in range(6):
            lo, hi = (ti, si) if order == 0 else (si, ti)
            late, early = lo, hi
            lev.append(same & (si >> (b + 1) == ti >> (b + 1)) & ((late >> b) % 2 == 1) & ((early >> b) % 2 == 0))
    out["level"] = np.stack(lev, 1).reshape(P, 2, 6, P).astype(np.int32)
    out["same"] = same.astype(np.float32)
    z = np.ones((P, 2, GT), np.float32)
    z[:, 0, ::C] = 0
    z[:, 1, C - 1::C] = 0
    out["reset"] = z
    n = np.arange(PAIRS * NG)
    out["flag"] = np.broadcast_to((n % NG != 0).astype(np.float32), (P, PAIRS * NG)).copy()
    return out


class Core:

    def __init__(self, nc, stack, tag):
        self.nc, self.stack, self.tag = nc, stack, tag

    def sb(self, name, shape, dt=F32):
        return self.stack.enter_context(self.nc.sbuf_tensor(f"{self.tag}_{name}", shape, dt))

    def ps(self, name, shape, dt=F32):
        return self.stack.enter_context(self.nc.psum_tensor(f"{self.tag}_{name}", shape, dt))


class Link:

    def __init__(self, eng, sem, base=0):
        self.eng, self.sem, self.base, self.n = eng, sem, base, 0

    def __call__(self, ins):
        self.n += 1
        ins.then_inc(self.sem, 1)
        self.eng.wait_ge(self.sem, self.base + self.n)


def settle(eng, sem):
    eng.sem_inc(sem, 1)


def modulate(nc, sem, keep, A):
    with ExitStack() as stack:
        core = Core(nc, stack, "mod")
        HALF = 3 * D // 2
        MH = HALF // P
        w = core.sb("w", [P, 2, KD, HALF])
        cond = core.sb("cond", [P, KD, 2])
        act = core.sb("act", [P, KD, 2])
        bias = core.sb("bias", [P, 2, 3 * KD])
        norm_g = core.sb("norm_g", [P, 2, KD])
        mod = core.sb("mod", [P, 2, 3 * KD, 2])
        diag = core.sb("diag", [P, 3, KD, P])
        ones = core.sb("ones", [P, P])
        acc = core.ps("acc", [P, 2 * 3 * KD, 2])
        rows = [core.ps(f"rows{i}", [P, 512]) for i in range(2)]
        small, wload = sem("mod_small_loaded"), [sem(f"mod_w{i}_loaded") for i in range(2)]
        silu_done, mm_done, added = sem("mod_silu_done"), sem("mod_mm_done"), sem("mod_added")
        diag_done, row_mm, row_out, set_up = sem("mod_diag"), sem("mod_row_mm"), sem("mod_row_out"), sem("mod_setup")

        with nc.Block() as block:
            @block.sync
            def _(sp):
                with nc.allow_non_contiguous_dma("short vectors as columns"):
                    sp.dma_start(cond[:, :, 0], A["c"].rearrange("a (k p) -> p (a k)", p=P)).then_inc(small, 16)
                    sp.dma_start(cond[:, :, 1], A["c_ctx"].rearrange("(k p) -> p k", p=P)).then_inc(small, 16)
                    for layer in range(2):
                        sp.dma_start(bias[:, layer, :], A["ada_b"][layer].rearrange("(m p) -> p m", p=P)).then_inc(small, 16)
                        sp.dma_start(norm_g[:, layer, :], A["norm_g"][layer].rearrange("(k p) -> p k", p=P)).then_inc(small, 16)
                sp.dma_start(keep["ident"][:], A["ident"]).then_inc(small, 16)
                for n in range(4):
                    layer, half = divmod(n, 2)
                    if n >= 2:
                        sp.wait_ge(mm_done, n - 1)
                    sp.dma_start(w[:, n % 2], A["ada_w"][layer, :, half * HALF:(half + 1) * HALF]
                                 .rearrange("(k p) n -> p k n", p=P)).then_inc(wload[n % 2], 16)

            @block.scalar
            def _(a):
                a.wait_ge(small, 7 * 16)
                nc.scalar.activation(act[:], cond[:], ACT.Silu).then_inc(silu_done, 1)
                for i in range(6):
                    a.wait_ge(row_mm, i + 1)
                    nc.scalar.copy(keep["gate"][:, i // 2, (i % 2) * 512:(i % 2 + 1) * 512], rows[i % 2][:]).then_inc(row_out, 1)

            @block.tensor
            def _(pe):
                pe.wait_ge(silu_done, 1)
                for n in range(4):
                    pe.wait_ge(wload[n % 2], 16 * (n // 2 + 1))
                    for m in range(MH):
                        for k in range(KD):
                            last = pe.matmul(acc[:, n * MH + m, :], w[:, n % 2, k, m * P:(m + 1) * P], act[:, k, :],
                                             start=(k == 0), stop=(k == KD - 1))
                    last.then_inc(mm_done, 1)
                pe.wait_ge(diag_done, 3 * KD)
                pe.wait_ge(set_up, 1)
                for i in range(6):
                    if i >= 2:
                        pe.wait_ge(row_out, i - 1)
                    pe.matmul(rows[i % 2][:], ones[:], diag[:, i // 2, (i % 2) * 4:(i % 2) * 4 + 4, :]
                              .rearrange("p a b -> p (a b)"), start=True, stop=True).then_inc(row_mm, 1)

            @block.vector
            def _(v):
                nc.vector.memset(ones[:], 1.0).then_inc(set_up, 1)
                v.wait_ge(mm_done, 4)
                v.wait_ge(small, 7 * 16)
                psum = acc[:].rearrange("p (l m) s -> p l m s", l=2)
                for s in range(2):
                    nc.vector.tensor_tensor(mod[:, :, :, s], psum[:, :, :, s], bias[:], ALU.add).then_inc(added, 1)
                v.wait_ge(added, 2)
                for s in range(2):
                    nc.vector.scalar_tensor_tensor(out=keep["scale"][:, :, :, s], in0=mod[:, :, KD:2 * KD, s], scalar=1.0,
                                                   in1=norm_g[:], op0=ALU.add, op1=ALU.mult)
                    nc.vector.tensor_copy(keep["shift"][:, :, :, s], mod[:, :, 0:KD, s])
                for i, (layer, s) in enumerate(((0, 0), (0, 1), (1, 0))):
                    for k in range(KD):
                        nc.vector.tensor_scalar(diag[:, i, k, :], keep["ident"][:], mod[:, layer, 2 * KD + k, s:s + 1],
                                                None, ALU.mult).then_inc(diag_done, 1)


def project0(nc, sem, keep, A, W):
    with ExitStack() as stack:
        core = Core(nc, stack, "p0")
        w_in = core.sb("w_in", [P, KD, EVEN_IN])
        w_ukv = core.sb("w_ukv", [P, 2, HEADS * 128])
        w_uq = core.sb("w_uq", [P, 3, HEADS * QK])
        w_fn = core.sb("w_fn", [P, FG, FD])
        chan = core.sb("chan", [P, 2, FD])
        m_fn = core.sb("m_fn", [P, FG, 2 * FD])
        kvn = core.sb("kvn", [P, 2])
        qn = core.sb("qn", [P, 3])
        gk = core.sb("gk", [P, 2, QK])
        half = core.sb("half", [P, 32])
        xt = core.sb("xt", [P, 2, D])
        xsq = core.sb("xsq", [P, D])
        xss = core.sb("xss", [P, 1])
        xms = core.sb("xms", [P, 1])
        xr = core.sb("xr", [P, 1])
        xn = core.sb("xn", [P, D])
        hT = core.sb("hT", [P, 2, KD, P])
        rope = core.sb("rope", [P, 2, 2 * ROPE])
        lss = core.sb("lss", [P, 2])
        lms = core.sb("lms", [P, 2])
        lr = core.sb("lr", [P, 2])
        lsq = core.sb("lsq", [P, KVL + QL])
        ckv = core.sb("ckv", [P, KVL])
        cq = core.sb("cq", [P, QL])
        kpe = core.sb("kpe", [P, ROPE])
        ckvT = core.sb("ckvT", [P, 2, P])
        cqT = core.sb("cqT", [P, 3, P])
        fT = core.sb("fT", [P, FG, P])
        qk = [core.sb(f"{n}_heads", [P, HEADS, QK]) for n in "qk"]
        hsq = core.sb("hsq", [P, HEADS, QK])
        hss = core.sb("hss", [P, HEADS])
        hms = core.sb("hms", [P, HEADS])
        hr = core.sb("hr", [P, HEADS])
        rc = core.sb("rc", [P, HEADS, ROPE])
        rs = core.sb("rs", [P, HEADS, ROPE])
        vt = core.sb("vt", [P, HEADS, VH])
        gt = core.sb("gt", [P, GW])
        fx = core.sb("fx", [P, 2, FG, FD])

        bIn = core.ps("bIn", [P, 2, 512])
        bG = core.ps("bG", [P, 2, 512])
        bF = core.ps("bF", [P, 512])
        bT = core.ps("bT", [P, 512])
        bX = core.ps("bX", [P, 2, 512])

        w_loaded, c_loaded = sem("p0_w_loaded"), sem("p0_consts_loaded")
        x_loaded = [sem(f"p0_x_loaded{i}") for i in range(2)]
        rope_loaded = [sem(f"p0_rope_loaded{i}") for i in range(2)]
        prep, m_mm, m_out = sem("p0_prep"), sem("p0_m_mm"), sem("p0_m_out")
        x_sq, x_ms, x_rs, x_n = sem("p0_x_sq"), sem("p0_x_ms"), sem("p0_x_rs"), sem("p0_x_normed")
        x_tr, x_hT = sem("p0_x_transposed"), sem("p0_hT_ready")
        in_kvq, in_gate, in_f = sem("p0_kvq_mm"), sem("p0_gate_mm"), sem("p0_f_mm")
        l_sq, l_ms, l_rs, l_n = sem("p0_l_sq"), sem("p0_l_ms"), sem("p0_l_rs"), sem("p0_l_normed")
        l_tr, l_T = sem("p0_l_transposed"), sem("p0_lT_ready")
        f_T, fx_mm, fx_out, fx_st = sem("p0_fT"), sem("p0_fx_mm"), sem("p0_fx_out"), sem("p0_fx_stored")
        kv_mm, q_mm, v_out, v_st = sem("p0_kv_mm"), sem("p0_q_mm"), sem("p0_v_out"), sem("p0_v_stored")
        k_out, q_out, kpe_out = sem("p0_k_out"), sem("p0_q_out"), sem("p0_kpe_out")
        g_out, g_st = sem("p0_gate_out"), sem("p0_gate_stored")
        h_ms, h_rs, h_done, h_st = sem("p0_h_ms"), sem("p0_h_rs"), sem("p0_head_done"), sem("p0_head_stored")
        dchain, pchain = sem("p0_dve_chain"), sem("p0_pool_chain")
        LINKS = 22

        with nc.Block() as block:
            @block.sync
            def _(sp):
                with nc.allow_non_contiguous_dma("short vectors as columns"):
                    sp.dma_start(kvn[:], A["e_kv_norm"][0].rearrange("(k p) -> p k", p=P)).then_inc(c_loaded, 16)
                    sp.dma_start(qn[:], A["e_q_norm"][0].rearrange("(k p) -> p k", p=P)).then_inc(c_loaded, 16)
                    sp.dma_start(gk[:, 0, :], A["e_q_head_norm"].broadcast_to([P, QK])).then_inc(c_loaded, 16)
                    sp.dma_start(gk[:, 1, :], A["e_k_head_norm"].broadcast_to([P, QK])).then_inc(c_loaded, 16)
                sp.dma_start(w_ukv[:], A["e_w_ukv"][0].rearrange("(k p) n -> p k n", p=P)).then_inc(c_loaded, 16)
                sp.dma_start(w_uq[:], A["e_w_uq"][0].rearrange("(k p) n -> p k n", p=P)).then_inc(c_loaded, 16)
                sp.dma_start(w_fn[:], A["e_w_fnet"][0].rearrange("g c d -> c g d")).then_inc(c_loaded, 16)
                sp.dma_start(chan[:], A["chan"]).then_inc(c_loaded, 16)
                for i in range(2):
                    sp.dma_start(xt[:, i, :], A["ctx"][0, i * P:(i + 1) * P, :]).then_inc(x_loaded[i], 16)
                    sp.dma_start(rope[:, i, :], A["rope"][i * P:(i + 1) * P, :]).then_inc(rope_loaded[i], 16)
                sp.dma_start(w_in[:], A["e_w_in"][0].rearrange("(k p) n -> p k n", p=P)).then_inc(w_loaded, 16)

                def store(t):
                    rows = slice(t * P, (t + 1) * P) if isinstance(t, int) else bass.ds(t * P, P)
                    sp.wait_ge(g_out, t + 1)
                    sp.dma_start(W["gate"][rows, :], gt[:]).then_inc(g_st, 16)
                    sp.wait_ge(fx_out, 2 * t + 2)
                    sp.dma_start(W["fx"][rows, :], fx[:].rearrange("p r g c -> p (r g c)")).then_inc(fx_st, 16)
                    sp.wait_ge(v_out, 2 * t + 2)
                    sp.dma_start(W["v"][:, rows, :].rearrange("h p d -> p h d"), vt[:]).then_inc(v_st, 16)
                    for j, name in enumerate("qk"):
                        sp.wait_ge(h_done, 2 * t + j + 1)
                        sp.dma_start(W[name][:, rows, :].rearrange("h p d -> p h d"), qk[j][:]).then_inc(h_st, 16)

                with sp.Fori(0, NT // 2 - 1) as i:
                    for s in range(2):
                        t = 2 * i + s
                        sp.wait_ge(x_n, t + 1)
                        sp.dma_start(xt[:, s, :], A["x"][0, bass.ds(t * P, P), :]).then_inc(x_loaded[s], 16)
                        store(t)
                        sp.dma_start(rope[:, s, :], A["rope"][bass.ds((t + 2) * P, P), :]).then_inc(rope_loaded[s], 16)
                store(NT - 2)
                store(NT - 1)
                sp.wait_ge(g_st, 16 * NT)
                sp.wait_ge(fx_st, 16 * NT)
                sp.wait_ge(v_st, 16 * NT)
                sp.wait_ge(h_st, 32 * NT)

            @block.gpsimd
            def _(g):
                nc.gpsimd.memset(half[:], -0.5).then_inc(pchain, 1)
                g.wait_ge(pchain, 1)

                def rsqrt(out, ms, n):
                    return nc.gpsimd.tensor_tensor(out, ms, half[:, 0:n], ALU.pow)

                g.wait_ge(x_ms, 1)
                rsqrt(xr[:], xms[:], 1).then_inc(x_rs, 1)
                with g.Fori(0, NT - 1) as t:
                    g.wait_ge(x_ms, t + 2)
                    g.wait_ge(x_n, t + 1)
                    rsqrt(xr[:], xms[:], 1).then_inc(x_rs, 1)
                    g.wait_ge(l_ms, t + 1)
                    g.wait_ge(l_n, 2 * t)
                    rsqrt(lr[:], lms[:], 2).then_inc(l_rs, 1)
                    for j in range(2):
                        g.wait_ge(h_ms, 2 * t + j + 1)
                        rsqrt(hr[:], hms[:], HEADS).then_inc(h_rs, 1)
                g.wait_ge(l_ms, NT)
                g.wait_ge(l_n, 2 * NT - 2)
                rsqrt(lr[:], lms[:], 2).then_inc(l_rs, 1)
                for j in range(2):
                    g.wait_ge(h_ms, 2 * NT - 1 + j)
                    rsqrt(hr[:], hms[:], HEADS).then_inc(h_rs, 1)

            @block.tensor
            def _(pe):
                ident = keep["ident"]
                pe.wait_ge(c_loaded, 8 * 16)
                for g in range(FG):
                    for j in range(2):
                        last = pe.matmul(bG[:, g // 2, (g % 2 * 2 + j) * FD:(g % 2 * 2 + j + 1) * FD], chan[:, j, :],
                                         w_fn[:, g, :], start=True, stop=True)
                last.then_inc(m_mm, 1)

                def transpose_x():
                    for k in range(KD):
                        last = pe.transpose(bX[:, k // 4, (k % 4) * P:(k % 4 + 1) * P], xn[:, k * P:(k + 1) * P], ident[:])
                    last.then_inc(x_tr, 1)

                def tile(t, s, more):
                    pe.wait_ge(x_hT, t + 1)
                    pe.wait_ge(q_out, t)
                    for k in range(KD):
                        pe.matmul(bIn[:, 0, 0:E_Q0], hT[:, s, k, :], w_in[:, k, 0:E_Q0], start=(k == 0), stop=(k == KD - 1))
                    for k in range(KD):
                        last = pe.matmul(bIn[:, 1, 0:QL], hT[:, s, k, :], w_in[:, k, E_Q0:E_F0], start=(k == 0), stop=(k == KD - 1))
                    last.then_inc(in_kvq, 1)
                    pe.wait_ge(fx_out, 2 * t)
                    for j in range(2):
                        for k in range(KD):
                            last = pe.matmul(bG[:, j, :], hT[:, s, k, :], w_in[:, k, E_G0 + 512 * j:E_G0 + 512 * (j + 1)],
                                             start=(k == 0), stop=(k == KD - 1))
                    last.then_inc(in_gate, 1)
                    if more:
                        pe.wait_ge(x_n, t + 2)
                        pe.wait_ge(k_out, t)
                        pe.wait_ge(v_out, 2 * t)
                        transpose_x()
                    pe.wait_ge(f_T, t)
                    for g in range(FG):
                        for k in range(KD):
                            last = pe.matmul(bF[:, g * P:(g + 1) * P], w_in[:, k, E_F0 + g * FD:E_F0 + (g + 1) * FD],
                                             hT[:, s, k, :], start=(k == 0), stop=(k == KD - 1))
                    last.then_inc(in_f, 1)
                    pe.wait_ge(l_n, 2 * t + 2)
                    for k in range(2):
                        pe.transpose(bT[:, k * P:(k + 1) * P], ckv[:, k * P:(k + 1) * P], ident[:])
                    for k in range(2):
                        pe.transpose(bT[:, (2 + k) * P:(3 + k) * P], cq[:, k * P:(k + 1) * P], ident[:])
                    pe.transpose(bIn[:, 1, QL:512], cq[:, 2 * P:3 * P], ident[:]).then_inc(l_tr, 1)
                    pe.wait_ge(f_T, t + 1)
                    pe.wait_ge(g_out, t + 1)
                    for g in range(FG):
                        last = pe.matmul(bG[:, g // 2, (g % 2) * 256:(g % 2 + 1) * 256], fT[:, g, :],
                                         m_fn[:, g, :], start=True, stop=True)
                    last.then_inc(fx_mm, 1)
                    pe.wait_ge(l_T, 2 * t + 2)
                    pe.wait_ge(kpe_out, t + 1)
                    for j in range(2):
                        for k in range(3):
                            n = 512 if j == 0 else HEADS * QK - 512
                            last = pe.matmul(bIn[:, j, 0:n], cqT[:, k, :], w_uq[:, k, 512 * j:512 * j + n],
                                             start=(k == 0), stop=(k == 2))
                    last.then_inc(q_mm, 1)
                    if more:
                        pe.wait_ge(x_hT, t + 2)
                    for j in range(2):
                        for k in range(2):
                            last = pe.matmul(bX[:, j, :], ckvT[:, k, :], w_ukv[:, k, 512 * j:512 * (j + 1)],
                                             start=(k == 0), stop=(k == 1))
                    last.then_inc(kv_mm, 1)

                pe.wait_ge(x_n, 1)
                transpose_x()
                pe.wait_ge(w_loaded, 16)
                pe.wait_ge(prep, 2)
                pe.wait_ge(m_out, 1)
                with pe.Fori(0, NT // 2 - 1) as i:
                    tile(2 * i, 0, True)
                    tile(2 * i + 1, 1, True)
                tile(NT - 2, 0, True)
                pe.wait_ge(k_out, NT - 1)
                pe.wait_ge(v_out, 2 * NT - 2)
                tile(NT - 1, 1, False)

            @block.scalar
            def _(a):
                def x_squares(t, s, loaded):
                    a.wait_ge(x_loaded[s], loaded)
                    a.wait_ge(x_ms, t)
                    nc.scalar.activation(xsq[:], xt[:, s, :], ACT.Square, accum_out=xss[:]).then_inc(x_sq, 1)

                def modulated(t, s, stream):
                    a.wait_ge(x_tr, t + 1)
                    for k in range(KD):
                        last = nc.scalar.activation(hT[:, s, k, :], bX[:, k // 4, (k % 4) * P:(k % 4 + 1) * P], ACT.Identity,
                                                    scale=keep["scale"][:, 0, k, stream:stream + 1],
                                                    bias=keep["shift"][:, 0, k, stream:stream + 1])
                    last.then_inc(x_hT, 1)

                def tile(t, s, next_stream, loaded):
                    if loaded is not None:
                        x_squares(t + 1, 1 - s, loaded)
                    a.wait_ge(in_kvq, t + 1)
                    a.wait_ge(l_ms, t)
                    nc.scalar.activation(lsq[:, 0:KVL], bIn[:, 0, 0:KVL], ACT.Square, scale=KVL ** -0.5,
                                         accum_out=lss[:, 0:1]).then_inc(l_sq, 1)
                    nc.scalar.activation(lsq[:, KVL:], bIn[:, 1, 0:QL], ACT.Square, scale=QL ** -0.5,
                                         accum_out=lss[:, 1:2]).then_inc(l_sq, 1)
                    a.wait_ge(in_gate, t + 1)
                    a.wait_ge(g_st, 16 * t)
                    nc.scalar.activation(gt[:], bG[:].rearrange("p a b -> p (a b)"), ACT.Silu).then_inc(g_out, 1)
                    if loaded is not None:
                        modulated(t + 1, 1 - s, next_stream)
                    a.wait_ge(l_tr, t + 1)
                    nc.scalar.copy(ckvT[:].rearrange("p a b -> p (a b)"), bT[:, 0:256])
                    nc.scalar.copy(cqT[:, 0:2, :].rearrange("p a b -> p (a b)"), bT[:, 256:512]).then_inc(l_T, 1)
                    nc.scalar.copy(cqT[:, 2, :], bIn[:, 1, QL:512]).then_inc(l_T, 1)
                    a.wait_ge(fx_mm, t + 1)
                    a.wait_ge(fx_st, 16 * t)
                    for j in range(2):
                        nc.scalar.copy(fx[:, :, 2 * j:2 * j + 2, :].rearrange("p r g c -> p g r c"),
                                       bG[:, j, :].rearrange("p (g r c) -> p g r c", g=2, r=2)).then_inc(fx_out, 1)
                    a.wait_ge(k_out, t + 1)
                    a.wait_ge(v_st, 16 * t)
                    for j in range(2):
                        nc.scalar.copy(vt[:, 4 * j:4 * j + 4, :],
                                       bX[:, j, :].rearrange("p (h d) -> p h d", h=4)[:, :, NOPE:]).then_inc(v_out, 1)

                x_squares(0, 0, 16)
                modulated(0, 0, 1)
                tile(0, 0, 1, 16)
                tile(1, 1, 0, 32)
                with a.Fori(1, NT // 2 - 1) as i:
                    tile(2 * i, 0, 0, 16 * i + 16)
                    tile(2 * i + 1, 1, 0, 16 * i + 32)
                tile(NT - 2, 0, 0, 16 * (NT // 2))
                tile(NT - 1, 1, 0, None)

            @block.vector
            def _(v):
                v.wait_ge(c_loaded, 8 * 16)
                for k in range(2):
                    last = nc.vector.tensor_scalar(w_ukv[:, k, :], w_ukv[:, k, :], kvn[:, k:k + 1], None, ALU.mult)
                last.then_inc(prep, 1)
                for k in range(3):
                    last = nc.vector.tensor_scalar(w_uq[:, k, :], w_uq[:, k, :], qn[:, k:k + 1], None, ALU.mult)
                last.then_inc(prep, 1)
                v.wait_ge(m_mm, 1)
                nc.vector.tensor_copy(m_fn[:].rearrange("p g c -> p (g c)"), bG[:].rearrange("p a b -> p (a b)")).then_inc(m_out, 1)

                def x_norm(t, s):
                    v.wait_ge(x_sq, t + 1)
                    v.wait_ge(x_rs, t)
                    nc.vector.tensor_scalar(xms[:], xss[:], 1.0 / D, EPS, ALU.mult, ALU.add).then_inc(x_ms, 1)
                    v.wait_ge(x_rs, t + 1)
                    v.wait_ge(x_tr, t)
                    nc.vector.tensor_scalar(xn[:], xt[:, s, :], xr[:], None, ALU.mult).then_inc(x_n, 1)

                def heads(t, s, j, link):
                    h = qk[j]
                    link(nc.vector.tensor_tensor(hsq[:], h[:], h[:], ALU.mult))
                    link(nc.vector.tensor_reduce(hss[:], hsq[:], AX.X, ALU.add))
                    v.wait_ge(h_rs, 2 * t + j)
                    nc.vector.tensor_scalar(hms[:], hss[:], 1.0 / QK, EPS, ALU.mult, ALU.add).then_inc(h_ms, 1)
                    v.wait_ge(h_rs, 2 * t + j + 1)
                    link(nc.vector.tensor_tensor(h[:], h[:], hr[:, :, None].broadcast_to([P, HEADS, QK]), ALU.mult))
                    link(nc.vector.tensor_tensor(h[:], h[:], gk[:, j, None, :].broadcast_to([P, HEADS, QK]), ALU.mult))
                    tail = h[:, :, NOPE:]
                    nc.vector.tensor_tensor(rc[:], tail, rope[:, s, None, 0:ROPE].broadcast_to([P, HEADS, ROPE]), ALU.mult)
                    nf = ROPE // 4
                    for o in range(0, ROPE, nf):
                        other = o + nf if o // nf % 2 == 0 else o - nf
                        last = nc.vector.tensor_tensor(rs[:, :, o:o + nf], h[:, :, NOPE + other:NOPE + other + nf],
                                                       rope[:, s, None, ROPE + o:ROPE + o + nf].broadcast_to([P, HEADS, nf]), ALU.mult)
                    link(last)
                    nc.vector.tensor_tensor(tail, rc[:], rs[:], ALU.add).then_inc(h_done, 1)

                def tile(t, s, loaded, more):
                    link = Link(v, dchain, LINKS // 2 * t)
                    if more:
                        x_norm(t + 1, 1 - s)
                    v.wait_ge(l_sq, 2 * t + 2)
                    v.wait_ge(l_rs, t)
                    nc.vector.tensor_scalar(lms[:], lss[:], 1.0, EPS, ALU.mult, ALU.add).then_inc(l_ms, 1)
                    v.wait_ge(l_rs, t + 1)
                    v.wait_ge(l_tr, t)
                    nc.vector.tensor_scalar(ckv[:], bIn[:, 0, 0:KVL], lr[:, 0:1], None, ALU.mult).then_inc(l_n, 1)
                    nc.vector.tensor_scalar(cq[:], bIn[:, 1, 0:QL], lr[:, 1:2], None, ALU.mult).then_inc(l_n, 1)
                    nc.vector.tensor_copy(kpe[:], bIn[:, 0, KVL:E_Q0]).then_inc(kpe_out, 1)
                    v.wait_ge(in_f, t + 1)
                    v.wait_ge(fx_mm, t)
                    nc.vector.tensor_copy(fT[:].rearrange("p a b -> p (a b)"), bF[:]).then_inc(f_T, 1)
                    v.wait_ge(rope_loaded[s], loaded)
                    v.wait_ge(q_mm, t + 1)
                    v.wait_ge(h_st, 32 * t)
                    q = qk[0][:].rearrange("p h d -> p (h d)")
                    nc.vector.tensor_copy(q[:, 0:512], bIn[:, 0, :])
                    nc.vector.tensor_copy(q[:, 512:], bIn[:, 1, 0:HEADS * QK - 512]).then_inc(q_out, 1)
                    v.wait_ge(q_out, t + 1)
                    heads(t, s, 0, link)
                    v.wait_ge(kv_mm, t + 1)
                    for j in range(2):
                        last = nc.vector.tensor_copy(qk[1][:, 4 * j:4 * j + 4, 0:NOPE],
                                                     bX[:, j, :].rearrange("p (h d) -> p h d", h=4)[:, :, 0:NOPE])
                    last.then_inc(k_out, 1)
                    v.wait_ge(kpe_out, t + 1)
                    link(nc.vector.tensor_copy(qk[1][:, :, NOPE:], kpe[:, None, :].broadcast_to([P, HEADS, ROPE])))
                    heads(t, s, 1, link)
                    assert link.n == LINKS // 2, link.n

                x_norm(0, 0)
                with v.Fori(0, NT // 2 - 1) as i:
                    tile(2 * i, 0, 16 * i + 16, True)
                    tile(2 * i + 1, 1, 16 * i + 16, True)
                tile(NT - 2, 0, 16 * (NT // 2), True)
                tile(NT - 1, 1, 16 * (NT // 2), False)


def attend(nc, sem, keep, A, W):
    with ExitStack() as stack:
        core = Core(nc, stack, "at")
        SCALE = QK ** -0.5
        QB, NB = 4, 4
        NLT = NT - NC_CTX
        kraw = core.sb("kraw", [P, NT, QK])
        qraw = core.sb("qraw", [P, NT, QK])
        va = core.sb("va", [P, 2, NT, VH + 1])
        kT = core.sb("kT", [QK + 1, 2, T])
        qT = core.sb("qT", [QK + 1, 2, T])
        kTb = core.sb("kTb", [QK, 2, T], BF16)
        qTb = core.sb("qTb", [QK, 2, T], BF16)
        pT = core.sb("pT", [P, 3, 512])
        mx = core.sb("mx", [P, QB, 5])
        nm = core.sb("nm", [P, QB])
        oT = core.sb("oT", [VH + 1, 512])
        rec = core.sb("rec", [P, QB])
        o = core.sb("o", [P, QB, VH])
        bS = core.ps("bS", [P, 3, 512])
        bM = core.ps("bM", [P, 2, 512])
        bT = core.ps("bT", [P, 512])
        bO = core.ps("bO", [P, 512])
        bR = core.ps("bR", [P, 512])

        raw_l, v_l, set_up = [sem(f"at_{n}_loaded") for n in "kq"], [sem(f"at_v{i}_loaded") for i in range(2)], sem("at_setup")
        tr, tev, cast = sem("at_transposed"), sem("at_T_out"), sem("at_cast")
        max_mm, max_red, max_fin = sem("at_max_mm"), sem("at_max_reduced"), sem("at_max_final")
        row_mm, row_out = sem("at_row_mm"), sem("at_row_out")
        s_mm, exp_done, pv_mm = sem("at_scores"), sem("at_exp"), sem("at_pv")
        settled = [sem(f"at_settled{i}") for i in range(2)]
        oT_out, o_tr, rec_done, o_done, o_st = (sem("at_oT_out"), sem("at_o_transposed"), sem("at_reciprocal"),
                                                sem("at_o_done"), sem("at_o_stored"))

        BLOCKS = [(NC_CTX + QB * b, QB, NT) for b in range(NB)] + [(0, NC_CTX, NC_CTX)]
        NBLK = len(BLOCKS)
        STEPS = [nk for _, _, nk in BLOCKS]
        SH = sum(STEPS)
        GROUPS = [(j, min(4, NT - j)) for j in range(0, NT, 4)]
        NGR = 2 * len(GROUPS)

        def items(b):
            _, nq, nk = BLOCKS[b]
            return [(j, c // 512, c, min(512, nk * P - c)) for j in range(nq) for c in range(0, nk * P, 512)]

        FIRST_ITEM = [sum(len(items(x)) for x in range(b)) for b in range(NBLK + 1)]
        IH = FIRST_ITEM[-1]
        assert IH % 2 == 0
        FIRST_STEP = [sum(STEPS[:b]) for b in range(NBLK)]

        def side(b, s, h, has_next):
            if b < 3:
                return [(h, s, b + 1)]
            if b == 3:
                return [(h, s, 4)] + ([(h + 1, 1 - s, 0)] if has_next else [])
            return []

        def beside(b, s, h, has_next):
            jobs = []
            for hh, ss, bb in side(b, s, h, has_next):
                jobs += [("max", hh, ss, bb, i) for i in range(len(items(bb)))] + [("row", hh, ss, bb, b)]
            if b == 2 and has_next:
                jobs += [("turn", h + 1, 1 - s, n, None) for n in range(NGR)]
            nk = STEPS[b]
            return [jobs[len(jobs) * k // nk:len(jobs) * (k + 1) // nk] for k in range(nk)]

        def heads(fori, one):
            with fori(0, HEADS // 2 - 1) as i:
                one(2 * i, 0, True)
                one(2 * i + 1, 1, True)
            one(HEADS - 2, 0, True)
            one(HEADS - 1, 1, False)

        with nc.Block() as block:
            @block.sync
            def _(sp):
                def load(dst, name, h, done):
                    head = slice(h, h + 1) if isinstance(h, int) else bass.ds(h, 1)
                    sp.dma_start(dst[:, 0:NC_CTX, :], W[name][head, 0:CTX].rearrange("a (p j) d -> p (a j) d", p=P)).then_inc(done, 16)
                    sp.dma_start(dst[:, NC_CTX:NT, :], W[name][head, CTX:T].rearrange("a (p j) d -> p (a j) d", p=P)).then_inc(done, 16)

                def store(h, b, s):
                    q0, nq, _ = BLOCKS[b]
                    sp.wait_ge(o_done, h * NBLK + b + 1)
                    settle(sp, settled[0])
                    col = slice(h * VH, (h + 1) * VH) if isinstance(h, int) else bass.ds(h * VH, VH)
                    if b < NB:
                        dst = W["mix"][CTX:T, col].rearrange("(p j) d -> p j d", p=P)[:, q0 - NC_CTX:q0 - NC_CTX + nq, :]
                    else:
                        dst = W["mix"][0:CTX, col].rearrange("(p j) d -> p j d", p=P)
                    sp.dma_start(dst, o[:, 0:nq, :]).then_inc(o_st, 16)

                def head(h, s, has_next):
                    if has_next:
                        sp.wait_ge(tr, (h + 1) * NGR)
                        load(kraw, "k", h + 1, raw_l[0])
                        load(qraw, "q", h + 1, raw_l[1])
                        sp.wait_ge(pv_mm, h * SH)
                        load(va[:, 1 - s, :, 0:VH], "v", h + 1, v_l[1 - s])
                    for b in range(NBLK):
                        store(h, b, s)

                load(kraw, "k", 0, raw_l[0])
                load(qraw, "q", 0, raw_l[1])
                sp.wait_ge(set_up, 2)
                load(va[:, 0, :, 0:VH], "v", 0, v_l[0])
                heads(sp.Fori, head)
                sp.wait_ge(o_st, 16 * NBLK * HEADS)

            @block.gpsimd
            def _(g):
                nc.gpsimd.memset(va[:], 1.0).then_inc(set_up, 1)

                def prepare(h, s):
                    for n in range(NGR):
                        j, w = GROUPS[n % len(GROUPS)]
                        src, dst = (kT, kTb) if n < len(GROUPS) else (qT, qTb)
                        g.wait_ge(tev, h * NGR + n + 1)
                        settle(g, settled[1])
                        nc.gpsimd.tensor_copy(dst[:, s, j * P:(j + w) * P], src[0:QK, s, j * P:(j + w) * P]).then_inc(cast, 1)

                prepare(0, 0)
                def head(h, s, has_next):
                    if has_next:
                        g.wait_ge(max_red, h * IH + FIRST_ITEM[1])
                        prepare(h + 1, 1 - s)

                heads(g.Fori, head)

            @block.tensor
            def _(pe):
                ident = keep["ident"]

                def transpose_group(h, s, n):
                    j, w = GROUPS[n % len(GROUPS)]
                    raw, first = (kraw, n == 0) if n < len(GROUPS) else (qraw, n == len(GROUPS))
                    if first:
                        pe.wait_ge(raw_l[0 if raw is kraw else 1], 32 * (h + 1))
                    pe.wait_ge(tev, h * NGR + n)
                    for x in range(w):
                        last = pe.transpose(bT[0:QK, x * P:(x + 1) * P], raw[:, j + x, :], ident[:])
                    last.then_inc(tr, 1)

                def max_item(h, s, b, i):
                    j, _, c, n = items(b)[i]
                    q0 = BLOCKS[b][0]
                    count = h * IH + FIRST_ITEM[b] + i
                    if b == 0 and i == 0:
                        pe.wait_ge(cast, (h + 1) * NGR)
                    if not (isinstance(count, int) and count < 2):
                        pe.wait_ge(max_red, count - 1)
                    pe.matmul(bM[:, (FIRST_ITEM[b] + i) % 2, 0:n], qTb[:, s, (q0 + j) * P:(q0 + j + 1) * P],
                              kTb[:, s, c:c + n], start=True, stop=True).then_inc(max_mm, 1)

                def row(h, s, b, outputs_done):
                    pe.wait_ge(o_done, outputs_done)
                    pe.wait_ge(row_out, h * NBLK + b)
                    pe.wait_ge(max_fin, h * NBLK + b + 1)
                    for j in range(BLOCKS[b][1]):
                        last = pe.matmul(bR[0:1, j * P:(j + 1) * P], nm[:, j:j + 1], ident[:], start=True, stop=True)
                    last.then_inc(row_mm, 1)

                def o_transposes(h, b, rows_done):
                    pe.wait_ge(oT_out, h * NBLK + b + 1)
                    pe.wait_ge(row_out, rows_done)
                    for j in range(BLOCKS[b][1]):
                        last = pe.transpose(bR[:, j * P:j * P + VH + 1], oT[:, j * P:(j + 1) * P], ident[0:VH + 1, 0:VH + 1])
                    last.then_inc(o_tr, 1)

                def scores(h, s, b, k):
                    q0, nq, nk = BLOCKS[b]
                    g = FIRST_STEP[b] + k
                    if k == 0:
                        pe.wait_ge(row_out, h * NBLK + b + 1)
                    pe.wait_ge(exp_done, h * SH + max(0, g - 2))
                    pe.matmul(bS[:, g % 3, 0:nq * P], kT[:, s, k * P:(k + 1) * P], qT[:, s, q0 * P:(q0 + nq) * P],
                              start=True, stop=True).then_inc(s_mm, 1)

                def pv(h, s, b, k):
                    _, nq, nk = BLOCKS[b]
                    g = FIRST_STEP[b] + k
                    if k == 0:
                        pe.wait_ge(oT_out, h * NBLK + b)
                        if b == 0:
                            pe.wait_ge(v_l[s], (h - s) * 16 + 32)
                    pe.wait_ge(exp_done, h * SH + g + 1)
                    pe.matmul(bO[0:VH + 1, 0:nq * P], va[:, s, k, :], pT[:, g % 3, 0:nq * P],
                              start=(k == 0), stop=(k == nk - 1)).then_inc(pv_mm, 1)

                def head(h, s, has_next):
                    for b in range(NBLK):
                        jobs = beside(b, s, h, has_next)
                        nk = STEPS[b]
                        for k in range(min(2, nk)):
                            scores(h, s, b, k)
                        if b > 0:
                            rows = h * NBLK + b + 1 if b < 4 or not has_next else (h + 1) * NBLK + 1
                            o_transposes(h, b - 1, rows)
                        for k in range(nk):
                            if k + 2 < nk:
                                scores(h, s, b, k + 2)
                            for kind, hh, ss, n, i in jobs[k]:
                                if kind == "max":
                                    max_item(hh, ss, n, i)
                                elif kind == "row":
                                    row(hh, ss, n, h * NBLK + b)
                                else:
                                    transpose_group(hh, ss, n)
                            pv(h, s, b, k)
                    o_transposes(h, NBLK - 1, (h + 1) * NBLK)

                pe.wait_ge(set_up, 2)
                for n in range(NGR):
                    transpose_group(0, 0, n)
                for i in range(len(items(0))):
                    max_item(0, 0, 0, i)
                row(0, 0, 0, 0)
                heads(pe.Fori, head)

            @block.scalar
            def _(a):
                def evict(h, s, n):
                    j, w = GROUPS[n % len(GROUPS)]
                    dst = kT if n < len(GROUPS) else qT
                    a.wait_ge(tr, h * NGR + n + 1)
                    nc.scalar.copy(dst[0:QK, s, j * P:(j + w) * P], bT[0:QK, 0:w * P]).then_inc(tev, 1)

                def head(h, s, has_next):
                    for b in range(NBLK):
                        q0, nq, nk = BLOCKS[b]
                        jobs = beside(b, s, h, has_next)
                        for k in range(nk):
                            g = FIRST_STEP[b] + k
                            a.wait_ge(s_mm, h * SH + g + 1)
                            a.wait_ge(pv_mm, h * SH + max(0, g - 2))
                            nc.scalar.activation(pT[:, g % 3, 0:nq * P], bS[:, g % 3, 0:nq * P], ACT.Exp,
                                                 scale=SCALE).then_inc(exp_done, 1)
                            for kind, hh, ss, n, i in jobs[k]:
                                if kind == "turn":
                                    evict(hh, ss, n)

                for n in range(NGR):
                    evict(0, 0, n)
                heads(a.Fori, head)

            @block.vector
            def _(v):
                def maxima(h, s, b):
                    for i, (j, piece, c, n) in enumerate(items(b)):
                        count = h * IH + FIRST_ITEM[b] + i
                        v.wait_ge(max_mm, count + 1)
                        if i == 0:
                            v.wait_ge(max_fin, h * NBLK + b)
                        nc.vector.tensor_reduce(mx[:, j, piece:piece + 1], bM[:, (FIRST_ITEM[b] + i) % 2, 0:n], AX.X, ALU.max).then_inc(max_red, 1)
                    pieces = -(-STEPS[b] * P // 512)
                    nq = BLOCKS[b][1]
                    v.wait_ge(max_red, h * IH + FIRST_ITEM[b + 1])
                    v.wait_ge(row_mm, h * NBLK + b)
                    nc.vector.tensor_reduce(nm[:, 0:nq], mx[:, 0:nq, 0:pieces], AX.X, ALU.max, negate=True).then_inc(max_fin, 1)

                def row(h, s, b):
                    q0, nq, _ = BLOCKS[b]
                    v.wait_ge(row_mm, h * NBLK + b + 1)
                    nc.vector.tensor_copy(qT[QK:QK + 1, s, q0 * P:(q0 + nq) * P], bR[0:1, 0:nq * P]).then_inc(row_out, 1)

                def finish_a(h, b):
                    nq = BLOCKS[b][1]
                    v.wait_ge(pv_mm, h * SH + FIRST_STEP[b] + STEPS[b])
                    nc.vector.tensor_copy(oT[:, 0:nq * P], bO[0:VH + 1, 0:nq * P]).then_inc(oT_out, 1)

                def finish_b(h, b):
                    nq = BLOCKS[b][1]
                    v.wait_ge(o_tr, h * NBLK + b + 1)
                    back = bR[:].rearrange("p (j c) -> p j c", c=P)
                    nc.vector.reciprocal(rec[:, 0:nq], back[:, 0:nq, VH]).then_inc(rec_done, 1)
                    v.wait_ge(rec_done, h * NBLK + b + 1)
                    v.wait_ge(o_st, 16 * (h * NBLK + b))
                    nc.vector.tensor_tensor(o[:, 0:nq, :], back[:, 0:nq, 0:VH], rec[:, 0:nq, None].broadcast_to([P, nq, VH]),
                                            ALU.mult).then_inc(o_done, 1)

                def head(h, s, has_next):
                    for b in range(NBLK):
                        if b > 0:
                            finish_b(h, b - 1)
                        for hh, ss, bb in side(b, s, h, has_next):
                            maxima(hh, ss, bb)
                            row(hh, ss, bb)
                        finish_a(h, b)
                    finish_b(h, NBLK - 1)

                nc.vector.memset(kT[QK:QK + 1, :, :], 1.0).then_inc(set_up, 1)
                maxima(0, 0, 0)
                row(0, 0, 0)
                heads(v.Fori, head)


def fourier(nc, sem, keep, A, W):
    with ExitStack() as stack:
        core = Core(nc, stack, "ft")
        K1H = P // (P // N2)
        CH = 4
        step1 = core.sb("step1", [P, N2, 3, P])
        step2 = core.sb("step2", [P, 2, P])
        cdft = core.sb("cdft", [P, NC_CTX, 2, CTX])
        ab = core.sb("ab", [P, N2, 2 * FW])
        cab = core.sb("cab", [P, NC_CTX, 2 * FW])
        z = core.sb("z", [P, 4, 2, FW])
        zin = core.sb("zin", [P, 2, 2, K1H, FW // 2])
        fo = core.sb("fo", [P, 4, FW])
        bZ = core.ps("bZ", [P, 4, FW])
        bF = core.ps("bF", [P, 4, FW])
        tab, ctx_l = sem("ft_tables_loaded"), sem("ft_ctx_loaded")
        ab_l = [sem(f"ft_ab_loaded{i}") for i in range(N2 // CH)]
        mm1, re_out, im_out = sem("ft_step1"), sem("ft_re_out"), sem("ft_im_out")
        z_st = [sem(f"ft_z_stored{i}") for i in range(4)]
        z_l = [sem(f"ft_z_loaded{i}") for i in range(2)]
        mm2, f_out = sem("ft_step2"), sem("ft_f_out")
        f_st = [sem(f"ft_f_stored{i}") for i in range(4)]
        NCTX_OUT = CTX // P

        with nc.Block() as block:
            @block.sync
            def _(sp):
                src = W["fx"][CTX:T].rearrange("(p n) c -> p n c", n=N2)
                sp.dma_start(step1[:, 0:CH], A["step1"][:, 0:CH]).then_inc(tab, 16)
                sp.dma_start(ab[:, 0:CH], src[:, 0:CH]).then_inc(ab_l[0], 16)
                sp.dma_start(step1[:, CH:N2], A["step1"][:, CH:N2]).then_inc(tab, 16)
                for i in range(1, N2 // CH):
                    sp.dma_start(ab[:, CH * i:CH * (i + 1)], src[:, CH * i:CH * (i + 1)]).then_inc(ab_l[i], 16)
                sp.dma_start(step2[:], A["step2"]).then_inc(ctx_l, 16)
                sp.dma_start(cdft[:], A["ctxdft"]).then_inc(ctx_l, 16)
                sp.dma_start(cab[:], W["fx"][0:CTX].rearrange("(k p) c -> p k c", p=P)).then_inc(ctx_l, 16)
                for n in range(N2):
                    sp.wait_ge(re_out, n + 1)
                    sp.wait_ge(im_out, n + 1)
                    sp.dma_start(W["z"][:, n].rearrange("r p c -> p r c"), z[:, n % 4]).then_inc(z_st[n % 4], 16)
                for i in range(4):
                    sp.wait_ge(z_st[i], 16 * N2 // 4)
                for hc in range(2):
                    for r in range(2):
                        sp.dma_start(zin[:, hc, r], W["z"][r].rearrange("n (lo hi) c -> (n lo) hi c", hi=K1H)
                                     [:, :, hc * FW // 2:(hc + 1) * FW // 2]).then_inc(z_l[hc], 16)

                dst = W["mix"][CTX:T, HEADS * VH:GW].rearrange("(p hi) c -> p hi c", hi=K1H)
                for i in range(NCTX_OUT):
                    sp.wait_ge(f_out, i + 1)
                    sp.dma_start(W["mix"][i * P:(i + 1) * P, HEADS * VH:GW], fo[:, i]).then_inc(f_st[i], 16)
                for n in range(K1H):
                    hc, pair = divmod(n, K1H // 2)
                    sp.wait_ge(f_out, NCTX_OUT + n + 1)
                    sp.dma_start(dst[:, 2 * pair:2 * pair + 2, hc * FW // 2:(hc + 1) * FW // 2],
                                fo[:, (NCTX_OUT + n) % 4].rearrange("p (a c) -> p a c", a=2)).then_inc(f_st[(NCTX_OUT + n) % 4], 16)
                for i in range(4):
                    sp.wait_ge(f_st[i], 16 * len(range(i, NCTX_OUT + K1H, 4)))

            @block.tensor
            def _(pe):
                pe.wait_ge(tab, 16)
                for n in range(N2):
                    if n == CH:
                        pe.wait_ge(tab, 32)
                    if n % CH == 0:
                        pe.wait_ge(ab_l[n // CH], 16)
                    if n >= 2:
                        pe.wait_ge(re_out, n - 1)
                        pe.wait_ge(im_out, n - 1)
                    b = 2 * (n % 2)
                    cos, sin, neg_sin = (step1[:, n, x, :] for x in range(3))
                    pe.matmul(bZ[:, b, :], cos, ab[:, n, 0:FW], start=True, stop=False)
                    pe.matmul(bZ[:, b, :], neg_sin, ab[:, n, FW:], start=False, stop=True)
                    pe.matmul(bZ[:, b + 1, :], sin, ab[:, n, 0:FW], start=True, stop=False)
                    pe.matmul(bZ[:, b + 1, :], cos, ab[:, n, FW:], start=False, stop=True).then_inc(mm1, 1)
                pe.wait_ge(ctx_l, 48)
                for i in range(NCTX_OUT):
                    for x in range(2 * NC_CTX):
                        kt, part = divmod(x, 2)
                        last = pe.matmul(bF[:, i, :], cdft[:, kt, part, i * P:(i + 1) * P], cab[:, kt, part * FW:(part + 1) * FW],
                                         start=(x == 0), stop=(x == 2 * NC_CTX - 1))
                    last.then_inc(mm2, 1)
                for hc in range(2):
                    pe.wait_ge(z_l[hc], 32)
                    for hi in range(0, K1H, 2):
                        n = NCTX_OUT + (hc * K1H + hi) // 2
                        if n >= 4:
                            pe.wait_ge(f_out, n - 3)
                        for r in range(2):
                            last = pe.matmul(bF[:, n % 4, :], step2[:, r, :], zin[:, hc, r, hi:hi + 2, :].rearrange("p a c -> p (a c)"),
                                             start=(r == 0), stop=(r == 1))
                        last.then_inc(mm2, 1)

            @block.scalar
            def _(a):
                for n in range(N2):
                    a.wait_ge(mm1, n + 1)
                    if n >= 4:
                        a.wait_ge(z_st[n % 4], 16 * (n // 4))
                    nc.scalar.copy(z[:, n % 4, 0, :], bZ[:, 2 * (n % 2), :]).then_inc(re_out, 1)

            @block.vector
            def _(v):
                for n in range(N2):
                    v.wait_ge(mm1, n + 1)
                    if n >= 4:
                        v.wait_ge(z_st[n % 4], 16 * (n // 4))
                    nc.vector.tensor_copy(z[:, n % 4, 1, :], bZ[:, 2 * (n % 2) + 1, :]).then_inc(im_out, 1)
                for n in range(NCTX_OUT + K1H):
                    v.wait_ge(mm2, n + 1)
                    if n >= 4:
                        v.wait_ge(f_st[n % 4], 16 * (n // 4))
                    nc.vector.tensor_copy(fo[:, n % 4, :], bF[:, n % 4, :]).then_inc(f_out, 1)


def merge0(nc, sem, keep, A, W):
    with ExitStack() as stack:
        core = Core(nc, stack, "m0")
        w = core.sb("w", [P, KD, D])
        mix, gate, xt = (core.sb(n, [P, 2, D]) for n in ("mix", "gate", "xt"))
        m = core.sb("m", [P, D])
        mT = core.sb("mT", [P, 2, KD, P])
        gy = core.sb("gy", [P, D])
        x1 = core.sb("x1", [P, 2, D])
        xsq, xss, xms, xr, xn = (core.sb(n, [P, c]) for n, c in (("xsq", D), ("xss", 1), ("xms", 1), ("xr", 1), ("xn", D)))
        half = core.sb("half", [P, 1])
        bM = core.ps("bM", [P, 2, 512])
        bY = core.ps("bY", [P, 2, 512])
        bX = core.ps("bX", [P, 2, 512])
        w_l, in_l = sem("m0_w_loaded"), [sem(f"m0_tile_loaded{i}") for i in range(2)]
        m_done, m_tr, m_T, y_mm, gy_done = sem("m0_gated"), sem("m0_m_tr"), sem("m0_mT"), sem("m0_y_mm"), sem("m0_gy")
        x1_done, x1_st = sem("m0_x1"), [sem(f"m0_x1_stored{i}") for i in range(2)]
        x_sq, x_ms, x_rs, x_n, x_tr, x_hT = (sem(f"m0_{n}") for n in ("x_sq", "x_ms", "x_rs", "x_n", "x_tr", "hT"))
        pchain = sem("m0_pool_setup")
        hT = keep["hT"]

        def tiles(fori, one):
            one(0, 0, True, True)
            one(1, 1, True, False)
            with fori(1, NT // 2) as i:
                one(2 * i, 0, False, False)
                one(2 * i + 1, 1, False, False)

        def rows(t):
            return slice(t * P, (t + 1) * P) if isinstance(t, int) else bass.ds(t * P, P)

        with nc.Block() as block:
            @block.sync
            def _(sp):
                def load(t, s, src, at):
                    sp.dma_start(mix[:, s, :], W["mix"][rows(t), :]).then_inc(in_l[s], 16)
                    sp.dma_start(gate[:, s, :], W["gate"][rows(t), :]).then_inc(in_l[s], 16)
                    sp.dma_start(xt[:, s, :], src[0, rows(at), :]).then_inc(in_l[s], 16)

                def store(t, s):
                    sp.wait_ge(x1_done, t + 1)
                    sp.dma_start(W["x1"][rows(t), :], x1[:, s, :]).then_inc(x1_st[s], 16)

                load(0, 0, A["ctx"], 0)
                sp.dma_start(w[:], A["e_w_out"][0].rearrange("(k p) n -> p k n", p=P)).then_inc(w_l, 16)
                load(1, 1, A["ctx"], 1)
                with sp.Fori(1, NT // 2) as i:
                    for s in range(2):
                        sp.wait_ge(m_done, 2 * i + s - 1)
                        store(2 * i + s - 2, s)
                        load(2 * i + s, s, A["x"], 2 * i + s - 2)
                store(NT - 2, 0)
                store(NT - 1, 1)
                for s in range(2):
                    sp.wait_ge(x1_st[s], 16 * NT // 2)

            @block.gpsimd
            def _(g):
                nc.gpsimd.memset(half[:], -0.5).then_inc(pchain, 1)
                g.wait_ge(pchain, 1)
                with g.Fori(0, NT) as t:
                    g.wait_ge(x_ms, t + 1)
                    g.wait_ge(x_n, t)
                    nc.gpsimd.tensor_tensor(xr[:], xms[:], half[:], ALU.pow).then_inc(x_rs, 1)

            @block.tensor
            def _(pe):
                ident = keep["ident"]

                def turn(dst, src, done):
                    for k in range(KD):
                        last = pe.transpose(dst[:, k // 4, (k % 4) * P:(k % 4 + 1) * P], src[:, k * P:(k + 1) * P], ident[:])
                    last.then_inc(done, 1)

                def turn_m(t):
                    pe.wait_ge(m_done, t + 1)
                    pe.wait_ge(m_T, 2 * t)
                    turn(bM, m, m_tr)

                def turn_x(t):
                    pe.wait_ge(x_n, t + 1)
                    pe.wait_ge(x_hT, t)
                    turn(bX, xn, x_tr)

                def project(t, s):
                    pe.wait_ge(m_T, 2 * t + 2)
                    for j in range(2):
                        pe.wait_ge(gy_done, 2 * t - 1 + j if not isinstance(t, int) or t else 0)
                        for k in range(KD):
                            last = pe.matmul(bY[:, j, :], mT[:, s, k, :], w[:, k, j * 512:(j + 1) * 512],
                                             start=(k == 0), stop=(k == KD - 1))
                        last.then_inc(y_mm, 1)

                turn_m(0)
                pe.wait_ge(w_l, 16)
                turn_m(1)
                project(0, 0)
                with pe.Fori(1, NT // 2) as i:
                    turn_m(2 * i)
                    project(2 * i - 1, 1)
                    turn_x(2 * i - 2)
                    turn_m(2 * i + 1)
                    project(2 * i, 0)
                    turn_x(2 * i - 1)
                project(NT - 1, 1)
                turn_x(NT - 2)
                turn_x(NT - 1)

            @block.scalar
            def _(a):
                def evict_m(t, s):
                    a.wait_ge(m_tr, t + 1)
                    for j in range(2):
                        nc.scalar.copy(mT[:, s, 4 * j:4 * j + 4, :].rearrange("p k c -> p (k c)"), bM[:, j, :]).then_inc(m_T, 1)

                def squares(t, s):
                    a.wait_ge(x1_done, t + 1)
                    a.wait_ge(x_ms, t)
                    nc.scalar.activation(xsq[:], x1[:, s, :], ACT.Square, accum_out=xss[:]).then_inc(x_sq, 1)

                def modulated(t, stream):
                    a.wait_ge(x_tr, t + 1)
                    for k in range(KD):
                        last = nc.scalar.activation(hT[:, k, rows(t)], bX[:, k // 4, (k % 4) * P:(k % 4 + 1) * P],
                                                    ACT.Identity, scale=keep["scale"][:, 1, k, stream:stream + 1],
                                                    bias=keep["shift"][:, 1, k, stream:stream + 1])
                    last.then_inc(x_hT, 1)

                evict_m(0, 0)
                evict_m(1, 1)
                squares(0, 0)
                evict_m(2, 0)
                squares(1, 1)
                modulated(0, 1)
                evict_m(3, 1)
                squares(2, 0)
                modulated(1, 1)
                with a.Fori(2, NT // 2) as i:
                    evict_m(2 * i, 0)
                    squares(2 * i - 1, 1)
                    modulated(2 * i - 2, 0)
                    evict_m(2 * i + 1, 1)
                    squares(2 * i, 0)
                    modulated(2 * i - 1, 0)
                squares(NT - 1, 1)
                modulated(NT - 2, 0)
                modulated(NT - 1, 0)

            @block.vector
            def _(v):
                def gated(t, s, loaded):
                    v.wait_ge(in_l[s], loaded)
                    v.wait_ge(m_tr, t)
                    nc.vector.tensor_tensor(m[:], mix[:, s, :], gate[:, s, :], ALU.mult).then_inc(m_done, 1)

                def residual(t, s, stream):
                    for j in range(2):
                        v.wait_ge(y_mm, 2 * t + j + 1)
                        nc.vector.tensor_tensor(gy[:, j * 512:(j + 1) * 512], bY[:, j, :],
                                                keep["gate"][:, stream, j * 512:(j + 1) * 512], ALU.mult).then_inc(gy_done, 1)
                    v.wait_ge(gy_done, 2 * t + 2)
                    v.wait_ge(x1_st[s], (t - s) * 8)
                    nc.vector.tensor_tensor(x1[:, s, :], gy[:], xt[:, s, :], ALU.add).then_inc(x1_done, 1)

                def norm(t, s):
                    v.wait_ge(x_sq, t + 1)
                    nc.vector.tensor_scalar(xms[:], xss[:], 1.0 / D, EPS, ALU.mult, ALU.add).then_inc(x_ms, 1)
                    v.wait_ge(x_rs, t + 1)
                    v.wait_ge(x_tr, t)
                    nc.vector.tensor_scalar(xn[:], x1[:, s, :], xr[:], None, ALU.mult).then_inc(x_n, 1)

                gated(0, 0, 48)
                gated(1, 1, 48)
                residual(0, 0, 1)
                norm(0, 0)
                gated(2, 0, 96)
                residual(1, 1, 1)
                norm(1, 1)
                with v.Fori(1, NT // 2 - 1) as i:
                    gated(2 * i + 1, 1, 48 * i + 48)
                    residual(2 * i, 0, 0)
                    norm(2 * i, 0)
                    gated(2 * i + 2, 0, 48 * i + 96)
                    residual(2 * i + 1, 1, 0)
                    norm(2 * i + 1, 1)
                gated(NT - 1, 1, 48 * (NT // 2))
                residual(NT - 2, 0, 0)
                norm(NT - 2, 0)
                residual(NT - 1, 1, 0)
                norm(NT - 1, 1)


def project1(nc, sem, keep, A, W):
    with ExitStack() as stack:
        core = Core(nc, stack, "p1")
        TZ = T + 2
        L0 = CTX + 2
        slab = core.sb("slab", [P, 4, KD, P])
        u = core.sb("u", [P, 2, T + 4])
        z = core.sb("z", [P, 2, TZ])
        kq = core.sb("kq", [P, TZ])
        rn = core.sb("rn", [P, TZ])
        kk = core.sb("kk", [P, TZ])
        gs = core.sb("gs", [P, SEQ])
        shift = core.sb("shift", [P, SHIFT_ROWS, O_G0 // P])
        k_k = core.sb("k_k", [P, PAIRS])
        same = core.sb("same", [P, P])
        bU = core.ps("bU", [P, 4, 512])
        bS = core.ps("bS", [P, 2, 512])
        BLK = [(0, 1, CTX)] + [(CTX + 512 * j, CTX + 3 + 512 * j, 512) for j in range(SEQ // 512)]
        SBLK = [(c, min(512, TZ - c)) for c in range(0, TZ, 512)]
        NB, NS = len(BLK), len(SBLK)
        PRE = 2 * NB
        PB = 4 * NB - 1
        c_l, s_l = sem("p1_consts_loaded"), [sem(f"p1_slab{i}_loaded") for i in range(4)]
        set_up, mm, ev = sem("p1_setup"), sem("p1_block_mm"), sem("p1_block_out")
        u_used, z1, z_done = sem("p1_u_used"), sem("p1_z_middle"), sem("p1_z_done")
        z_st = [sem(f"p1_z{i}_stored") for i in range(2)]
        t_done = sem("p1_tanh_done")
        kq_done, ss_mm, root, kk_done, kk_st, gs_st = (sem(f"p1_{n}") for n in (
            "k_squared", "ss_mm", "root", "kk_done", "kk_stored", "gate_stored"))
        dchain = sem("p1_dve_chain")
        hT = keep["hT"]
        STARTS = [0, D, O_R0, O_G0]
        ROWS = {0: 0, 1: 3, 2: 2}

        def zslot(i):
            return i % 2

        with nc.Block() as block:
            @block.sync
            def _(sp):
                def load(i, at):
                    sp.dma_start(slab[:, i], A["o_w_in"][0, :, at].rearrange("(k p) n -> p k n", p=P)).then_inc(s_l[i], 16)

                def store(dst, src, done):
                    sp.dma_start(dst[:, 0:CTX], src[:, 0:CTX]).then_inc(done, 16)
                    sp.dma_start(dst[:, CTX:T], src[:, L0:TZ]).then_inc(done, 16)

                load(0, slice(O_WD0, O_WD0 + P))
                load(1, slice(O_AD0, O_AD0 + P))
                with nc.allow_non_contiguous_dma("short vectors as columns"):
                    for r in range(SHIFT_ROWS):
                        sp.dma_start(shift[:, r, :], A["o_shift_w"][0, r].rearrange("(k p) -> p k", p=P)).then_inc(c_l, 16)
                    sp.dma_start(k_k[:], A["o_k_k"][0].rearrange("(k p) -> p k", p=P)).then_inc(c_l, 16)
                sp.dma_start(same[:], A["same"]).then_inc(c_l, 16)
                load(2, slice(O_R0, O_R0 + P))
                load(3, slice(O_G0, O_G0 + P))
                for i in range(2):
                    sp.wait_ge(mm, NB * (i + 1))
                    load(i, slice(STARTS[i], STARTS[i] + P))
                sp.wait_ge(t_done, 1)
                store(W["lora"][0], z[:, 0], z_st[0])
                sp.wait_ge(z_done, 2)
                store(W["lora"][1], z[:, 1], z_st[1])

                def pair(p, more):
                    row = slice(p, p + 1) if isinstance(p, int) else bass.ds(p, 1)
                    heads = W["heads"][row].rearrange("a c f t -> (a c) f t")
                    for i in range(3):
                        s = i % 2
                        sp.wait_ge(z_done, 2 + 3 * p + i + 1)
                        store(heads[:, ROWS[i], :], z[:, zslot(i)], z_st[zslot(i)])
                        if more:
                            sp.wait_ge(mm, PRE + PB * p + NB * (i + 1))
                            at = bass.ds((p + 1) * P + STARTS[i], P) if not isinstance(p, int) else slice((p + 1) * P + STARTS[i], (p + 2) * P + STARTS[i])
                            load(i, at)
                        if i == 1:
                            sp.wait_ge(kk_done, p + 1)
                            store(heads[:, 1, :], kk, kk_st)
                    sp.wait_ge(ev, PRE + PB * (p + 1))
                    if more:
                        load(3, bass.ds((p + 1) * P + STARTS[3], P) if not isinstance(p, int) else slice((p + 1) * P + STARTS[3], (p + 2) * P + STARTS[3]))
                    sp.dma_start(W["gsT"][row].rearrange("a c t -> (a c) t"), gs[:]).then_inc(gs_st, 16)

                with sp.Fori(0, PAIRS - 1) as p:
                    pair(p, True)
                pair(PAIRS - 1, False)
                sp.wait_ge(z_st[0], 32 * (1 + 2 * PAIRS))
                sp.wait_ge(z_st[1], 32 * (1 + PAIRS))
                sp.wait_ge(kk_st, 32 * PAIRS)
                sp.wait_ge(gs_st, 16 * PAIRS)

            @block.tensor
            def _(pe):
                def blocks(i, base, n0, first):
                    for b in range(first, NB):
                        tok, _, w = BLK[b]
                        n = n0 + b - first
                        pe.wait_ge(ev, base + max(0, n - 3))
                        for k in range(KD):
                            last = pe.matmul(bU[:, n % 4, 0:w], slab[:, i, k, :], hT[:, k, tok:tok + w],
                                             start=(k == 0), stop=(k == KD - 1))
                        last.then_inc(mm, 1)

                pe.wait_ge(c_l, 16 * 5)
                for i in range(2):
                    pe.wait_ge(s_l[i], 16)
                    blocks(i, 0, i * NB, 0)
                with pe.Fori(0, PAIRS) as p:
                    base = PRE + PB * p
                    for i in range(4):
                        pe.wait_ge(s_l[i], 16 * p + (32 if i < 2 else 16))
                        blocks(i, base, NB * i, 1 if i == 3 else 0)
                        if i == 1:
                            pe.wait_ge(kq_done, p + 1)
                            for x, (c, w) in enumerate(SBLK):
                                pe.wait_ge(root, NS * p + max(0, x - 1))
                                pe.matmul(bS[:, x % 2, 0:w], same[:], kq[:, c:c + w], start=True, stop=True).then_inc(ss_mm, 1)

            @block.scalar
            def _(a):
                def evict(n, base, b, us):
                    _, col, w = BLK[b]
                    a.wait_ge(mm, base + n + 1)
                    nc.scalar.copy(u[:, us, col:col + w], bU[:, n % 4, 0:w]).then_inc(ev, 1)

                def middle(us, zs, tile, jobs, stored):
                    a.wait_ge(ev, jobs)
                    a.wait_ge(z_st[zs], stored)
                    nc.scalar.activation(z[:, zs, :], u[:, us, 1:T + 3], ACT.Identity, scale=shift[:, 1, tile]).then_inc(z1, 1)

                a.wait_ge(set_up, 1)
                a.wait_ge(c_l, 16 * 5)
                for i in range(2):
                    for b in range(NB):
                        evict(i * NB + b, 0, b, i)
                    middle(i, i, slice((O_WD0 // P) + i, (O_WD0 // P) + i + 1), (i + 1) * NB, 0)
                a.wait_ge(z_done, 1)
                nc.scalar.activation(z[:, 0, :], z[:, 0, :], ACT.Tanh).then_inc(t_done, 1)
                with a.Fori(0, PAIRS) as p:
                    base = PRE + PB * p
                    for i in range(3):
                        us = i % 2
                        a.wait_ge(z_done, 3 * p + max(2, i + 1))
                        for b in range(NB):
                            evict(NB * i + b, base, b, us)
                        z_before = (32 * (2 * p + 1) + (32 if i == 2 else 0)) if zslot(i) == 0 else 32 * (p + 1)
                        if i == 2:
                            a.wait_ge(kk_done, p + 1)
                        middle(us, zslot(i), bass.ds(p + (0, KD, O_R0 // P)[i], 1), base + NB * (i + 1), z_before)
                        if i == 0:
                            a.wait_ge(z_done, 3 * p + 3)
                            a.wait_ge(ss_mm, NS * p)
                            nc.scalar.activation(kq[:], z[:, 0, :], ACT.Square, scale=k_k[:, bass.ds(p, 1)]).then_inc(kq_done, 1)
                        if i == 1:
                            a.wait_ge(kk_done, p)
                            for x, (c, w) in enumerate(SBLK):
                                a.wait_ge(ss_mm, NS * p + x + 1)
                                nc.scalar.activation(rn[:, c:c + w], bS[:, x % 2, 0:w], ACT.Sqrt).then_inc(root, 1)
                    a.wait_ge(gs_st, 16 * p)
                    for b in range(1, NB):
                        n = 3 * NB + b - 1
                        a.wait_ge(mm, base + n + 1)
                        nc.scalar.activation(gs[:, BLK[b][0] - CTX:BLK[b][0] - CTX + 512], bU[:, n % 4, :], ACT.Silu).then_inc(ev, 1)

            @block.vector
            def _(v):
                def shift_taps(us, zs, tile, n, dn):
                    v.wait_ge(z1, n + 1)
                    nc.vector.scalar_tensor_tensor(out=z[:, zs, :], in0=u[:, us, 0:TZ], scalar=shift[:, 0, tile],
                                                   in1=z[:, zs, :], op0=ALU.mult, op1=ALU.add).then_inc(dchain, 1)
                    v.wait_ge(dchain, dn + 1)
                    nc.vector.scalar_tensor_tensor(out=z[:, zs, :], in0=u[:, us, 2:T + 4], scalar=shift[:, 2, tile],
                                                   in1=z[:, zs, :], op0=ALU.mult, op1=ALU.add).then_inc(z_done, 1)

                nc.vector.memset(u[:], 0.0).then_inc(set_up, 1)
                v.wait_ge(c_l, 16 * 5)
                for i in range(2):
                    shift_taps(i, i, slice((O_WD0 // P) + i, (O_WD0 // P) + i + 1), i, i)
                with v.Fori(0, PAIRS) as p:
                    links = 2 + 5 * p
                    for i in range(3):
                        shift_taps(i % 2, zslot(i), bass.ds(p + (0, KD, O_R0 // P)[i], 1), 2 + 3 * p + i, links + i + (2 if i == 2 else 0))
                        if i == 1:
                            v.wait_ge(root, NS * (p + 1))
                            nc.vector.tensor_scalar(rn[:], rn[:], 1e-12, None, ALU.max).then_inc(dchain, 1)
                            v.wait_ge(dchain, links + 3)
                            nc.vector.reciprocal(rn[:], rn[:]).then_inc(dchain, 1)
                            v.wait_ge(dchain, links + 4)
                            v.wait_ge(kk_st, 32 * p)
                            nc.vector.scalar_tensor_tensor(out=kk[:], in0=z[:, 0, :], scalar=k_k[:, bass.ds(p, 1)], in1=rn[:],
                                                           op0=ALU.mult, op1=ALU.mult).then_inc(kk_done, 1)


def rwkv(nc, sem, keep, A, W):
    with ExitStack() as stack:
        core = Core(nc, stack, "rw")
        NBODY = PAIRS * NG
        U = 2 * NCH
        PER_LOAD = 6
        x4 = [P, 2, NCH, P]
        zin = core.sb("zin", [P, 2, 2, 4, GT])
        wl = core.sb("wl", [P, 2, 2, 2, P])
        lora = core.sb("lora", [P, 2, T])
        par = core.sb("par", [P, PAIRS, 7])
        cur = core.sb("cur", [P, 7])
        tri = core.sb("tri", [P, 2, 2, P])
        level = core.sb("level", [P, 2, 6, P], I32)
        same = core.sb("same", [P, P])
        reset = core.sb("reset", [P, 2, GT])
        flag = core.sb("flag", [P, NBODY])
        ee = core.sb("ee", [P, 2, 2, GT])
        cs, cx, ep, en, ex, t1, kd, b0, q, bv = (core.sb(n, [P, 2, GT]) for n in (
            "cs", "cx", "ep", "en", "ex", "t1", "kd", "b0", "q", "bv"))
        AR = core.sb("AR", [P, 2, NCH, 2, C])
        Abd, Rbd = core.sb("Abd", [P, 2, 2, NCH, P]), core.sb("Rbd", [P, 2, 2, NCH, P])
        dec = core.sb("dec", [P, 2, 2, NCH])
        Kbd, Bbd, Vbd = (core.sb(n, x4) for n in ("Kbd", "Bbd", "Vbd"))
        Kt, Bt, Vt = (core.sb(n, x4) for n in ("Kt", "Bt", "Vt"))
        NB_ = core.sb("NB", [P, 2, NCH, 2, P])
        KK_ = core.sb("KK", [P, 2, NCH, 2, P])
        X, XT, Pm = (core.sb(n, x4) for n in ("X", "XT", "Pm"))
        S = core.sb("S", [P, 2, P])
        r1, sa = core.sb("r1", [P, 2, P]), core.sb("sa", [P, 2, P])
        ysb = core.sb("ysb", [C, 2, NCH, P])
        bank = [core.ps(f"bank{i}", [P, 512]) for i in range(8)]

        c_l = sem("rw_consts_loaded")
        in_l = [sem(f"rw_in{i}_loaded") for i in range(2)]
        set_up, par_done = sem("rw_setup"), sem("rw_params")
        cur_done, lora_mm, ee_done, cs_done, cx_done = (sem(f"rw_{n}") for n in ("cur", "lora_mm", "ee", "cs", "cx"))
        ep_done, ex_done, ar_done, kb_done, bd_done = (sem(f"rw_{n}") for n in ("ep_en", "ex", "ar", "kb", "bd"))
        q_done, bon_mm, bv_done = (sem(f"rw_{n}") for n in ("q", "bonus_mm", "bv"))
        bv_st = sem("rw_bv_stored")
        dch, pch = sem("rw_dve_chain"), sem("rw_pool_chain")
        tr_mm, tr_out = sem("rw_turned"), sem("rw_turned_out")
        sc_mm, sc_out = sem("rw_scores"), sem("rw_scores_out")
        xt_id, x_tr, x_in = ([sem(f"rw_{n}{d}") for d in range(2)] for n in ("xt_identity", "x_turned", "x_start"))
        p_mm, p_out, q_mm, x_up, qt_mm, xt_up = ([sem(f"rw_{n}{d}") for d in range(2)] for n in (
            "p_mm", "p_out", "q_mm", "x_up", "qt_mm", "xt_up"))
        r1_mm, r1_out, sa_mm, sa_out, s_mm, s_out, y_mm, y_out, y_st = ([sem(f"rw_{n}{d}") for d in range(2)] for n in (
            "r1_mm", "r1_out", "sa_mm", "sa_out", "s_mm", "s_out", "y_mm", "y_out", "y_stored"))
        s_reset = sem("rw_state_reset")
        settled = [sem(f"rw_settled{i}") for i in range(3)]
        EL = 6

        def pos(d, c):
            return c if d == 0 else NCH - 1 - c

        def tokens(n, d):
            g = n % NG
            return g * GT if d == 0 else ((NG - g) % NG) * GT

        def span(first, size):
            return slice(first, first + size) if isinstance(first, int) else bass.ds(first, size)

        def bodies(fori, one):
            with fori(0, NBODY // 2 - 1) as i:
                one(2 * i, 0, True, True)
                one(2 * i + 1, 1, True, True)
            one(NBODY - 2, 0, True, False)
            one(NBODY - 1, 1, False, False)

        with nc.Block() as block:
            @block.sync
            def _(sp):
                def load(n, s):
                    p = n // NG
                    for d in range(2):
                        src = W["heads"][span(p, 1), :, :, span(tokens(n, d), GT)].rearrange("a c f t -> (a c) f t")
                        sp.dma_start(zin[:, s, d], src).then_inc(in_l[s], 16)
                        for i, name in enumerate(("o_w2", "o_a2")):
                            sp.dma_start(wl[HP * d:HP * d + HP, s, i, d, :], A[name][0, d, :, span(p * P, P)]).then_inc(in_l[s], 16)

                def body(n, s, has_next, has_after):
                    if has_after:
                        sp.wait_ge(bv_done, n + 1)
                        sp.wait_ge(bd_done, n + 1)
                        load(n + 2, s)
                    if has_next:
                        sp.wait_ge(bv_done, n + 2)
                        p = (n + 1) // NG
                        for d in range(2):
                            sp.dma_start(W["bv"][d, span(p * P, P), span(tokens(n + 1, d), GT)], bv[:, d]).then_inc(bv_st, 16)
                    for d in range(2):
                        sp.wait_ge(y_out[d], n * 2 + 2)
                        settle(sp, settled[2])
                        sp.dma_start(W["y"][d, span(tokens(n, d), GT), span((n // NG) * P, P)].rearrange("(c t) v -> t c v", t=C),
                                     ysb[:, d]).then_inc(y_st[d], 16)

                with nc.allow_non_contiguous_dma("short vectors as columns"):
                    for d in range(2):
                        sp.dma_start(par[:, :, d], A["o_w0"][0, d].rearrange("(k p) -> p k", p=P)).then_inc(c_l, 16)
                        sp.dma_start(par[:, :, 2 + d], A["o_a0"][0, d].rearrange("(k p) -> p k", p=P)).then_inc(c_l, 16)
                    sp.dma_start(par[:, :, 4], A["o_k_a"][0].rearrange("(k p) -> p k", p=P)).then_inc(c_l, 16)
                    sp.dma_start(par[:, :, 6], A["o_r_k"][0].rearrange("(k h) c -> (h c) k", h=2)).then_inc(c_l, 16)
                for dst, name in ((tri, "tri"), (level, "level"), (same, "same"), (reset, "reset"), (flag, "flag")):
                    sp.dma_start(dst[:], A[name]).then_inc(c_l, 16)
                sp.dma_start(lora[:], W["lora"].rearrange("i c t -> c i t")).then_inc(c_l, 16)
                sp.wait_ge(set_up, 4)
                load(0, 0)
                load(1, 1)
                sp.wait_ge(bv_done, 1)
                for d in range(2):
                    sp.dma_start(W["bv"][d, 0:P, span(tokens(0, d), GT)], bv[:, d]).then_inc(bv_st, 16)
                bodies(sp.Fori, body)
                sp.wait_ge(bv_st, 32 * NBODY)
                for d in range(2):
                    sp.wait_ge(y_st[d], 16 * NBODY)

            @block.gpsimd
            def _(g):
                def operands(n, s):
                    g.wait_ge(cs_done, 2 * n + 2)
                    g.wait_ge(ex_done, n)
                    nc.gpsimd.tensor_tensor(cx[:], cs[:], ee[:, 0], ALU.subtract).then_inc(cx_done, 1)
                    g.wait_ge(cx_done, n + 1)
                    link = Link(g, pch, 6 * n)
                    g.wait_ge(in_l[s], (n - s) * 8 * PER_LOAD + 16 * PER_LOAD)
                    g.wait_ge(tr_mm, 6 * n)
                    for h in range(2):
                        rows, cols = slice(HP * h, HP * h + HP), slice(C * h, C * h + C)
                        settle(g, settled[1])
                        link(nc.gpsimd.tensor_copy(Vbd[rows, :, :, cols], zin[rows, s, :, 3, :].rearrange("p d (c t) -> p d c t", t=C)))
                    g.wait_ge(ar_done, 2 * n + 2)
                    for x, dst in enumerate((Abd, Rbd)):
                        for h in range(2):
                            rows, cols = slice(HP * h, HP * h + HP), slice(C * h, C * h + C)
                            settle(g, settled[1])
                            link(nc.gpsimd.tensor_copy(dst[rows, s, :, :, cols], AR[rows, :, :, x, :]))
                    g.sem_inc(bd_done, 1)

                g.wait_ge(set_up, 11)
                operands(0, 0)

                def body(n, s, has_next, has_after):
                    if has_next:
                        for d in range(2):
                            g.wait_ge(s_out[d], 4 * n)
                            g.wait_ge(y_out[d], 2 * n)
                        operands(n + 1, 1 - s)

                bodies(g.Fori, body)

            @block.tensor
            def _(pe):
                ident = keep["ident"]

                def low_rank(n, s):
                    pe.wait_ge(in_l[s], (n - s) * 8 * PER_LOAD + 16 * PER_LOAD)
                    for d in range(2):
                        pe.wait_ge(x_in[d], n)
                    for i in range(2):
                        for d in range(2):
                            last = pe.matmul(bank[6 + i][:, GT * d:GT * (d + 1)], wl[:, s, i, d, :],
                                             lora[:, i, span(tokens(n, d), GT)], start=True, stop=True)
                    last.then_inc(lora_mm, 1)

                def bonus(n):
                    pe.wait_ge(q_done, n + 1)
                    pe.wait_ge(ee_done, n + 1)
                    pe.matmul(bank[6][:], same[:], q[:].rearrange("p d t -> p (d t)"), start=True, stop=True).then_inc(bon_mm, 1)

                def triangles(n, s):
                    pe.wait_ge(bd_done, n + 1)
                    pe.wait_ge(kb_done, n + 1)
                    for i, src in enumerate((Kbd, Bbd, Vbd)):
                        for d in range(2):
                            if i:
                                pe.wait_ge(tr_out, 6 * n + 2 * i + d - 1)
                            for c in range(NCH):
                                last = pe.transpose(bank[d][:, c * P:(c + 1) * P], src[:, d, c, :], ident[:])
                            last.then_inc(tr_mm, 1)
                    for d in range(2):
                        for x, src in enumerate((Bbd, Kbd)):
                            for c in range(NCH):
                                last = pe.matmul(bank[2 + 2 * d + x][:, c * P:(c + 1) * P], src[:, d, c, :],
                                                 AR[:, d, c].rearrange("p a b -> p (a b)"), start=True, stop=True)
                            last.then_inc(sc_mm, 1)

                def inverse(n):
                    for d in range(2):
                        pe.wait_ge(xt_up[d], 6 * n + 1)
                        pe.wait_ge(bv_done, n + 1)
                        for c in range(NCH):
                            last = pe.transpose(bank[6 + d][:, c * P:(c + 1) * P], XT[:, d, c, :], ident[:])
                        last.then_inc(x_tr[d], 1)
                    for k in range(1, 6):
                        for d in range(2):
                            if k == 1:
                                pe.wait_ge(x_in[d], n + 1)
                                pe.wait_ge(tr_out, 6 * n + 6)
                            else:
                                pe.wait_ge(x_up[d], 4 * n + k - 1)
                            for c in range(NCH):
                                last = pe.matmul(bank[d][:, c * P:(c + 1) * P], NB_[:, d, c, 0, :], X[:, d, c, :], start=True, stop=True)
                            last.then_inc(p_mm[d], 1)
                        for d in range(2):
                            pe.wait_ge(p_out[d], 5 * n + k)
                            pe.wait_ge(xt_up[d], 6 * n + k)
                            if k == 1:
                                pe.wait_ge(sc_out, 16 * n + 16)
                            if k < 5:
                                for c in range(NCH):
                                    last = pe.matmul(bank[2 + d][:, c * P:(c + 1) * P], XT[:, d, c, :], Pm[:, d, c, :], start=True, stop=True)
                                last.then_inc(q_mm[d], 1)
                            for c in range(NCH):
                                last = pe.matmul(bank[4 + d][:, c * P:(c + 1) * P], Pm[:, d, c, :], XT[:, d, c, :], start=True, stop=True)
                            last.then_inc(qt_mm[d], 1)

                def steps(n, s):
                    pe.wait_ge(s_reset, n + 1)
                    pe.wait_ge(sc_out, 16 * n + 16)
                    for c in range(NCH):
                        for d in range(2):
                            u = pos(d, c)
                            pe.wait_ge(s_out[d], 4 * n + c)
                            if c == 0:
                                pe.wait_ge(xt_up[d], 6 * n + 6)
                            pe.matmul(bank[d][:, 0:P], Abd[:, s, d, u, :], S[:, d, :], start=True, stop=False)
                            pe.matmul(bank[d][:, 0:P], KK_[:, d, u, 0, :], Vt[:, d, u, :], start=False, stop=True).then_inc(r1_mm[d], 1)
                        for d in range(2):
                            u = pos(d, c)
                            pe.matmul(bank[2 + d][:, u * P:(u + 1) * P], Rbd[:, s, d, u, :], S[:, d, :], start=True, stop=False)
                            pe.matmul(bank[2 + d][:, u * P:(u + 1) * P], KK_[:, d, u, 1, :], Vt[:, d, u, :], start=False, stop=False)
                        for d in range(2):
                            pe.wait_ge(r1_out[d], 4 * n + c + 1)
                            pe.matmul(bank[d][:, P:2 * P], XT[:, d, pos(d, c), :], r1[:, d, :], start=True, stop=True).then_inc(sa_mm[d], 1)
                        for d in range(2):
                            u = pos(d, c)
                            pe.matmul(bank[4 + d][:, 0:P], ident[:], S[:, d, :], start=True, stop=False)
                            pe.matmul(bank[4 + d][:, 0:P], Kt[:, d, u, :], Vt[:, d, u, :], start=False, stop=False)
                        for d in range(2):
                            u = pos(d, c)
                            pe.wait_ge(sa_out[d], 4 * n + c + 1)
                            pe.matmul(bank[4 + d][:, 0:P], Bt[:, d, u, :], sa[:, d, :], start=False, stop=True).then_inc(s_mm[d], 1)
                        for d in range(2):
                            u = pos(d, c)
                            pe.matmul(bank[2 + d][:, u * P:(u + 1) * P], NB_[:, d, u, 1, :], sa[:, d, :], start=False, stop=True).then_inc(y_mm[d], 1)

                pe.wait_ge(c_l, 16 * 12)
                low_rank(0, 0)
                bonus(0)
                triangles(0, 0)
                inverse(0)

                def body(n, s, has_next, has_after):
                    if has_next:
                        low_rank(n + 1, 1 - s)
                    steps(n, s)
                    if has_next:
                        bonus(n + 1)
                        for d in range(2):
                            pe.wait_ge(y_out[d], 2 * n + 2)
                            pe.wait_ge(s_out[d], 4 * n + 4)
                        triangles(n + 1, 1 - s)
                        inverse(n + 1)

                bodies(pe.Fori, body)

            @block.scalar
            def _(a):
                def rates(n):
                    a.wait_ge(lora_mm, n + 1)
                    a.wait_ge(cur_done, n + 1)
                    a.wait_ge(ar_done, 2 * n)
                    a.wait_ge(kb_done, n)
                    a.wait_ge(cx_done, n)
                    for i in range(2):
                        for d in range(2):
                            last = nc.scalar.activation(ee[:, i, d], bank[6 + i][:, GT * d:GT * (d + 1)], ACT.Exp, scale=-1.0,
                                                        bias=cur[:, 2 * i + d:2 * i + d + 1])
                    last.then_inc(ee_done, 1)

                def decays(n):
                    a.wait_ge(cs_done, 2 * n + 2)
                    nc.scalar.activation(ep[:], cs[:], ACT.Exp, scale=-KAPPA)
                    nc.scalar.activation(en[:], cs[:], ACT.Exp, scale=KAPPA).then_inc(ep_done, 1)

                def decay_before(n):
                    a.wait_ge(cx_done, n + 1)
                    nc.scalar.activation(ex[:], cx[:], ACT.Exp, scale=-KAPPA).then_inc(ex_done, 1)

                def token_major(n):
                    for i, dst in enumerate((Kt, Bt, Vt)):
                        for d in range(2):
                            a.wait_ge(tr_mm, 6 * n + 2 * i + d + 1)
                            nc.scalar.copy(dst[:, d].rearrange("p c t -> p (c t)"), bank[d][:]).then_inc(tr_out, 1)

                def inverse(n):
                    for d in range(2):
                        a.wait_ge(x_tr[d], n + 1)
                        nc.scalar.copy(X[:, d].rearrange("p c t -> p (c t)"), bank[6 + d][:]).then_inc(x_in[d], 1)
                    for k in range(1, 6):
                        for d in range(2):
                            a.wait_ge(p_mm[d], 5 * n + k)
                            a.wait_ge(qt_mm[d], 5 * n + k - 1)
                            nc.scalar.copy(Pm[:, d].rearrange("p c t -> p (c t)"), bank[d][:]).then_inc(p_out[d], 1)

                def step(n, s, c):
                    a.wait_ge(r1_mm[0], 4 * n + c + 1)
                    nc.scalar.copy(r1[:, 0, :], bank[0][:, 0:P]).then_inc(r1_out[0], 1)
                    a.wait_ge(sa_mm[0], 4 * n + c + 1)
                    nc.scalar.copy(sa[:, 0, :], bank[0][:, P:2 * P]).then_inc(sa_out[0], 1)
                    a.wait_ge(s_mm[0], 4 * n + c + 1)
                    a.wait_ge(y_mm[0], 4 * n + c + 1)
                    nc.scalar.activation(S[:, 0, :], bank[4][:, 0:P], ACT.Copy, scale=dec[:, s, 0, c:c + 1]).then_inc(s_out[0], 1)

                def outputs(n):
                    for d in range(2):
                        a.wait_ge(y_mm[d], 4 * n + 4)
                        a.wait_ge(y_st[d], 16 * n)
                        for h in range(2):
                            nc.scalar.copy(ysb[:, d, :, C * h:C * h + C],
                                           bank[2 + d][HP * h:HP * h + HP, :].rearrange("p (c v) -> p c v", v=P)[:, :, HP * h:HP * h + HP])\
                                .then_inc(y_out[d], 1)

                a.wait_ge(c_l, 16 * 12)
                rates(0)
                decays(0)
                decay_before(0)
                token_major(0)
                inverse(0)

                def body(n, s, has_next, has_after):
                    if has_next:
                        rates(n + 1)
                    step(n, s, 0)
                    if has_next:
                        decays(n + 1)
                    step(n, s, 1)
                    if has_next:
                        decay_before(n + 1)
                    step(n, s, 2)
                    step(n, s, 3)
                    outputs(n)
                    if has_next:
                        token_major(n + 1)
                        inverse(n + 1)

                bodies(a.Fori, body)

            @block.vector
            def _(v):
                one_minus = par[:, :, 5]

                def chain(n):
                    return Link(v, dch, EL * n)

                def parameters(n):
                    v.wait_ge(ee_done, n)
                    v.wait_ge(q_done, n)
                    nc.vector.tensor_copy(cur[:], par[:, span(n // NG, 1), :].rearrange("p a b -> p (a b)")).then_inc(cur_done, 1)

                def sums(n, link):
                    v.wait_ge(ee_done, n + 1)
                    link(nc.vector.tensor_scalar(ee[:], ee[:], 1.0, None, ALU.add))
                    link(nc.vector.reciprocal(ee[:], ee[:]))
                    v.wait_ge(ep_done, n)
                    v.wait_ge(cx_done, n)
                    nc.vector.tensor_tensor_scan(cs[:, 0, :], reset[:, 0, :], ee[:, 0, 0, :], 0.0, ALU.mult, ALU.add).then_inc(cs_done, 1)
                    nc.vector.tensor_tensor_scan(cs[:, 1, ::-1], reset[:, 1, ::-1], ee[:, 0, 1, ::-1], 0.0, ALU.mult, ALU.add).then_inc(cs_done, 1)

                def keys(n, s, link):
                    v.wait_ge(in_l[s], (n - s) * 8 * PER_LOAD + 16 * PER_LOAD)
                    link(nc.vector.tensor_scalar(t1[:], ee[:, 1], cur[:, 4:5], cur[:, 5:6], ALU.mult, ALU.add))
                    link(nc.vector.tensor_tensor(kd[:], t1[:], zin[:, s, :, 0, :], ALU.mult))
                    link(nc.vector.scalar_tensor_tensor(out=b0[:], in0=ee[:, 1], scalar=-1.0, in1=zin[:, s, :, 1, :], op0=ALU.mult, op1=ALU.mult))
                    v.wait_ge(bon_mm, n)
                    nc.vector.scalar_tensor_tensor(out=q[:], in0=zin[:, s, :, 2, :], scalar=cur[:, 6:7], in1=kd[:],
                                                   op0=ALU.mult, op1=ALU.mult).then_inc(q_done, 1)

                def queries(n, s):
                    v.wait_ge(ep_done, n + 1)
                    v.wait_ge(ex_done, n + 1)
                    v.wait_ge(sc_mm, 4 * n)
                    v.wait_ge(bd_done, n)
                    by_chunk = lambda t: t.rearrange("p d (c t) -> p d c t", t=C)
                    nc.vector.tensor_tensor(AR[:, :, :, 1, :], by_chunk(ep[:]), by_chunk(zin[:, s, :, 2, :]), ALU.mult).then_inc(ar_done, 1)
                    nc.vector.tensor_tensor(AR[:, :, :, 0, :], by_chunk(ex[:]), by_chunk(zin[:, s, :, 1, :]), ALU.mult).then_inc(ar_done, 1)

                def weights(n, s, link):
                    v.wait_ge(tr_mm, 6 * n)
                    by_chunk = lambda t: t.rearrange("p d (c t) -> p d c t", t=C)
                    for src, dst in ((kd, Kbd), (b0, Bbd)):
                        for h in range(2):
                            rows, cols = slice(HP * h, HP * h + HP), slice(C * h, C * h + C)
                            last = nc.vector.tensor_tensor(dst[rows, :, :, cols], by_chunk(src[rows]), by_chunk(en[rows]), ALU.mult)
                    last.then_inc(kb_done, 1)
                    nc.vector.tensor_copy(dec[:, s, 0, :], ep[:, 0, C - 1::C])
                    link(nc.vector.tensor_copy(dec[:, s, 1, ::-1], ep[:, 1, ::C]))

                def bonus(n, s):
                    v.wait_ge(bon_mm, n + 1)
                    v.wait_ge(bv_st, 32 * n)
                    nc.vector.tensor_tensor(bv[:], bank[6][:].rearrange("p (d t) -> p d t", d=2), zin[:, s, :, 3, :], ALU.mult).then_inc(bv_done, 1)

                def masks(n):
                    for d in range(2):
                        for x, dst in enumerate((NB_, KK_)):
                            v.wait_ge(sc_mm, 4 * n + 2 * d + x + 1)
                            for h in range(2):
                                rows = slice(HP * h, HP * h + HP)
                                for part in range(2):
                                    nc.vector.tensor_tensor(
                                        dst[rows, d, :, part, C * h:C * h + C],
                                        bank[2 + 2 * d + x][rows, :].rearrange("p (c a t) -> p c a t", c=NCH, a=2)[:, :, part, :],
                                        tri[rows, d, part, None, C * h:C * h + C].broadcast_to([HP, NCH, C]), ALU.mult)\
                                        .then_inc(sc_out, 1)

                def start(n, link):
                    for d in range(2):
                        nc.vector.tensor_copy(XT[:, d], keep["ident"][:, None, :].broadcast_to([P, NCH, P])).then_inc(xt_id[d], 1)
                    for d in range(2):
                        v.wait_ge(xt_id[d], n + 1)
                        v.wait_ge(sc_out, 16 * n + 8 * d + 4)
                        settle(v, settled[0])
                        nc.vector.copy_predicated(XT[:, d], level[:, d, 0, None, :].broadcast_to([P, NCH, P]), NB_[:, d, :, 0, :]).then_inc(xt_up[d], 1)

                def inverse(n):
                    by_unit = lambda b: b[:].rearrange("p (c t) -> p c t", c=NCH)
                    for k in range(1, 6):
                        for d in range(2):
                            if k < 5:
                                v.wait_ge(q_mm[d], 4 * n + k)
                                if k == 1:
                                    v.wait_ge(x_in[d], n + 1)
                                settle(v, settled[0])
                                nc.vector.copy_predicated(X[:, d], level[:, 1 - d, k, None, :].broadcast_to([P, NCH, P]), by_unit(bank[2 + d])).then_inc(x_up[d], 1)
                            v.wait_ge(qt_mm[d], 5 * n + k)
                            settle(v, settled[0])
                            nc.vector.copy_predicated(XT[:, d], level[:, d, k, None, :].broadcast_to([P, NCH, P]), by_unit(bank[4 + d])).then_inc(xt_up[d], 1)

                def step(n, s, c):
                    v.wait_ge(r1_mm[1], 4 * n + c + 1)
                    nc.vector.tensor_copy(r1[:, 1, :], bank[1][:, 0:P]).then_inc(r1_out[1], 1)
                    v.wait_ge(sa_mm[1], 4 * n + c + 1)
                    nc.vector.tensor_copy(sa[:, 1, :], bank[1][:, P:2 * P]).then_inc(sa_out[1], 1)
                    v.wait_ge(s_mm[1], 4 * n + c + 1)
                    v.wait_ge(y_mm[1], 4 * n + c + 1)
                    nc.vector.tensor_scalar(S[:, 1, :], bank[5][:, 0:P], dec[:, s, 1, c:c + 1], None, ALU.mult).then_inc(s_out[1], 1)

                for t in (wl, Abd, Rbd, Kbd):
                    nc.vector.memset(t[:], 0.0).then_inc(set_up, 1)
                for t in (Bbd, Vbd, NB_, KK_, S, X, XT):
                    nc.vector.memset(t[:], 0.0).then_inc(set_up, 1)
                v.wait_ge(set_up, 11)
                v.wait_ge(c_l, 16 * 12)
                nc.vector.tensor_scalar(one_minus, par[:, :, 4], -1.0, 1.0, ALU.mult, ALU.add).then_inc(par_done, 1)
                nc.vector.tensor_scalar(par[:, :, 0:4], par[:, :, 0:4], -1.0, None, ALU.mult).then_inc(par_done, 1)
                v.wait_ge(par_done, 2)

                link = chain(0)
                parameters(0)
                sums(0, link)
                keys(0, 0, link)
                queries(0, 0)
                weights(0, 0, link)
                bonus(0, 0)
                masks(0)
                start(0, link)
                inverse(0)

                def body(n, s, has_next, has_after):
                    m, t = n + 1, 1 - s
                    link = chain(m)
                    for d in range(2):
                        v.wait_ge(s_out[d], 4 * n)
                    nc.vector.tensor_scalar(S[:], S[:], flag[:, span(n, 1)], None, ALU.mult).then_inc(s_reset, 1)
                    if has_next:
                        parameters(m)
                    step(n, s, 0)
                    if has_next:
                        sums(m, link)
                    step(n, s, 1)
                    if has_next:
                        keys(m, t, link)
                    step(n, s, 2)
                    if has_next:
                        queries(m, t)
                    step(n, s, 3)
                    if has_next:
                        weights(m, t, link)
                        bonus(m, t)
                        masks(m)
                        start(m, link)
                        inverse(m)

                bodies(v.Fori, body)


def merge1(nc, sem, keep, A, W, out):
    with ExitStack() as stack:
        core = Core(nc, stack, "m1")
        NL = SEQ // P
        G = D // C
        w = core.sb("w", [P, KD, D])
        gn = core.sb("gn", [P, 2, KD])
        half = core.sb("half", [P, G])
        yin = core.sb("yin", [P, 2, 2, D])
        bin_ = core.sb("bonus", [P, 2, 2, KD, P])
        gs = core.sb("gs", [P, 2, KD, P])
        xt = core.sb("xt", [P, 2, D])
        ysum, yc, ysq = (core.sb(n, [P, G, C]) for n in ("ysum", "yc", "ysq"))
        mu, nmu, ss, ms, rs = (core.sb(n, [P, G]) for n in ("mu", "nmu", "ss", "ms", "rs"))
        yn = core.sb("yn", [P, 2, D])
        nT, bsum, mT = (core.sb(n, [P, KD, P]) for n in ("nT", "bsum", "mT"))
        oT = core.sb("oT", [P, 2, KD, P])
        gy = core.sb("gy", [P, D])
        xo = core.sb("xo", [P, 2, D])
        bT = [core.ps(f"bT{i}", [P, 512]) for i in range(2)]
        bY = core.ps("bY", [P, 4, 512])
        c_l, w_l = sem("m1_consts_loaded"), sem("m1_w_loaded")
        y_l, b_l, x_l, x_st = ([sem(f"m1_{n}{i}") for i in range(2)] for n in ("y_loaded", "bonus_loaded", "x_loaded", "x_stored"))
        dch, half_set = sem("m1_dve_chain"), sem("m1_half_set")
        y_used, cen, sq, ms_done, rs_done, yn_done = (sem(f"m1_{n}") for n in ("y_used", "centred", "squared", "ms", "rs", "yn"))
        tr_mm, nT_done, bs_done, m_done, o_done = (sem(f"m1_{n}") for n in ("turned", "nT", "bonus_sum", "merged", "oT"))
        y_mm, gy_done, x_done, y_free = sem("m1_y_mm"), sem("m1_gy"), sem("m1_x"), sem("m1_y_free")
        settled = sem("m1_settled")
        ML = 3

        def rows(t, base=0):
            return slice(base + t * P, base + (t + 1) * P) if isinstance(t, int) else bass.ds(t * P + base, P)

        def iterations(fori, one):
            with fori(0, NL // 2 - 1) as i:
                one(2 * i, 0, True, True)
                one(2 * i + 1, 1, True, True)
            one(NL - 2, 0, True, False)
            one(NL - 1, 1, False, False)

        with nc.Block() as block:
            @block.sync
            def _(sp):
                def load_y(t, s):
                    for d in range(2):
                        sp.dma_start(yin[:, s, d, :], W["y"][d, rows(t, CTX), :]).then_inc(y_l[s], 16)

                def load_bonus(t, s):
                    for d in range(2):
                        sp.dma_start(bin_[:, s, d], W["bv"][d, :, rows(t, CTX)].rearrange("(k p) t -> p k t", p=P)).then_inc(b_l[s], 16)
                    sp.dma_start(gs[:, s], W["gsT"][:, :, rows(t)].rearrange("k p t -> p k t")).then_inc(b_l[s], 16)

                def load_x(t, s):
                    sp.dma_start(xt[:, s, :], W["x1"][rows(t, CTX), :]).then_inc(x_l[s], 16)

                with nc.allow_non_contiguous_dma("short vectors as columns"):
                    for i, name in enumerate(("o_gn_w", "o_gn_b")):
                        sp.dma_start(gn[:, i, :], A[name][0].rearrange("(k p) -> p k", p=P)).then_inc(c_l, 16)
                for t in range(2):
                    load_y(t, t)
                    load_bonus(t, t)
                sp.dma_start(w[:], A["o_w_out"][0].rearrange("(k p) n -> p k n", p=P)).then_inc(w_l, 16)
                for t in range(2):
                    load_x(t, t)
                for t in range(2):
                    sp.wait_ge(y_used, t + 1)
                    load_y(t + 2, t)
                sp.wait_ge(o_done, 1)
                load_bonus(2, 0)

                def one(t, s, next1, next2, next3, next4):
                    if next4:
                        sp.wait_ge(y_used, t + 3)
                        load_y(t + 4, s)
                    if next3:
                        sp.wait_ge(o_done, t + 2)
                        settle(sp, settled)
                        load_bonus(t + 3, 1 - s)
                    sp.wait_ge(x_done, t + 1)
                    sp.dma_start(out[0, rows(t), :], xo[:, s, :]).then_inc(x_st[s], 16)
                    if next2:
                        load_x(t + 2, s)

                with sp.Fori(0, NL // 2 - 2) as i:
                    one(2 * i, 0, True, True, True, True)
                    one(2 * i + 1, 1, True, True, True, True)
                one(NL - 4, 0, True, True, True, False)
                one(NL - 3, 1, True, True, False, False)
                one(NL - 2, 0, True, False, False, False)
                one(NL - 1, 1, False, False, False, False)
                for s in range(2):
                    sp.wait_ge(x_st[s], 16 * NL // 2)

            @block.gpsimd
            def _(g):
                def bonus(t, s):
                    g.wait_ge(b_l[s], (t - s) * 24 + 48)
                    g.wait_ge(m_done, t)
                    nc.gpsimd.tensor_tensor(bsum[:], bin_[:, s, 0], bin_[:, s, 1], ALU.add).then_inc(bs_done, 1)
                    g.wait_ge(bs_done, t + 1)

                def rstd(t):
                    g.wait_ge(ms_done, t + 1)
                    g.wait_ge(yn_done, t)
                    nc.gpsimd.tensor_tensor(rs[:], ms[:], half[:], ALU.pow).then_inc(rs_done, 1)
                    g.wait_ge(rs_done, t + 1)

                g.wait_ge(half_set, 1)
                rstd(0)
                rstd(1)
                bonus(0, 0)

                def one(t, s, next1, next2):
                    if next1:
                        bonus(t + 1, 1 - s)
                    if next2:
                        rstd(t + 2)

                iterations(g.Fori, one)

            @block.tensor
            def _(pe):
                def turn(t, s):
                    pe.wait_ge(yn_done, t + 1)
                    pe.wait_ge(nT_done, t)
                    for k in range(KD):
                        last = pe.transpose(bT[k // 4][:, (k % 4) * P:(k % 4 + 1) * P], yn[:, s, k * P:(k + 1) * P], keep["ident"][:])
                    last.then_inc(tr_mm, 1)

                def one(t, s, next1, next2):
                    if next1:
                        turn(t + 1, 1 - s)
                    pe.wait_ge(o_done, t + 1)
                    pe.wait_ge(y_free, t + 1)
                    for j in range(2):
                        for k in range(KD):
                            last = pe.matmul(bY[:, 2 * s + j, :], oT[:, s, k, :], w[:, k, j * 512:(j + 1) * 512],
                                             start=(k == 0), stop=(k == KD - 1))
                        last.then_inc(y_mm, 1)

                turn(0, 0)
                pe.wait_ge(w_l, 16)
                iterations(pe.Fori, one)

            @block.scalar
            def _(a):
                def square(t):
                    a.wait_ge(cen, t + 1)
                    a.wait_ge(ms_done, t)
                    nc.scalar.activation(ysq[:], yc[:], ACT.Square).then_inc(sq, 1)

                def evict(t):
                    a.wait_ge(tr_mm, t + 1)
                    a.wait_ge(m_done, t)
                    for k in range(KD):
                        last = nc.scalar.activation(nT[:, k, :], bT[k // 4][:, (k % 4) * P:(k % 4 + 1) * P], ACT.Identity,
                                                    scale=gn[:, 0, k:k + 1], bias=gn[:, 1, k:k + 1])
                    last.then_inc(nT_done, 1)

                square(0)
                square(1)
                a.wait_ge(c_l, 32)
                evict(0)

                def one(t, s, next1, next2):
                    if next1:
                        evict(t + 1)
                    if next2:
                        square(t + 2)

                iterations(a.Fori, one)

            @block.vector
            def _(v):
                groups = lambda small: small[:, :, None].broadcast_to([P, G, C])

                def centre(t, s, link):
                    v.wait_ge(y_l[s], (t - s) * 16 + 32)
                    nc.vector.tensor_tensor(ysum[:].rearrange("p g c -> p (g c)"), yin[:, s, 0, :], yin[:, s, 1, :], ALU.add).then_inc(y_used, 1)
                    v.wait_ge(y_used, t + 1)
                    link(nc.vector.tensor_reduce(mu[:], ysum[:], AX.X, ALU.add))
                    link(nc.vector.tensor_scalar(nmu[:], mu[:], -1.0 / C, None, ALU.mult))
                    nc.vector.tensor_tensor(yc[:], ysum[:], groups(nmu), ALU.add).then_inc(cen, 1)

                def normalise(t, s, link):
                    v.wait_ge(sq, t + 1)
                    link(nc.vector.tensor_reduce(ss[:], ysq[:], AX.X, ALU.add))
                    v.wait_ge(rs_done, t)
                    nc.vector.tensor_scalar(ms[:], ss[:], 1.0 / C, GN_EPS, ALU.mult, ALU.add).then_inc(ms_done, 1)

                def scale(t, s):
                    v.wait_ge(rs_done, t + 1)
                    v.wait_ge(cen, t + 1)
                    if not (isinstance(t, int) and t < 2):
                        v.wait_ge(tr_mm, t - 1)
                    nc.vector.tensor_tensor(yn[:, s, :].rearrange("p (g c) -> p g c", c=C), yc[:], groups(rs), ALU.mult).then_inc(yn_done, 1)

                def merge(t, s):
                    v.wait_ge(nT_done, t + 1)
                    v.wait_ge(bs_done, t + 1)
                    nc.vector.tensor_tensor(mT[:], nT[:], bsum[:], ALU.add).then_inc(m_done, 1)
                    v.wait_ge(m_done, t + 1)
                    v.wait_ge(b_l[s], (t - s) * 24 + 48)
                    if not (isinstance(t, int) and t < 2):
                        v.wait_ge(y_mm, 2 * t - 2)
                    nc.vector.tensor_tensor(oT[:, s], mT[:], gs[:, s], ALU.mult).then_inc(o_done, 1)

                def residual(t, s):
                    v.wait_ge(x_done, t)
                    for j in range(2):
                        v.wait_ge(y_mm, 2 * t + j + 1)
                        nc.vector.tensor_tensor(gy[:, j * 512:(j + 1) * 512], bY[:, 2 * s + j, :],
                                                keep["gate"][:, 2, j * 512:(j + 1) * 512], ALU.mult).then_inc(gy_done, 1)
                    v.wait_ge(gy_done, 2 * t + 2)
                    v.sem_inc(y_free, 1)
                    v.wait_ge(x_l[s], (t - s) * 8 + 16)
                    v.wait_ge(x_st[s], (t - s) * 8)
                    nc.vector.tensor_tensor(xo[:, s, :], gy[:], xt[:, s, :], ALU.add).then_inc(x_done, 1)

                nc.vector.memset(half[:], -0.5).then_inc(half_set, 1)
                v.sem_inc(y_free, 2)
                for t in range(2):
                    link = Link(v, dch, ML * t)
                    centre(t, t, link)
                    normalise(t, t, link)
                    scale(t, t)
                merge(0, 0)

                def one(t, s, next1, next2):
                    link = Link(v, dch, ML * (t + 2))
                    if next2:
                        centre(t + 2, s, link)
                    if next1:
                        merge(t + 1, 1 - s)
                    if next2:
                        normalise(t + 2, s, link)
                        scale(t + 2, s)
                    residual(t, s)

                iterations(v.Fori, one)


def clear_semaphores(nc, sems):
    with nc.Block() as block:
        @block.sync
        def _(sp):
            for one in sems:
                sp.sem_clear(one)


def program(nc, A, out):
    with ExitStack() as stack:
        first_half, second_half = ExitStack(), stack
        used = []

        def sem_of(owner):
            def sem(name):
                used.append(owner.enter_context(nc.semaphore(name)))
                return used[-1]
            return sem

        sem = sem_of(first_half)

        def keep_sb(name, shape):
            return stack.enter_context(nc.sbuf_tensor(f"keep_{name}", shape, F32))

        def scratch(name, shape):
            return nc.dram_tensor(f"scratch_{name}", shape, F32).ap()

        keep = {
            "ident": keep_sb("ident", [P, P]),
            "scale": keep_sb("scale", [P, 2, KD, 2]),
            "shift": keep_sb("shift", [P, 2, KD, 2]),
            "gate": keep_sb("gate", [P, 3, D]),
        }
        W = {
            "q": scratch("q", (HEADS, T, QK)), "k": scratch("k", (HEADS, T, QK)), "v": scratch("v", (HEADS, T, VH)),
            "gate": scratch("gate", (T, GW)), "fx": scratch("fx", (T, 2 * FW)),
            "mix": scratch("mix", (T, GW)), "z": scratch("z", (2, N2, P, FW)),
            "x1": scratch("x1", (T, D)),
            "heads": scratch("heads", (PAIRS, P, 4, T)), "gsT": scratch("gsT", (PAIRS, P, SEQ)), "lora": scratch("lora", (2, P, T)),
            "bv": scratch("bv", (2, D, T)), "y": scratch("y", (2, T, D)),
        }
        modulate(nc, sem, keep, A)
        project0(nc, sem, keep, A, W)
        attend(nc, sem, keep, A, W)
        fourier(nc, sem, keep, A, W)
        with nc.sbuf_tensor("keep_hT", [P, KD, T], F32) as hT:
            keep["hT"] = hT
            merge0(nc, sem, keep, A, W)
            project1(nc, sem, keep, A, W)
        clear_semaphores(nc, used)
        first_half.close()
        sem = sem_of(second_half)
        rwkv(nc, sem, keep, A, W)
        merge1(nc, sem, keep, A, W, out)


_INS = ["x", "c", "ctx", "c_ctx", "ada_w", "ada_b", "norm_g", "e_w_in", "e_kv_norm", "e_q_norm", "e_w_uq", "e_w_ukv",
        "e_q_head_norm", "e_k_head_norm", "e_w_fnet", "e_w_out", "o_w_in", "o_shift_w", "o_w0", "o_w2", "o_a0",
        "o_a2", "o_k_k", "o_k_a", "o_r_k", "o_gn_w", "o_gn_b", "o_w_out"]


def kernel(**inputs):
    import numpy as _np
    import concourse.bacc as _bacc
    from concourse import mybir as _mybir
    from concourse.bass_utils import run_bass_kernel_spmd as _run

    nc = _bacc.Bacc("TRN2", target_bir_lowering=False, num_devices=1)
    arrays, A = {}, {}
    tables = constant_tables()
    for name in _INS + list(tables):
        a = _np.ascontiguousarray(tables[name] if name in tables else inputs[name])
        arrays[f"in_{name}_dram"] = a
        A[name] = nc.dram_tensor(f"in_{name}_dram", a.shape, _mybir.dt.from_np(a.dtype), kind="ExternalInput").ap()
    out = nc.dram_tensor("out_0_dram", (1, SEQ, D), _mybir.dt.float32, kind="ExternalOutput").ap()
    program(nc, A, out)
    r = _run(nc, [arrays], core_ids=[0])
    return r.results[0]["out_0_dram"]
```

```python
from contextlib import ExitStack

import numpy as np

import concourse.bass as bass
from concourse import mybir

F32 = mybir.dt.float32
BF16 = mybir.dt.bfloat16
I32 = mybir.dt.int32
ALU = mybir.AluOpType
ACT = mybir.ActivationFunctionType
AX = mybir.AxisListType

P = 128
D = 1024
SEQ = 2048
CTX = 256
T = CTX + SEQ
NT = T // P
NC_CTX = CTX // P
KD = D // P
EPS = 1e-6

HEADS = 8
NOPE = 64
ROPE = 32
QK = NOPE + ROPE
VH = 64
QL = 384
KVL = 256
KVQ = KVL + ROPE + QL
FG = 4
FD = 128
FW = FG * FD
GW = HEADS * VH + FW
E_Q0 = KVL + ROPE
E_F0 = E_Q0 + QL
E_G0 = E_F0 + FW
EVEN_IN = E_G0 + GW
GRID_W = 64
N2 = SEQ // P


def constant_tables():
    k = np.arange(P)
    ang = 2 * np.pi * np.outer(k, k) / FD
    norm = 1.0 / np.sqrt(SEQ * FD)
    chan = np.stack([np.cos(ang), np.sin(ang)], 1) * norm
    n1, k1 = np.arange(P), np.arange(P)
    t = np.arange(N2)[None, :, None] + N2 * n1[:, None, None]
    a1 = 2 * np.pi * (t * k1[None, None, :] % SEQ) / SEQ
    step1 = np.stack([np.cos(a1), np.sin(a1), -np.sin(a1)], 2)
    a2 = 2 * np.pi * np.outer(np.arange(N2), np.arange(N2)) / N2
    eye8 = np.eye(P // N2)
    step2 = np.stack([np.kron(np.cos(a2), eye8), -np.kron(np.sin(a2), eye8)], 1)
    tc = np.arange(CTX)
    ac = 2 * np.pi * np.outer(tc, tc) / CTX
    up = np.sqrt(SEQ / CTX)
    ctxdft = np.stack([np.cos(ac) * up, -np.sin(ac) * up], 1)
    ctxdft = ctxdft.reshape(CTX // P, P, 2, CTX).transpose(1, 0, 2, 3)
    nf = ROPE // 4
    pos = np.arange(SEQ)
    inv = 1.0 / (10000.0 ** (np.arange(nf) / nf))
    angle = np.stack([(pos // GRID_W)[:, None] * inv, (pos % GRID_W)[:, None] * inv], 1)
    cos = np.concatenate([np.ones((CTX, 2, nf)), np.cos(angle)])
    sin = np.concatenate([np.zeros((CTX, 2, nf)), np.sin(angle)])
    rope = np.concatenate([np.stack([cos, cos], 2).reshape(T, -1), np.stack([-sin, sin], 2).reshape(T, -1)], 1)
    f = np.float32
    return {
        "ident": np.eye(P, dtype=f), "chan": chan.astype(f), "step1": step1.astype(f), "step2": step2.astype(f),
        "ctxdft": ctxdft.astype(f), "rope": rope.astype(f),
    } | rwkv_tables()


HP = 64
C = 64
GT = 256
NG = T // GT
NCH = GT // C
PAIRS = D // P
KAPPA = float(np.exp(-0.5))
GN_EPS = 64e-5
SHIFT_ROWS = 3
O_WD0 = 2 * D
O_AD0 = O_WD0 + P
O_R0 = O_AD0 + P
O_G0 = O_R0 + D


def rwkv_tables():
    s = np.arange(P)
    head = s // C
    same = head[:, None] == head[None, :]
    si, ti = s[:, None] % C, s[None, :] % C
    out = {}
    masks = []
    for before in (si < ti, si > ti):
        masks.append(np.stack([same & before, same & (before | (si == ti))], 1))
    out["tri"] = np.stack(masks, 1).astype(np.float32)
    lev = []
    for order in (0, 1):
        for b in range(6):
            lo, hi = (ti, si) if order == 0 else (si, ti)
            late, early = lo, hi
            lev.append(same & (si >> (b + 1) == ti >> (b + 1)) & ((late >> b) % 2 == 1) & ((early >> b) % 2 == 0))
    out["level"] = np.stack(lev, 1).reshape(P, 2, 6, P).astype(np.int32)
    out["same"] = same.astype(np.float32)
    z = np.ones((P, 2, GT), np.float32)
    z[:, 0, ::C] = 0
    z[:, 1, C - 1::C] = 0
    out["reset"] = z
    n = np.arange(PAIRS * NG)
    out["flag"] = np.broadcast_to((n % NG != NG - 1).astype(np.float32), (P, PAIRS * NG)).copy()
    return out


class Core:

    def __init__(self, nc, stack, tag):
        self.nc, self.stack, self.tag = nc, stack, tag

    def sb(self, name, shape, dt=F32):
        return self.stack.enter_context(self.nc.sbuf_tensor(f"{self.tag}_{name}", shape, dt))

    def ps(self, name, shape, dt=F32):
        return self.stack.enter_context(self.nc.psum_tensor(f"{self.tag}_{name}", shape, dt))


class Link:

    def __init__(self, eng, sem, base=0):
        self.eng, self.sem, self.base, self.n = eng, sem, base, 0

    def __call__(self, ins):
        self.n += 1
        ins.then_inc(self.sem, 1)
        self.eng.wait_ge(self.sem, self.base + self.n)


def settle(eng, sem):
    eng.sem_inc(sem, 1)


def modulate(nc, sem, keep, A):
    with ExitStack() as stack:
        core = Core(nc, stack, "mod")
        HALF = 3 * D // 2
        NBLK = 2 * 3 * D // 512
        PER_SLAB = NBLK // 4
        w = core.sb("w", [P, 2, KD, HALF])
        cond = core.sb("cond", [P, KD, 2])
        act = core.sb("act", [P, KD, 2])
        bias = core.sb("bias", [P, 2, 3 * KD])
        norm_g = core.sb("norm_g", [P, 2, KD])
        mod = core.sb("mod", [P, 2, 3 * KD, 2])
        diag = core.sb("diag", [P, 3, KD, P])
        ones = core.sb("ones", [P, P])
        acc = core.ps("acc", [P, 2 * 3 * KD, 2])
        row = core.sb("row", [2, 4, 512])
        bR = [core.ps(f"bR{i}", [2, 512]) for i in range(2)]
        row_done, row_sb = sem("mod_row_done"), sem("mod_row_copied")
        rows = [core.ps(f"rows{i}", [P, 512]) for i in range(2)]
        small, wload = sem("mod_small_loaded"), [sem(f"mod_w{i}_loaded") for i in range(2)]
        silu_done, mm_done, added = sem("mod_silu_done"), sem("mod_mm_done"), sem("mod_added")
        diag_done, row_mm, row_out, set_up = sem("mod_diag"), sem("mod_row_mm"), sem("mod_row_out"), sem("mod_setup")

        with nc.Block() as block:
            @block.sync
            def _(sp):
                with nc.allow_non_contiguous_dma("short vectors as columns"):
                    sp.dma_start(cond[:, :, 0], A["c"].rearrange("a (k p) -> p (a k)", p=P)).then_inc(small, 16)
                    sp.dma_start(cond[:, :, 1], A["c_ctx"].rearrange("(k p) -> p k", p=P)).then_inc(small, 16)
                    for layer in range(2):
                        sp.dma_start(bias[:, layer, :], A["ada_b"][layer].rearrange("(m p) -> p m", p=P)).then_inc(small, 16)
                        sp.dma_start(norm_g[:, layer, :], A["norm_g"][layer].rearrange("(k p) -> p k", p=P)).then_inc(small, 16)
                sp.dma_start(keep["ident"][:], A["ident"]).then_inc(small, 16)
                for n in range(4):
                    layer, half = divmod(n, 2)
                    if n >= 2:
                        sp.wait_ge(row_done, PER_SLAB * (n - 1))
                    sp.dma_start(w[:, n % 2], A["ada_w"][layer, :, half * HALF:(half + 1) * HALF]
                                 .rearrange("(k p) n -> p k n", p=P)).then_inc(wload[n % 2], 16)
                sp.dma_start(keep["w_in"][:], A["e_w_in"][0].rearrange("(k p) n -> p k n", p=P)).then_inc(keep["w_in_loaded"], 16)

            @block.scalar
            def _(a):
                a.wait_ge(small, 7 * 16)
                nc.scalar.activation(act[:], cond[:], ACT.Silu).then_inc(silu_done, 1)
                for j in range(NBLK):
                    a.wait_ge(row_done, j + 1)
                    if j >= 4:
                        a.wait_ge(mm_done, j - 3)
                    nc.scalar.copy(row[:, j % 4, :], bR[j % 2][:]).then_inc(row_sb, 1)
                for i in range(6):
                    a.wait_ge(row_mm, i + 1)
                    nc.scalar.copy(keep["gate"][:, i // 2, (i % 2) * 512:(i % 2 + 1) * 512], rows[i % 2][:]).then_inc(row_out, 1)

            @block.tensor
            def _(pe):
                pe.wait_ge(silu_done, 1)
                def turn(j):
                    pe.wait_ge(row_sb, j + 1)
                    for i in range(4):
                        last = pe.matmul(acc[:, 4 * j + i, :], row[:, j % 4, i * P:(i + 1) * P], keep["ident"][0:2, 0:2],
                                         start=True, stop=True)
                    last.then_inc(mm_done, 1)

                for j in range(NBLK):
                    n, at = divmod(j, PER_SLAB)
                    pe.wait_ge(wload[n % 2], 16 * (n // 2 + 1))
                    if j >= 2:
                        pe.wait_ge(row_sb, j - 1)
                    for k in range(KD):
                        last = pe.matmul(bR[j % 2][:], act[:, k, :], w[:, n % 2, k, at * 512:(at + 1) * 512],
                                         start=(k == 0), stop=(k == KD - 1))
                    last.then_inc(row_done, 1)
                    if j:
                        turn(j - 1)
                turn(NBLK - 1)
                pe.wait_ge(diag_done, 3 * KD)
                pe.wait_ge(set_up, 1)
                for i in range(6):
                    if i >= 2:
                        pe.wait_ge(row_out, i - 1)
                    pe.matmul(rows[i % 2][:], ones[:], diag[:, i // 2, (i % 2) * 4:(i % 2) * 4 + 4, :]
                              .rearrange("p a b -> p (a b)"), start=True, stop=True).then_inc(row_mm, 1)

            @block.vector
            def _(v):
                nc.vector.memset(ones[:], 1.0).then_inc(set_up, 1)
                v.wait_ge(mm_done, NBLK)
                v.wait_ge(small, 7 * 16)
                psum = acc[:].rearrange("p (l m) s -> p l m s", l=2)
                for s in range(2):
                    nc.vector.tensor_tensor(mod[:, :, :, s], psum[:, :, :, s], bias[:], ALU.add).then_inc(added, 1)
                v.wait_ge(added, 2)
                for s in range(2):
                    nc.vector.scalar_tensor_tensor(out=keep["scale"][:, :, :, s], in0=mod[:, :, KD:2 * KD, s], scalar=1.0,
                                                   in1=norm_g[:], op0=ALU.add, op1=ALU.mult)
                    nc.vector.tensor_copy(keep["shift"][:, :, :, s], mod[:, :, 0:KD, s])
                for i, (layer, s) in enumerate(((0, 0), (0, 1), (1, 0))):
                    for k in range(KD):
                        nc.vector.tensor_scalar(diag[:, i, k, :], keep["ident"][:], mod[:, layer, 2 * KD + k, s:s + 1],
                                                None, ALU.mult).then_inc(diag_done, 1)


def project0(nc, sem, keep, A, W):
    with ExitStack() as stack:
        core = Core(nc, stack, "p0")
        w_in, w_loaded = keep["w_in"], keep["w_in_loaded"]
        w_ukv = core.sb("w_ukv", [P, 2, HEADS * 128])
        w_uq = core.sb("w_uq", [P, 3, HEADS * QK])
        w_fn = core.sb("w_fn", [P, FG, FD])
        chan = core.sb("chan", [P, 2, FD])
        m_fn = core.sb("m_fn", [P, FG, 2 * FD])
        kvn = core.sb("kvn", [P, 2])
        qn = core.sb("qn", [P, 3])
        gk = core.sb("gk", [P, 2, QK])
        half = core.sb("half", [P, 32])
        xt = core.sb("xt", [P, 2, D])
        xsq = core.sb("xsq", [P, D])
        xss = core.sb("xss", [P, 1])
        xms = core.sb("xms", [P, 1])
        xr = core.sb("xr", [P, 1])
        xn = core.sb("xn", [P, D])
        hT = core.sb("hT", [P, 2, KD, P])
        rope = core.sb("rope", [P, 2, 2 * ROPE])
        lss = core.sb("lss", [P, 2])
        lms = core.sb("lms", [P, 2])
        lr = core.sb("lr", [P, 2])
        lsq = core.sb("lsq", [P, KVL + QL])
        ckv = core.sb("ckv", [P, KVL])
        cq = core.sb("cq", [P, QL])
        kpe = core.sb("kpe", [P, ROPE])
        ckvT = core.sb("ckvT", [P, 2, P])
        cqT = core.sb("cqT", [P, 3, P])
        fT = core.sb("fT", [P, FG, P])
        qk = [core.sb(f"{n}_heads", [P, HEADS, QK]) for n in "qk"]
        hsq = core.sb("hsq", [P, HEADS, QK])
        hss = core.sb("hss", [P, HEADS])
        hms = core.sb("hms", [P, HEADS])
        hr = core.sb("hr", [P, HEADS])
        rc = core.sb("rc", [P, HEADS, ROPE])
        rs = core.sb("rs", [P, HEADS, ROPE])
        vt = core.sb("vt", [P, HEADS, VH])
        gt = core.sb("gt", [P, GW])
        fx = core.sb("fx", [P, 2, FG, FD])

        bIn = core.ps("bIn", [P, 2, 512])
        bG = core.ps("bG", [P, 2, 512])
        bF = core.ps("bF", [P, 512])
        bT = core.ps("bT", [P, 512])
        bX = core.ps("bX", [P, 2, 512])

        c_loaded = sem("p0_consts_loaded")
        x_loaded = [sem(f"p0_x_loaded{i}") for i in range(2)]
        rope_loaded = [sem(f"p0_rope_loaded{i}") for i in range(2)]
        prep, m_mm, m_out = sem("p0_prep"), sem("p0_m_mm"), sem("p0_m_out")
        x_sq, x_ms, x_rs, x_n = sem("p0_x_sq"), sem("p0_x_ms"), sem("p0_x_rs"), sem("p0_x_normed")
        x_tr, x_hT = sem("p0_x_transposed"), sem("p0_hT_ready")
        in_kvq, in_gate, in_f = sem("p0_kvq_mm"), sem("p0_gate_mm"), sem("p0_f_mm")
        l_sq, l_ms, l_rs, l_n = sem("p0_l_sq"), sem("p0_l_ms"), sem("p0_l_rs"), sem("p0_l_normed")
        l_tr, l_T = sem("p0_l_transposed"), sem("p0_lT_ready")
        f_T, fx_mm, fx_out, fx_st = sem("p0_fT"), sem("p0_fx_mm"), sem("p0_fx_out"), sem("p0_fx_stored")
        kv_mm, q_mm, v_out, v_st = sem("p0_kv_mm"), sem("p0_q_mm"), sem("p0_v_out"), sem("p0_v_stored")
        k_out, q_out, kpe_out = sem("p0_k_out"), sem("p0_q_out"), sem("p0_kpe_out")
        g_out, g_st = sem("p0_gate_out"), sem("p0_gate_stored")
        h_ms, h_rs, h_done, h_st = sem("p0_h_ms"), sem("p0_h_rs"), sem("p0_head_done"), sem("p0_head_stored")
        dchain, pchain = sem("p0_dve_chain"), sem("p0_pool_chain")
        LINKS = 22

        with nc.Block() as block:
            @block.sync
            def _(sp):
                with nc.allow_non_contiguous_dma("short vectors as columns"):
                    sp.dma_start(kvn[:], A["e_kv_norm"][0].rearrange("(k p) -> p k", p=P)).then_inc(c_loaded, 16)
                    sp.dma_start(qn[:], A["e_q_norm"][0].rearrange("(k p) -> p k", p=P)).then_inc(c_loaded, 16)
                    sp.dma_start(gk[:, 0, :], A["e_q_head_norm"].broadcast_to([P, QK])).then_inc(c_loaded, 16)
                    sp.dma_start(gk[:, 1, :], A["e_k_head_norm"].broadcast_to([P, QK])).then_inc(c_loaded, 16)
                sp.dma_start(w_ukv[:], A["e_w_ukv"][0].rearrange("(k p) n -> p k n", p=P)).then_inc(c_loaded, 16)
                sp.dma_start(w_uq[:], A["e_w_uq"][0].rearrange("(k p) n -> p k n", p=P)).then_inc(c_loaded, 16)
                sp.dma_start(w_fn[:], A["e_w_fnet"][0].rearrange("g c d -> c g d")).then_inc(c_loaded, 16)
                sp.dma_start(chan[:], A["chan"]).then_inc(c_loaded, 16)
                for i in range(2):
                    sp.dma_start(xt[:, i, :], A["ctx"][0, i * P:(i + 1) * P, :]).then_inc(x_loaded[i], 16)
                    sp.dma_start(rope[:, i, :], A["rope"][i * P:(i + 1) * P, :]).then_inc(rope_loaded[i], 16)

                def store(t):
                    rows = slice(t * P, (t + 1) * P) if isinstance(t, int) else bass.ds(t * P, P)
                    sp.wait_ge(g_out, t + 1)
                    sp.dma_start(W["gate"][rows, :], gt[:]).then_inc(g_st, 16)
                    sp.wait_ge(fx_out, 2 * t + 2)
                    sp.dma_start(W["fx"][rows, :], fx[:].rearrange("p r g c -> p (r g c)")).then_inc(fx_st, 16)
                    sp.wait_ge(v_out, 2 * t + 2)
                    sp.dma_start(W["v"][:, rows, :].rearrange("h p d -> p h d"), vt[:]).then_inc(v_st, 16)
                    for j, name in enumerate("qk"):
                        sp.wait_ge(h_done, 2 * t + j + 1)
                        sp.dma_start(W[name][:, rows, :].rearrange("h p d -> p h d"), qk[j][:]).then_inc(h_st, 16)

                with sp.Fori(0, NT // 2 - 1) as i:
                    for s in range(2):
                        t = 2 * i + s
                        sp.wait_ge(x_n, t + 1)
                        sp.dma_start(xt[:, s, :], A["x"][0, bass.ds(t * P, P), :]).then_inc(x_loaded[s], 16)
                        store(t)
                        sp.dma_start(rope[:, s, :], A["rope"][bass.ds((t + 2) * P, P), :]).then_inc(rope_loaded[s], 16)
                store(NT - 2)
                store(NT - 1)
                sp.wait_ge(g_st, 16 * NT)
                sp.wait_ge(fx_st, 16 * NT)
                sp.wait_ge(v_st, 16 * NT)
                sp.wait_ge(h_st, 32 * NT)

            @block.gpsimd
            def _(g):
                nc.gpsimd.memset(half[:], -0.5).then_inc(pchain, 1)
                g.wait_ge(pchain, 1)

                def rsqrt(out, ms, n):
                    return nc.gpsimd.tensor_tensor(out, ms, half[:, 0:n], ALU.pow)

                g.wait_ge(x_ms, 1)
                rsqrt(xr[:], xms[:], 1).then_inc(x_rs, 1)
                with g.Fori(0, NT - 1) as t:
                    g.wait_ge(x_ms, t + 2)
                    g.wait_ge(x_n, t + 1)
                    rsqrt(xr[:], xms[:], 1).then_inc(x_rs, 1)
                    g.wait_ge(l_ms, t + 1)
                    g.wait_ge(l_n, 2 * t)
                    rsqrt(lr[:], lms[:], 2).then_inc(l_rs, 1)
                    for j in range(2):
                        g.wait_ge(h_ms, 2 * t + j + 1)
                        rsqrt(hr[:], hms[:], HEADS).then_inc(h_rs, 1)
                g.wait_ge(l_ms, NT)
                g.wait_ge(l_n, 2 * NT - 2)
                rsqrt(lr[:], lms[:], 2).then_inc(l_rs, 1)
                for j in range(2):
                    g.wait_ge(h_ms, 2 * NT - 1 + j)
                    rsqrt(hr[:], hms[:], HEADS).then_inc(h_rs, 1)

            @block.tensor
            def _(pe):
                ident = keep["ident"]
                pe.wait_ge(c_loaded, 8 * 16)
                for g in range(FG):
                    for j in range(2):
                        last = pe.matmul(bG[:, g // 2, (g % 2 * 2 + j) * FD:(g % 2 * 2 + j + 1) * FD], chan[:, j, :],
                                         w_fn[:, g, :], start=True, stop=True)
                last.then_inc(m_mm, 1)

                def transpose_x():
                    for k in range(KD):
                        last = pe.transpose(bX[:, k // 4, (k % 4) * P:(k % 4 + 1) * P], xn[:, k * P:(k + 1) * P], ident[:])
                    last.then_inc(x_tr, 1)

                def tile(t, s, more):
                    pe.wait_ge(x_hT, t + 1)
                    pe.wait_ge(q_out, t)
                    for k in range(KD):
                        pe.matmul(bIn[:, 0, 0:E_Q0], hT[:, s, k, :], w_in[:, k, 0:E_Q0], start=(k == 0), stop=(k == KD - 1))
                    for k in range(KD):
                        last = pe.matmul(bIn[:, 1, 0:QL], hT[:, s, k, :], w_in[:, k, E_Q0:E_F0], start=(k == 0), stop=(k == KD - 1))
                    last.then_inc(in_kvq, 1)
                    pe.wait_ge(fx_out, 2 * t)
                    for j in range(2):
                        for k in range(KD):
                            last = pe.matmul(bG[:, j, :], hT[:, s, k, :], w_in[:, k, E_G0 + 512 * j:E_G0 + 512 * (j + 1)],
                                             start=(k == 0), stop=(k == KD - 1))
                    last.then_inc(in_gate, 1)
                    if more:
                        pe.wait_ge(x_n, t + 2)
                        pe.wait_ge(k_out, t)
                        pe.wait_ge(v_out, 2 * t)
                        transpose_x()
                    pe.wait_ge(f_T, t)
                    for g in range(FG):
                        for k in range(KD):
                            last = pe.matmul(bF[:, g * P:(g + 1) * P], w_in[:, k, E_F0 + g * FD:E_F0 + (g + 1) * FD],
                                             hT[:, s, k, :], start=(k == 0), stop=(k == KD - 1))
                    last.then_inc(in_f, 1)
                    pe.wait_ge(l_n, 2 * t + 2)
                    for k in range(2):
                        pe.transpose(bT[:, k * P:(k + 1) * P], ckv[:, k * P:(k + 1) * P], ident[:])
                    for k in range(2):
                        pe.transpose(bT[:, (2 + k) * P:(3 + k) * P], cq[:, k * P:(k + 1) * P], ident[:])
                    pe.transpose(bIn[:, 1, QL:512], cq[:, 2 * P:3 * P], ident[:]).then_inc(l_tr, 1)
                    pe.wait_ge(f_T, t + 1)
                    pe.wait_ge(g_out, t + 1)
                    for g in range(FG):
                        last = pe.matmul(bG[:, g // 2, (g % 2) * 256:(g % 2 + 1) * 256], fT[:, g, :],
                                         m_fn[:, g, :], start=True, stop=True)
                    last.then_inc(fx_mm, 1)
                    pe.wait_ge(l_T, 2 * t + 2)
                    pe.wait_ge(kpe_out, t + 1)
                    for j in range(2):
                        for k in range(3):
                            n = 512 if j == 0 else HEADS * QK - 512
                            last = pe.matmul(bIn[:, j, 0:n], cqT[:, k, :], w_uq[:, k, 512 * j:512 * j + n],
                                             start=(k == 0), stop=(k == 2))
                    last.then_inc(q_mm, 1)
                    if more:
                        pe.wait_ge(x_hT, t + 2)
                    for j in range(2):
                        for k in range(2):
                            last = pe.matmul(bX[:, j, :], ckvT[:, k, :], w_ukv[:, k, 512 * j:512 * (j + 1)],
                                             start=(k == 0), stop=(k == 1))
                    last.then_inc(kv_mm, 1)

                pe.wait_ge(x_n, 1)
                transpose_x()
                pe.wait_ge(w_loaded, 16)
                pe.wait_ge(prep, 2)
                pe.wait_ge(m_out, 1)
                with pe.Fori(0, NT // 2 - 1) as i:
                    tile(2 * i, 0, True)
                    tile(2 * i + 1, 1, True)
                tile(NT - 2, 0, True)
                pe.wait_ge(k_out, NT - 1)
                pe.wait_ge(v_out, 2 * NT - 2)
                tile(NT - 1, 1, False)

            @block.scalar
            def _(a):
                def x_squares(t, s, loaded):
                    a.wait_ge(x_loaded[s], loaded)
                    a.wait_ge(x_ms, t)
                    nc.scalar.activation(xsq[:], xt[:, s, :], ACT.Square, accum_out=xss[:]).then_inc(x_sq, 1)

                def modulated(t, s, stream):
                    a.wait_ge(x_tr, t + 1)
                    for k in range(KD):
                        last = nc.scalar.activation(hT[:, s, k, :], bX[:, k // 4, (k % 4) * P:(k % 4 + 1) * P], ACT.Identity,
                                                    scale=keep["scale"][:, 0, k, stream:stream + 1],
                                                    bias=keep["shift"][:, 0, k, stream:stream + 1])
                    last.then_inc(x_hT, 1)

                def tile(t, s, next_stream, loaded):
                    if loaded is not None:
                        x_squares(t + 1, 1 - s, loaded)
                    a.wait_ge(in_kvq, t + 1)
                    a.wait_ge(l_ms, t)
                    nc.scalar.activation(lsq[:, 0:KVL], bIn[:, 0, 0:KVL], ACT.Square, scale=KVL ** -0.5,
                                         accum_out=lss[:, 0:1]).then_inc(l_sq, 1)
                    nc.scalar.activation(lsq[:, KVL:], bIn[:, 1, 0:QL], ACT.Square, scale=QL ** -0.5,
                                         accum_out=lss[:, 1:2]).then_inc(l_sq, 1)
                    a.wait_ge(in_gate, t + 1)
                    a.wait_ge(g_st, 16 * t)
                    nc.scalar.activation(gt[:], bG[:].rearrange("p a b -> p (a b)"), ACT.Silu).then_inc(g_out, 1)
                    if loaded is not None:
                        modulated(t + 1, 1 - s, next_stream)
                    a.wait_ge(l_tr, t + 1)
                    nc.scalar.copy(ckvT[:].rearrange("p a b -> p (a b)"), bT[:, 0:256])
                    nc.scalar.copy(cqT[:, 0:2, :].rearrange("p a b -> p (a b)"), bT[:, 256:512]).then_inc(l_T, 1)
                    nc.scalar.copy(cqT[:, 2, :], bIn[:, 1, QL:512]).then_inc(l_T, 1)
                    a.wait_ge(fx_mm, t + 1)
                    a.wait_ge(fx_st, 16 * t)
                    for j in range(2):
                        nc.scalar.copy(fx[:, :, 2 * j:2 * j + 2, :].rearrange("p r g c -> p g r c"),
                                       bG[:, j, :].rearrange("p (g r c) -> p g r c", g=2, r=2)).then_inc(fx_out, 1)
                    a.wait_ge(k_out, t + 1)
                    a.wait_ge(v_st, 16 * t)
                    for j in range(2):
                        nc.scalar.copy(vt[:, 4 * j:4 * j + 4, :],
                                       bX[:, j, :].rearrange("p (h d) -> p h d", h=4)[:, :, NOPE:]).then_inc(v_out, 1)

                x_squares(0, 0, 16)
                modulated(0, 0, 1)
                tile(0, 0, 1, 16)
                tile(1, 1, 0, 32)
                with a.Fori(1, NT // 2 - 1) as i:
                    tile(2 * i, 0, 0, 16 * i + 16)
                    tile(2 * i + 1, 1, 0, 16 * i + 32)
                tile(NT - 2, 0, 0, 16 * (NT // 2))
                tile(NT - 1, 1, 0, None)

            @block.vector
            def _(v):
                v.wait_ge(c_loaded, 8 * 16)
                for k in range(2):
                    last = nc.vector.tensor_scalar(w_ukv[:, k, :], w_ukv[:, k, :], kvn[:, k:k + 1], None, ALU.mult)
                last.then_inc(prep, 1)
                for k in range(3):
                    last = nc.vector.tensor_scalar(w_uq[:, k, :], w_uq[:, k, :], qn[:, k:k + 1], None, ALU.mult)
                last.then_inc(prep, 1)
                v.wait_ge(m_mm, 1)
                nc.vector.tensor_copy(m_fn[:].rearrange("p g c -> p (g c)"), bG[:].rearrange("p a b -> p (a b)")).then_inc(m_out, 1)

                def x_norm(t, s):
                    v.wait_ge(x_sq, t + 1)
                    v.wait_ge(x_rs, t)
                    nc.vector.tensor_scalar(xms[:], xss[:], 1.0 / D, EPS, ALU.mult, ALU.add).then_inc(x_ms, 1)
                    v.wait_ge(x_rs, t + 1)
                    v.wait_ge(x_tr, t)
                    nc.vector.tensor_scalar(xn[:], xt[:, s, :], xr[:], None, ALU.mult).then_inc(x_n, 1)

                def heads(t, s, j, link):
                    h = qk[j]
                    link(nc.vector.tensor_tensor(hsq[:], h[:], h[:], ALU.mult))
                    link(nc.vector.tensor_reduce(hss[:], hsq[:], AX.X, ALU.add))
                    v.wait_ge(h_rs, 2 * t + j)
                    nc.vector.tensor_scalar(hms[:], hss[:], 1.0 / QK, EPS, ALU.mult, ALU.add).then_inc(h_ms, 1)
                    v.wait_ge(h_rs, 2 * t + j + 1)
                    link(nc.vector.tensor_tensor(h[:], h[:], hr[:, :, None].broadcast_to([P, HEADS, QK]), ALU.mult))
                    link(nc.vector.tensor_tensor(h[:], h[:], gk[:, j, None, :].broadcast_to([P, HEADS, QK]), ALU.mult))
                    tail = h[:, :, NOPE:]
                    nc.vector.tensor_tensor(rc[:], tail, rope[:, s, None, 0:ROPE].broadcast_to([P, HEADS, ROPE]), ALU.mult)
                    nf = ROPE // 4
                    for o in range(0, ROPE, nf):
                        other = o + nf if o // nf % 2 == 0 else o - nf
                        last = nc.vector.tensor_tensor(rs[:, :, o:o + nf], h[:, :, NOPE + other:NOPE + other + nf],
                                                       rope[:, s, None, ROPE + o:ROPE + o + nf].broadcast_to([P, HEADS, nf]), ALU.mult)
                    link(last)
                    nc.vector.tensor_tensor(tail, rc[:], rs[:], ALU.add).then_inc(h_done, 1)

                def tile(t, s, loaded, more):
                    link = Link(v, dchain, LINKS // 2 * t)
                    if more:
                        x_norm(t + 1, 1 - s)
                    v.wait_ge(l_sq, 2 * t + 2)
                    v.wait_ge(l_rs, t)
                    nc.vector.tensor_scalar(lms[:], lss[:], 1.0, EPS, ALU.mult, ALU.add).then_inc(l_ms, 1)
                    v.wait_ge(l_rs, t + 1)
                    v.wait_ge(l_tr, t)
                    nc.vector.tensor_scalar(ckv[:], bIn[:, 0, 0:KVL], lr[:, 0:1], None, ALU.mult).then_inc(l_n, 1)
                    nc.vector.tensor_scalar(cq[:], bIn[:, 1, 0:QL], lr[:, 1:2], None, ALU.mult).then_inc(l_n, 1)
                    nc.vector.tensor_copy(kpe[:], bIn[:, 0, KVL:E_Q0]).then_inc(kpe_out, 1)
                    v.wait_ge(in_f, t + 1)
                    v.wait_ge(fx_mm, t)
                    nc.vector.tensor_copy(fT[:].rearrange("p a b -> p (a b)"), bF[:]).then_inc(f_T, 1)
                    v.wait_ge(rope_loaded[s], loaded)
                    v.wait_ge(q_mm, t + 1)
                    v.wait_ge(h_st, 32 * t)
                    q = qk[0][:].rearrange("p h d -> p (h d)")
                    nc.vector.tensor_copy(q[:, 0:512], bIn[:, 0, :])
                    nc.vector.tensor_copy(q[:, 512:], bIn[:, 1, 0:HEADS * QK - 512]).then_inc(q_out, 1)
                    v.wait_ge(q_out, t + 1)
                    heads(t, s, 0, link)
                    v.wait_ge(kv_mm, t + 1)
                    for j in range(2):
                        last = nc.vector.tensor_copy(qk[1][:, 4 * j:4 * j + 4, 0:NOPE],
                                                     bX[:, j, :].rearrange("p (h d) -> p h d", h=4)[:, :, 0:NOPE])
                    last.then_inc(k_out, 1)
                    v.wait_ge(kpe_out, t + 1)
                    link(nc.vector.tensor_copy(qk[1][:, :, NOPE:], kpe[:, None, :].broadcast_to([P, HEADS, ROPE])))
                    heads(t, s, 1, link)
                    assert link.n == LINKS // 2, link.n

                x_norm(0, 0)
                with v.Fori(0, NT // 2 - 1) as i:
                    tile(2 * i, 0, 16 * i + 16, True)
                    tile(2 * i + 1, 1, 16 * i + 16, True)
                tile(NT - 2, 0, 16 * (NT // 2), True)
                tile(NT - 1, 1, 16 * (NT // 2), False)


def attend(nc, sem, keep, A, W):
    with ExitStack() as stack:
        core = Core(nc, stack, "at")
        SCALE = QK ** -0.5
        QB, NB = 4, 4
        NLT = NT - NC_CTX
        kraw = core.sb("kraw", [P, NT, QK])
        qraw = core.sb("qraw", [P, NT, QK])
        va = core.sb("va", [P, 2, NT, VH + 1])
        kT = core.sb("kT", [QK + 1, 2, T])
        qT = core.sb("qT", [QK + 1, 2, T])
        kTb = core.sb("kTb", [QK, 2, T], BF16)
        qTb = core.sb("qTb", [QK, 2, T], BF16)
        pT = core.sb("pT", [P, 3, 512])
        mx = core.sb("mx", [P, QB, 5])
        nm = core.sb("nm", [P, QB])
        oT = core.sb("oT", [VH + 1, 512])
        rec = core.sb("rec", [P, QB])
        o = core.sb("o", [P, QB, VH])
        bS = core.ps("bS", [P, 3, 512])
        bM = core.ps("bM", [P, 2, 512])
        bT = core.ps("bT", [P, 512])
        bO = core.ps("bO", [P, 512])
        bR = core.ps("bR", [P, 512])

        raw_l, v_l, set_up = [sem(f"at_{n}_loaded") for n in "kq"], [sem(f"at_v{i}_loaded") for i in range(2)], sem("at_setup")
        tr, tev, cast = sem("at_transposed"), sem("at_T_out"), sem("at_cast")
        max_mm, max_red, max_fin = sem("at_max_mm"), sem("at_max_reduced"), sem("at_max_final")
        row_mm, row_out = sem("at_row_mm"), sem("at_row_out")
        s_mm, exp_done, pv_mm = sem("at_scores"), sem("at_exp"), sem("at_pv")
        settled = [sem(f"at_settled{i}") for i in range(2)]
        oT_out, o_tr, rec_done, o_done, o_st = (sem("at_oT_out"), sem("at_o_transposed"), sem("at_reciprocal"),
                                                sem("at_o_done"), sem("at_o_stored"))

        BLOCKS = [(NC_CTX + QB * b, QB, NT) for b in range(NB)] + [(0, NC_CTX, NC_CTX)]
        NBLK = len(BLOCKS)
        STEPS = [nk for _, _, nk in BLOCKS]
        SH = sum(STEPS)
        GROUPS = [(j, min(4, NT - j)) for j in range(0, NT, 4)]
        NGR = 2 * len(GROUPS)

        def items(b):
            _, nq, nk = BLOCKS[b]
            return [(j, c // 512, c, min(512, nk * P - c)) for j in range(nq) for c in range(0, nk * P, 512)]

        FIRST_ITEM = [sum(len(items(x)) for x in range(b)) for b in range(NBLK + 1)]
        IH = FIRST_ITEM[-1]
        assert IH % 2 == 0
        FIRST_STEP = [sum(STEPS[:b]) for b in range(NBLK)]

        def side(b, s, h, has_next):
            if b < 3:
                return [(h, s, b + 1)]
            if b == 3:
                return [(h, s, 4)] + ([(h + 1, 1 - s, 0)] if has_next else [])
            return []

        def beside(b, s, h, has_next):
            jobs = []
            for hh, ss, bb in side(b, s, h, has_next):
                jobs += [("max", hh, ss, bb, i) for i in range(len(items(bb)))] + [("row", hh, ss, bb, b)]
            rows, jobs = jobs[-1:], jobs[:-1]
            if b == 2 and has_next:
                turns = [("turn", h + 1, 1 - s, n, None) for n in range(NGR)]
                every = -(-len(jobs) // NGR)
                jobs = [x for n in range(NGR) for x in jobs[every * n:every * (n + 1)] + [turns[n]]]
            nk = STEPS[b]
            return [jobs[len(jobs) * k // (nk - 1):len(jobs) * (k + 1) // (nk - 1)] for k in range(nk - 1)] + [rows]

        def heads(fori, one):
            with fori(0, HEADS // 2 - 1) as i:
                one(2 * i, 0, True)
                one(2 * i + 1, 1, True)
            one(HEADS - 2, 0, True)
            one(HEADS - 1, 1, False)

        with nc.Block() as block:
            @block.sync
            def _(sp):
                def load(dst, name, h, done):
                    head = slice(h, h + 1) if isinstance(h, int) else bass.ds(h, 1)
                    sp.dma_start(dst[:, 0:NC_CTX, :], W[name][head, 0:CTX].rearrange("a (p j) d -> p (a j) d", p=P)).then_inc(done, 16)
                    sp.dma_start(dst[:, NC_CTX:NT, :], W[name][head, CTX:T].rearrange("a (p j) d -> p (a j) d", p=P)).then_inc(done, 16)

                def store(h, b, s):
                    q0, nq, _ = BLOCKS[b]
                    sp.wait_ge(o_done, h * NBLK + b + 1)
                    settle(sp, settled[0])
                    col = slice(h * VH, (h + 1) * VH) if isinstance(h, int) else bass.ds(h * VH, VH)
                    if b < NB:
                        dst = W["mix"][CTX:T, col].rearrange("(p j) d -> p j d", p=P)[:, q0 - NC_CTX:q0 - NC_CTX + nq, :]
                    else:
                        dst = W["mix"][0:CTX, col].rearrange("(p j) d -> p j d", p=P)
                    sp.dma_start(dst, o[:, 0:nq, :]).then_inc(o_st, 16)

                def head(h, s, has_next):
                    if has_next:
                        sp.wait_ge(tr, (h + 1) * NGR)
                        load(kraw, "k", h + 1, raw_l[0])
                        load(qraw, "q", h + 1, raw_l[1])
                        sp.wait_ge(pv_mm, h * SH)
                        load(va[:, 1 - s, :, 0:VH], "v", h + 1, v_l[1 - s])
                    for b in range(NBLK):
                        store(h, b, s)

                load(kraw, "k", 0, raw_l[0])
                load(qraw, "q", 0, raw_l[1])
                sp.wait_ge(set_up, 2)
                load(va[:, 0, :, 0:VH], "v", 0, v_l[0])
                heads(sp.Fori, head)
                sp.wait_ge(o_st, 16 * NBLK * HEADS)

            @block.gpsimd
            def _(g):
                nc.gpsimd.memset(va[:, :, :, VH:VH + 1], 1.0).then_inc(set_up, 1)

                def prepare(h, s):
                    for n in range(NGR):
                        j, w = GROUPS[n % len(GROUPS)]
                        src, dst = (kT, kTb) if n < len(GROUPS) else (qT, qTb)
                        g.wait_ge(tev, h * NGR + n + 1)
                        settle(g, settled[1])
                        nc.gpsimd.tensor_copy(dst[:, s, j * P:(j + w) * P], src[0:QK, s, j * P:(j + w) * P]).then_inc(cast, 1)

                prepare(0, 0)
                def head(h, s, has_next):
                    if has_next:
                        g.wait_ge(max_red, h * IH + FIRST_ITEM[1])
                        prepare(h + 1, 1 - s)

                heads(g.Fori, head)

            @block.tensor
            def _(pe):
                ident = keep["ident"]

                def transpose_group(h, s, n):
                    j, w = GROUPS[n % len(GROUPS)]
                    raw, first = (kraw, n == 0) if n < len(GROUPS) else (qraw, n == len(GROUPS))
                    if first:
                        pe.wait_ge(raw_l[0 if raw is kraw else 1], 32 * (h + 1))
                    pe.wait_ge(tev, h * NGR + n)
                    for x in range(w):
                        last = pe.transpose(bT[0:QK, x * P:(x + 1) * P], raw[:, j + x, :], ident[:])
                    last.then_inc(tr, 1)

                def max_item(h, s, b, i):
                    j, _, c, n = items(b)[i]
                    q0 = BLOCKS[b][0]
                    count = h * IH + FIRST_ITEM[b] + i
                    if b == 0 and i == 0:
                        pe.wait_ge(cast, (h + 1) * NGR)
                    if not (isinstance(count, int) and count < 2):
                        pe.wait_ge(max_red, count - 1)
                    pe.matmul(bM[:, (FIRST_ITEM[b] + i) % 2, 0:n], qTb[:, s, (q0 + j) * P:(q0 + j + 1) * P],
                              kTb[:, s, c:c + n], start=True, stop=True).then_inc(max_mm, 1)

                def row(h, s, b, outputs_done):
                    pe.wait_ge(o_done, outputs_done)
                    pe.wait_ge(row_out, h * NBLK + b)
                    pe.wait_ge(max_fin, h * NBLK + b + 1)
                    for j in range(BLOCKS[b][1]):
                        last = pe.matmul(bR[0:1, j * P:(j + 1) * P], nm[:, j:j + 1], ident[:], start=True, stop=True)
                    last.then_inc(row_mm, 1)

                def o_transposes(h, b, rows_done):
                    pe.wait_ge(oT_out, h * NBLK + b + 1)
                    pe.wait_ge(row_out, rows_done)
                    for j in range(BLOCKS[b][1]):
                        last = pe.transpose(bR[:, j * P:j * P + VH + 1], oT[:, j * P:(j + 1) * P], ident[0:VH + 1, 0:VH + 1])
                    last.then_inc(o_tr, 1)

                def scores(h, s, b, k):
                    q0, nq, nk = BLOCKS[b]
                    g = FIRST_STEP[b] + k
                    if k == 0:
                        pe.wait_ge(row_out, h * NBLK + b + 1)
                    pe.wait_ge(exp_done, h * SH + max(0, g - 2))
                    pe.matmul(bS[:, g % 3, 0:nq * P], kT[:, s, k * P:(k + 1) * P], qT[:, s, q0 * P:(q0 + nq) * P],
                              start=True, stop=True).then_inc(s_mm, 1)

                def pv(h, s, b, k):
                    _, nq, nk = BLOCKS[b]
                    g = FIRST_STEP[b] + k
                    if k == 0:
                        pe.wait_ge(oT_out, h * NBLK + b)
                        if b == 0:
                            pe.wait_ge(v_l[s], (h - s) * 16 + 32)
                    pe.wait_ge(exp_done, h * SH + g + 1)
                    pe.matmul(bO[0:VH + 1, 0:nq * P], va[:, s, k, :], pT[:, g % 3, 0:nq * P],
                              start=(k == 0), stop=(k == nk - 1)).then_inc(pv_mm, 1)

                def head(h, s, has_next):
                    for b in range(NBLK):
                        jobs = beside(b, s, h, has_next)
                        nk = STEPS[b]
                        for k in range(min(2, nk)):
                            scores(h, s, b, k)
                        if b > 0:
                            rows = h * NBLK + b + 1 if b < 4 or not has_next else (h + 1) * NBLK + 1
                            o_transposes(h, b - 1, rows)
                        for k in range(nk):
                            if k + 2 < nk:
                                scores(h, s, b, k + 2)
                            for kind, hh, ss, n, i in jobs[k]:
                                if kind == "max":
                                    max_item(hh, ss, n, i)
                                elif kind == "row":
                                    row(hh, ss, n, h * NBLK + b)
                                else:
                                    transpose_group(hh, ss, n)
                            pv(h, s, b, k)
                    o_transposes(h, NBLK - 1, (h + 1) * NBLK)

                pe.wait_ge(set_up, 2)
                for n in range(NGR):
                    transpose_group(0, 0, n)
                for i in range(len(items(0))):
                    max_item(0, 0, 0, i)
                row(0, 0, 0, 0)
                heads(pe.Fori, head)

            @block.scalar
            def _(a):
                def evict(h, s, n):
                    j, w = GROUPS[n % len(GROUPS)]
                    dst = kT if n < len(GROUPS) else qT
                    a.wait_ge(tr, h * NGR + n + 1)
                    nc.scalar.copy(dst[0:QK, s, j * P:(j + w) * P], bT[0:QK, 0:w * P]).then_inc(tev, 1)

                def head(h, s, has_next):
                    for b in range(NBLK):
                        q0, nq, nk = BLOCKS[b]
                        jobs = beside(b, s, h, has_next)
                        for k in range(nk):
                            g = FIRST_STEP[b] + k
                            a.wait_ge(s_mm, h * SH + g + 1)
                            a.wait_ge(pv_mm, h * SH + max(0, g - 2))
                            nc.scalar.activation(pT[:, g % 3, 0:nq * P], bS[:, g % 3, 0:nq * P], ACT.Exp,
                                                 scale=SCALE).then_inc(exp_done, 1)
                            for kind, hh, ss, n, i in jobs[k]:
                                if kind == "turn":
                                    evict(hh, ss, n)

                for n in range(NGR):
                    evict(0, 0, n)
                heads(a.Fori, head)

            @block.vector
            def _(v):
                def maxima(h, s, b):
                    for i, (j, piece, c, n) in enumerate(items(b)):
                        count = h * IH + FIRST_ITEM[b] + i
                        v.wait_ge(max_mm, count + 1)
                        if i == 0:
                            v.wait_ge(max_fin, h * NBLK + b)
                        nc.vector.tensor_reduce(mx[:, j, piece:piece + 1], bM[:, (FIRST_ITEM[b] + i) % 2, 0:n], AX.X, ALU.max).then_inc(max_red, 1)
                    pieces = -(-STEPS[b] * P // 512)
                    nq = BLOCKS[b][1]
                    v.wait_ge(max_red, h * IH + FIRST_ITEM[b + 1])
                    v.wait_ge(row_mm, h * NBLK + b)
                    nc.vector.tensor_reduce(nm[:, 0:nq], mx[:, 0:nq, 0:pieces], AX.X, ALU.max, negate=True).then_inc(max_fin, 1)

                def row(h, s, b):
                    q0, nq, _ = BLOCKS[b]
                    v.wait_ge(row_mm, h * NBLK + b + 1)
                    nc.vector.tensor_copy(qT[QK:QK + 1, s, q0 * P:(q0 + nq) * P], bR[0:1, 0:nq * P]).then_inc(row_out, 1)

                def finish_a(h, b):
                    nq = BLOCKS[b][1]
                    v.wait_ge(pv_mm, h * SH + FIRST_STEP[b] + STEPS[b])
                    nc.vector.tensor_copy(oT[:, 0:nq * P], bO[0:VH + 1, 0:nq * P]).then_inc(oT_out, 1)

                def finish_b(h, b):
                    nq = BLOCKS[b][1]
                    v.wait_ge(o_tr, h * NBLK + b + 1)
                    back = bR[:].rearrange("p (j c) -> p j c", c=P)
                    nc.vector.reciprocal(rec[:, 0:nq], back[:, 0:nq, VH]).then_inc(rec_done, 1)
                    v.wait_ge(rec_done, h * NBLK + b + 1)
                    v.wait_ge(o_st, 16 * (h * NBLK + b))
                    nc.vector.tensor_tensor(o[:, 0:nq, :], back[:, 0:nq, 0:VH], rec[:, 0:nq, None].broadcast_to([P, nq, VH]),
                                            ALU.mult).then_inc(o_done, 1)

                def head(h, s, has_next):
                    for b in range(NBLK):
                        if b > 0:
                            finish_b(h, b - 1)
                        for hh, ss, bb in side(b, s, h, has_next):
                            maxima(hh, ss, bb)
                            row(hh, ss, bb)
                        finish_a(h, b)
                    finish_b(h, NBLK - 1)

                nc.vector.memset(kT[QK:QK + 1, :, :], 1.0).then_inc(set_up, 1)
                maxima(0, 0, 0)
                row(0, 0, 0)
                heads(v.Fori, head)


def fourier(nc, sem, keep, A, W):
    with ExitStack() as stack:
        core = Core(nc, stack, "ft")
        K1H = P // (P // N2)
        CH = 4
        step1 = core.sb("step1", [P, N2, 3, P])
        step2 = core.sb("step2", [P, 2, P])
        cdft = core.sb("cdft", [P, NC_CTX, 2, CTX])
        ab = core.sb("ab", [P, N2, 2 * FW])
        cab = core.sb("cab", [P, NC_CTX, 2 * FW])
        z = core.sb("z", [P, 4, 2, FW])
        zin = core.sb("zin", [P, 2, 2, K1H, FW // 2])
        fo = core.sb("fo", [P, 4, FW])
        bZ = core.ps("bZ", [P, 4, FW])
        bF = core.ps("bF", [P, 4, FW])
        tab, ctx_l = sem("ft_tables_loaded"), sem("ft_ctx_loaded")
        ab_l = [sem(f"ft_ab_loaded{i}") for i in range(N2 // CH)]
        mm1, re_out, im_out = sem("ft_step1"), sem("ft_re_out"), sem("ft_im_out")
        z_st = [sem(f"ft_z_stored{i}") for i in range(4)]
        z_l = [sem(f"ft_z_loaded{i}") for i in range(2)]
        mm2, f_out = sem("ft_step2"), sem("ft_f_out")
        f_st = [sem(f"ft_f_stored{i}") for i in range(4)]
        NCTX_OUT = CTX // P

        with nc.Block() as block:
            @block.sync
            def _(sp):
                src = W["fx"][CTX:T].rearrange("(p n) c -> p n c", n=N2)
                sp.dma_start(step1[:, 0:CH], A["step1"][:, 0:CH]).then_inc(tab, 16)
                sp.dma_start(ab[:, 0:CH], src[:, 0:CH]).then_inc(ab_l[0], 16)
                sp.dma_start(step1[:, CH:N2], A["step1"][:, CH:N2]).then_inc(tab, 16)
                for i in range(1, N2 // CH):
                    sp.dma_start(ab[:, CH * i:CH * (i + 1)], src[:, CH * i:CH * (i + 1)]).then_inc(ab_l[i], 16)
                sp.dma_start(step2[:], A["step2"]).then_inc(ctx_l, 16)
                sp.dma_start(cdft[:], A["ctxdft"]).then_inc(ctx_l, 16)
                sp.dma_start(cab[:], W["fx"][0:CTX].rearrange("(k p) c -> p k c", p=P)).then_inc(ctx_l, 16)
                for n in range(N2):
                    sp.wait_ge(re_out, n + 1)
                    sp.wait_ge(im_out, n + 1)
                    sp.dma_start(W["z"][:, n].rearrange("r p c -> p r c"), z[:, n % 4]).then_inc(z_st[n % 4], 16)
                for i in range(4):
                    sp.wait_ge(z_st[i], 16 * N2 // 4)
                for hc in range(2):
                    for r in range(2):
                        sp.dma_start(zin[:, hc, r], W["z"][r].rearrange("n (lo hi) c -> (n lo) hi c", hi=K1H)
                                     [:, :, hc * FW // 2:(hc + 1) * FW // 2]).then_inc(z_l[hc], 16)

                dst = W["mix"][CTX:T, HEADS * VH:GW].rearrange("(p hi) c -> p hi c", hi=K1H)
                for i in range(NCTX_OUT):
                    sp.wait_ge(f_out, i + 1)
                    sp.dma_start(W["mix"][i * P:(i + 1) * P, HEADS * VH:GW], fo[:, i]).then_inc(f_st[i], 16)
                for n in range(K1H):
                    hc, pair = divmod(n, K1H // 2)
                    sp.wait_ge(f_out, NCTX_OUT + n + 1)
                    sp.dma_start(dst[:, 2 * pair:2 * pair + 2, hc * FW // 2:(hc + 1) * FW // 2],
                                fo[:, (NCTX_OUT + n) % 4].rearrange("p (a c) -> p a c", a=2)).then_inc(f_st[(NCTX_OUT + n) % 4], 16)
                for i in range(4):
                    sp.wait_ge(f_st[i], 16 * len(range(i, NCTX_OUT + K1H, 4)))

            @block.tensor
            def _(pe):
                pe.wait_ge(tab, 16)
                for n in range(N2):
                    if n == CH:
                        pe.wait_ge(tab, 32)
                    if n % CH == 0:
                        pe.wait_ge(ab_l[n // CH], 16)
                    if n >= 2:
                        pe.wait_ge(re_out, n - 1)
                        pe.wait_ge(im_out, n - 1)
                    b = 2 * (n % 2)
                    cos, sin, neg_sin = (step1[:, n, x, :] for x in range(3))
                    pe.matmul(bZ[:, b, :], cos, ab[:, n, 0:FW], start=True, stop=False)
                    pe.matmul(bZ[:, b, :], neg_sin, ab[:, n, FW:], start=False, stop=True)
                    pe.matmul(bZ[:, b + 1, :], sin, ab[:, n, 0:FW], start=True, stop=False)
                    pe.matmul(bZ[:, b + 1, :], cos, ab[:, n, FW:], start=False, stop=True).then_inc(mm1, 1)
                pe.wait_ge(ctx_l, 48)
                for i in range(NCTX_OUT):
                    for x in range(2 * NC_CTX):
                        kt, part = divmod(x, 2)
                        last = pe.matmul(bF[:, i, :], cdft[:, kt, part, i * P:(i + 1) * P], cab[:, kt, part * FW:(part + 1) * FW],
                                         start=(x == 0), stop=(x == 2 * NC_CTX - 1))
                    last.then_inc(mm2, 1)
                for hc in range(2):
                    pe.wait_ge(z_l[hc], 32)
                    for hi in range(0, K1H, 2):
                        n = NCTX_OUT + (hc * K1H + hi) // 2
                        if n >= 4:
                            pe.wait_ge(f_out, n - 3)
                        for r in range(2):
                            last = pe.matmul(bF[:, n % 4, :], step2[:, r, :], zin[:, hc, r, hi:hi + 2, :].rearrange("p a c -> p (a c)"),
                                             start=(r == 0), stop=(r == 1))
                        last.then_inc(mm2, 1)

            @block.scalar
            def _(a):
                for n in range(N2):
                    a.wait_ge(mm1, n + 1)
                    if n >= 4:
                        a.wait_ge(z_st[n % 4], 16 * (n // 4))
                    nc.scalar.copy(z[:, n % 4, 0, :], bZ[:, 2 * (n % 2), :]).then_inc(re_out, 1)

            @block.vector
            def _(v):
                for n in range(N2):
                    v.wait_ge(mm1, n + 1)
                    if n >= 4:
                        v.wait_ge(z_st[n % 4], 16 * (n // 4))
                    nc.vector.tensor_copy(z[:, n % 4, 1, :], bZ[:, 2 * (n % 2) + 1, :]).then_inc(im_out, 1)
                for n in range(NCTX_OUT + K1H):
                    v.wait_ge(mm2, n + 1)
                    if n >= 4:
                        v.wait_ge(f_st[n % 4], 16 * (n // 4))
                    nc.vector.tensor_copy(fo[:, n % 4, :], bF[:, n % 4, :]).then_inc(f_out, 1)


def merge0(nc, sem, keep, A, W):
    with ExitStack() as stack:
        core = Core(nc, stack, "m0")
        w = core.sb("w", [P, KD, D])
        mix, gate, xt = (core.sb(n, [P, 2, D]) for n in ("mix", "gate", "xt"))
        m = core.sb("m", [P, D])
        mT = core.sb("mT", [P, 2, KD, P])
        gy = core.sb("gy", [P, D])
        x1 = core.sb("x1", [P, 2, D])
        xsq, xss, xms, xr, xn = (core.sb(n, [P, c]) for n, c in (("xsq", D), ("xss", 1), ("xms", 1), ("xr", 1), ("xn", D)))
        half = core.sb("half", [P, 1])
        bM = core.ps("bM", [P, 2, 512])
        bY = core.ps("bY", [P, 2, 512])
        bX = core.ps("bX", [P, 2, 512])
        w_l = [sem(f"m0_w{j}_loaded") for j in range(2)]
        in_l, x_l = [sem(f"m0_mix_loaded{i}") for i in range(2)], [sem(f"m0_x_loaded{i}") for i in range(2)]
        m_done, m_tr, m_T, y_mm, gy_done = sem("m0_gated"), sem("m0_m_tr"), sem("m0_mT"), sem("m0_y_mm"), sem("m0_gy")
        x1_done, x1_st = sem("m0_x1"), [sem(f"m0_x1_stored{i}") for i in range(2)]
        x_sq, x_ms, x_rs, x_n, x_tr, x_hT = (sem(f"m0_{n}") for n in ("x_sq", "x_ms", "x_rs", "x_n", "x_tr", "hT"))
        pchain = sem("m0_pool_setup")
        hT = keep["hT"]

        def tiles(fori, one):
            one(0, 0, True, True)
            one(1, 1, True, False)
            with fori(1, NT // 2) as i:
                one(2 * i, 0, False, False)
                one(2 * i + 1, 1, False, False)

        def rows(t):
            return slice(t * P, (t + 1) * P) if isinstance(t, int) else bass.ds(t * P, P)

        with nc.Block() as block:
            @block.sync
            def _(sp):
                def load(t, s):
                    sp.dma_start(mix[:, s, :], W["mix"][rows(t), :]).then_inc(in_l[s], 16)
                    sp.dma_start(gate[:, s, :], W["gate"][rows(t), :]).then_inc(in_l[s], 16)

                def load_x(s, src, at):
                    sp.dma_start(xt[:, s, :], src[0, rows(at), :]).then_inc(x_l[s], 16)

                def store(t, s):
                    sp.wait_ge(x1_done, t + 1)
                    sp.dma_start(W["x1"][rows(t), :], x1[:, s, :]).then_inc(x1_st[s], 16)

                load(0, 0)
                for j in range(2):
                    cols = slice(j * 512, (j + 1) * 512)
                    sp.dma_start(w[:, :, cols], A["e_w_out"][0, :, cols].rearrange("(k p) n -> p k n", p=P)).then_inc(w_l[j], 16)
                load(1, 1)
                load_x(0, A["ctx"], 0)
                load_x(1, A["ctx"], 1)
                sp.wait_ge(m_done, 1)
                load(2, 0)

                def tile(t, s, more):
                    store(t - 2, s)
                    load_x(s, A["x"], t - 2)
                    if more:
                        sp.wait_ge(m_done, t)
                        load(t + 1, 1 - s)

                with sp.Fori(1, NT // 2 - 1) as i:
                    tile(2 * i, 0, True)
                    tile(2 * i + 1, 1, True)
                tile(NT - 2, 0, True)
                tile(NT - 1, 1, False)
                store(NT - 2, 0)
                store(NT - 1, 1)
                for s in range(2):
                    sp.wait_ge(x1_st[s], 16 * NT // 2)

            @block.gpsimd
            def _(g):
                nc.gpsimd.memset(half[:], -0.5).then_inc(pchain, 1)
                g.wait_ge(pchain, 1)
                with g.Fori(0, NT) as t:
                    g.wait_ge(x_ms, t + 1)
                    g.wait_ge(x_n, t)
                    nc.gpsimd.tensor_tensor(xr[:], xms[:], half[:], ALU.pow).then_inc(x_rs, 1)

            @block.tensor
            def _(pe):
                ident = keep["ident"]

                def turn(dst, src, done):
                    for k in range(KD):
                        last = pe.transpose(dst[:, k // 4, (k % 4) * P:(k % 4 + 1) * P], src[:, k * P:(k + 1) * P], ident[:])
                    last.then_inc(done, 1)

                def turn_m(t):
                    pe.wait_ge(m_done, t + 1)
                    pe.wait_ge(m_T, 2 * t)
                    turn(bM, m, m_tr)

                def turn_x(t):
                    pe.wait_ge(x_n, t + 1)
                    pe.wait_ge(x_hT, t)
                    turn(bX, xn, x_tr)

                def project(t, s):
                    pe.wait_ge(m_T, 2 * t + 2)
                    for j in range(2):
                        if isinstance(t, int) and t == 0:
                            pe.wait_ge(w_l[j], 16)
                        pe.wait_ge(gy_done, 2 * t - 1 + j if not isinstance(t, int) or t else 0)
                        for k in range(KD):
                            last = pe.matmul(bY[:, j, :], mT[:, s, k, :], w[:, k, j * 512:(j + 1) * 512],
                                             start=(k == 0), stop=(k == KD - 1))
                        last.then_inc(y_mm, 1)

                turn_m(0)
                turn_m(1)
                project(0, 0)
                with pe.Fori(1, NT // 2) as i:
                    turn_m(2 * i)
                    project(2 * i - 1, 1)
                    turn_x(2 * i - 2)
                    turn_m(2 * i + 1)
                    project(2 * i, 0)
                    turn_x(2 * i - 1)
                project(NT - 1, 1)
                turn_x(NT - 2)
                turn_x(NT - 1)

            @block.scalar
            def _(a):
                def evict_m(t, s):
                    a.wait_ge(m_tr, t + 1)
                    for j in range(2):
                        nc.scalar.copy(mT[:, s, 4 * j:4 * j + 4, :].rearrange("p k c -> p (k c)"), bM[:, j, :]).then_inc(m_T, 1)

                def squares(t, s):
                    a.wait_ge(x1_done, t + 1)
                    a.wait_ge(x_ms, t)
                    nc.scalar.activation(xsq[:], x1[:, s, :], ACT.Square, accum_out=xss[:]).then_inc(x_sq, 1)

                def modulated(t, stream):
                    a.wait_ge(x_tr, t + 1)
                    for k in range(KD):
                        last = nc.scalar.activation(hT[:, k, rows(t)], bX[:, k // 4, (k % 4) * P:(k % 4 + 1) * P],
                                                    ACT.Identity, scale=keep["scale"][:, 1, k, stream:stream + 1],
                                                    bias=keep["shift"][:, 1, k, stream:stream + 1])
                    last.then_inc(x_hT, 1)

                evict_m(0, 0)
                evict_m(1, 1)
                squares(0, 0)
                evict_m(2, 0)
                squares(1, 1)
                modulated(0, 1)
                evict_m(3, 1)
                squares(2, 0)
                modulated(1, 1)
                with a.Fori(2, NT // 2) as i:
                    evict_m(2 * i, 0)
                    squares(2 * i - 1, 1)
                    modulated(2 * i - 2, 0)
                    evict_m(2 * i + 1, 1)
                    squares(2 * i, 0)
                    modulated(2 * i - 1, 0)
                squares(NT - 1, 1)
                modulated(NT - 2, 0)
                modulated(NT - 1, 0)

            @block.vector
            def _(v):
                def gated(t, s, loaded):
                    v.wait_ge(in_l[s], loaded)
                    v.wait_ge(m_tr, t)
                    nc.vector.tensor_tensor(m[:], mix[:, s, :], gate[:, s, :], ALU.mult).then_inc(m_done, 1)

                def residual(t, s, stream):
                    for j in range(2):
                        v.wait_ge(y_mm, 2 * t + j + 1)
                        nc.vector.tensor_tensor(gy[:, j * 512:(j + 1) * 512], bY[:, j, :],
                                                keep["gate"][:, stream, j * 512:(j + 1) * 512], ALU.mult).then_inc(gy_done, 1)
                    v.wait_ge(gy_done, 2 * t + 2)
                    v.wait_ge(x_l[s], (t - s) * 8 + 16)
                    v.wait_ge(x1_st[s], (t - s) * 8)
                    nc.vector.tensor_tensor(x1[:, s, :], gy[:], xt[:, s, :], ALU.add).then_inc(x1_done, 1)

                def norm(t, s):
                    v.wait_ge(x_sq, t + 1)
                    nc.vector.tensor_scalar(xms[:], xss[:], 1.0 / D, EPS, ALU.mult, ALU.add).then_inc(x_ms, 1)
                    v.wait_ge(x_rs, t + 1)
                    v.wait_ge(x_tr, t)
                    nc.vector.tensor_scalar(xn[:], x1[:, s, :], xr[:], None, ALU.mult).then_inc(x_n, 1)

                gated(0, 0, 32)
                gated(1, 1, 32)
                gated(2, 0, 64)
                residual(0, 0, 1)
                norm(0, 0)
                gated(3, 1, 64)
                residual(1, 1, 1)
                norm(1, 1)
                with v.Fori(1, NT // 2 - 1) as i:
                    gated(2 * i + 2, 0, 32 * i + 64)
                    residual(2 * i, 0, 0)
                    norm(2 * i, 0)
                    gated(2 * i + 3, 1, 32 * i + 64)
                    residual(2 * i + 1, 1, 0)
                    norm(2 * i + 1, 1)
                residual(NT - 2, 0, 0)
                norm(NT - 2, 0)
                residual(NT - 1, 1, 0)
                norm(NT - 1, 1)


def project1(nc, sem, keep, A, W):
    with ExitStack() as stack:
        core = Core(nc, stack, "p1")
        TZ = T + 2
        L0 = CTX + 2
        slab = core.sb("slab", [P, 4, KD, P])
        u = core.sb("u", [P, 2, T + 4])
        z = core.sb("z", [P, 2, TZ])
        kq = core.sb("kq", [P, TZ])
        rn = core.sb("rn", [P, TZ])
        kk = core.sb("kk", [P, TZ])
        gs = core.sb("gs", [P, SEQ])
        shift = core.sb("shift", [P, SHIFT_ROWS, O_G0 // P])
        k_k = core.sb("k_k", [P, PAIRS])
        same = core.sb("same", [P, P])
        bU = core.ps("bU", [P, 4, 512])
        bS = core.ps("bS", [P, 4, 512])
        BLK = [(0, 1, CTX)] + [(CTX + 512 * j, CTX + 3 + 512 * j, 512) for j in range(SEQ // 512)]
        SBLK = [(c, min(512, TZ - c)) for c in range(0, TZ, 512)]
        NB, NS = len(BLK), len(SBLK)
        PRE = 2 * NB
        PB = 4 * NB - 1
        c_l, s_l = sem("p1_consts_loaded"), [sem(f"p1_slab{i}_loaded") for i in range(4)]
        set_up, mm, ev = sem("p1_setup"), sem("p1_block_mm"), sem("p1_block_out")
        u_used, z1, z_done = sem("p1_u_used"), sem("p1_z_middle"), sem("p1_z_done")
        z_st = [sem(f"p1_z{i}_stored") for i in range(2)]
        t_done = sem("p1_tanh_done")
        kq_done, ss_mm, root, kk_done, kk_st, gs_st = (sem(f"p1_{n}") for n in (
            "k_squared", "ss_mm", "root", "kk_done", "kk_stored", "gate_stored"))
        dchain = sem("p1_dve_chain")
        hT = keep["hT"]
        STARTS = [0, D, O_R0, O_G0]
        ROWS = {0: 0, 1: 3, 2: 2}

        def zslot(i):
            return i % 2

        with nc.Block() as block:
            @block.sync
            def _(sp):
                def load(i, at):
                    sp.dma_start(slab[:, i], A["o_w_in"][0, :, at].rearrange("(k p) n -> p k n", p=P)).then_inc(s_l[i], 16)

                def store(dst, src, done):
                    sp.dma_start(dst[:, 0:CTX], src[:, 0:CTX]).then_inc(done, 16)
                    sp.dma_start(dst[:, CTX:T], src[:, L0:TZ]).then_inc(done, 16)

                load(0, slice(O_WD0, O_WD0 + P))
                load(1, slice(O_AD0, O_AD0 + P))
                with nc.allow_non_contiguous_dma("short vectors as columns"):
                    for r in range(SHIFT_ROWS):
                        sp.dma_start(shift[:, r, :], A["o_shift_w"][0, r].rearrange("(k p) -> p k", p=P)).then_inc(c_l, 16)
                    sp.dma_start(k_k[:], A["o_k_k"][0].rearrange("(k p) -> p k", p=P)).then_inc(c_l, 16)
                sp.dma_start(same[:], A["same"]).then_inc(c_l, 16)
                load(2, slice(O_R0, O_R0 + P))
                load(3, slice(O_G0, O_G0 + P))
                for i in range(2):
                    sp.wait_ge(mm, NB * (i + 1))
                    load(i, slice(STARTS[i], STARTS[i] + P))
                sp.wait_ge(t_done, 1)
                store(W["lora"][0], z[:, 0], z_st[0])
                sp.wait_ge(z_done, 2)
                store(W["lora"][1], z[:, 1], z_st[1])

                def pair(p, more):
                    row = slice(p, p + 1) if isinstance(p, int) else bass.ds(p, 1)
                    heads = W["heads"][row].rearrange("a c f t -> (a c) f t")
                    for i in range(3):
                        s = i % 2
                        sp.wait_ge(z_done, 2 + 3 * p + i + 1)
                        store(heads[:, ROWS[i], :], z[:, zslot(i)], z_st[zslot(i)])
                        if more:
                            sp.wait_ge(mm, PRE + PB * p + NB * (i + 1))
                            at = bass.ds((p + 1) * P + STARTS[i], P) if not isinstance(p, int) else slice((p + 1) * P + STARTS[i], (p + 2) * P + STARTS[i])
                            load(i, at)
                        if i == 1:
                            sp.wait_ge(kk_done, p + 1)
                            store(heads[:, 1, :], kk, kk_st)
                    sp.wait_ge(ev, PRE + PB * (p + 1))
                    if more:
                        load(3, bass.ds((p + 1) * P + STARTS[3], P) if not isinstance(p, int) else slice((p + 1) * P + STARTS[3], (p + 2) * P + STARTS[3]))
                    sp.dma_start(W["gsT"][row].rearrange("a c t -> (a c) t"), gs[:]).then_inc(gs_st, 16)

                with sp.Fori(0, PAIRS - 1) as p:
                    pair(p, True)
                pair(PAIRS - 1, False)
                sp.wait_ge(z_st[0], 32 * (1 + 2 * PAIRS))
                sp.wait_ge(z_st[1], 32 * (1 + PAIRS))
                sp.wait_ge(kk_st, 32 * PAIRS)
                sp.wait_ge(gs_st, 16 * PAIRS)

            @block.tensor
            def _(pe):
                def blocks(i, base, n0, first):
                    for b in range(first, NB):
                        tok, _, w = BLK[b]
                        n = n0 + b - first
                        pe.wait_ge(ev, base + max(0, n - 3))
                        for k in range(KD):
                            last = pe.matmul(bU[:, n % 4, 0:w], slab[:, i, k, :], hT[:, k, tok:tok + w],
                                             start=(k == 0), stop=(k == KD - 1))
                        last.then_inc(mm, 1)

                for i in range(2):
                    pe.wait_ge(s_l[i], 16)
                    blocks(i, 0, i * NB, 0)
                with pe.Fori(0, PAIRS) as p:
                    base = PRE + PB * p
                    for i in range(4):
                        pe.wait_ge(s_l[i], 16 * p + (32 if i < 2 else 16))
                        blocks(i, base, NB * i, 1 if i == 3 else 0)
                        if i == 1:
                            pe.wait_ge(c_l, 16 * 5)
                            pe.wait_ge(kq_done, p + 1)
                            for x, (c, w) in enumerate(SBLK):
                                pe.wait_ge(root, NS * p + max(0, x - 3))
                                pe.matmul(bS[:, x % 4, 0:w], same[:], kq[:, c:c + w], start=True, stop=True).then_inc(ss_mm, 1)

            @block.scalar
            def _(a):
                def evict(n, base, b, us):
                    _, col, w = BLK[b]
                    a.wait_ge(mm, base + n + 1)
                    nc.scalar.copy(u[:, us, col:col + w], bU[:, n % 4, 0:w]).then_inc(ev, 1)

                def middle(us, zs, tile, jobs, stored):
                    a.wait_ge(ev, jobs)
                    a.wait_ge(z_st[zs], stored)
                    nc.scalar.activation(z[:, zs, :], u[:, us, 1:T + 3], ACT.Identity, scale=shift[:, 1, tile]).then_inc(z1, 1)

                a.wait_ge(set_up, 1)
                a.wait_ge(c_l, 16 * 5)
                for i in range(2):
                    for b in range(NB):
                        evict(i * NB + b, 0, b, i)
                    middle(i, i, slice((O_WD0 // P) + i, (O_WD0 // P) + i + 1), (i + 1) * NB, 0)
                a.wait_ge(z_done, 1)
                nc.scalar.activation(z[:, 0, :], z[:, 0, :], ACT.Tanh).then_inc(t_done, 1)
                with a.Fori(0, PAIRS) as p:
                    base = PRE + PB * p
                    for i in range(3):
                        us = i % 2
                        a.wait_ge(z_done, 3 * p + max(2, i + 1))
                        for b in range(NB):
                            evict(NB * i + b, base, b, us)
                        z_before = (32 * (2 * p + 1) + (32 if i == 2 else 0)) if zslot(i) == 0 else 32 * (p + 1)
                        if i == 2:
                            a.wait_ge(kk_done, p + 1)
                        middle(us, zslot(i), bass.ds(p + (0, KD, O_R0 // P)[i], 1), base + NB * (i + 1), z_before)
                        if i == 0:
                            a.wait_ge(z_done, 3 * p + 3)
                            a.wait_ge(ss_mm, NS * p)
                            nc.scalar.activation(kq[:], z[:, 0, :], ACT.Square, scale=k_k[:, bass.ds(p, 1)]).then_inc(kq_done, 1)
                        if i == 1:
                            a.wait_ge(kk_done, p)
                            for x, (c, w) in enumerate(SBLK):
                                a.wait_ge(ss_mm, NS * p + x + 1)
                                nc.scalar.activation(rn[:, c:c + w], bS[:, x % 4, 0:w], ACT.Sqrt).then_inc(root, 1)
                    a.wait_ge(gs_st, 16 * p)
                    for b in range(1, NB):
                        n = 3 * NB + b - 1
                        a.wait_ge(mm, base + n + 1)
                        nc.scalar.activation(gs[:, BLK[b][0] - CTX:BLK[b][0] - CTX + 512], bU[:, n % 4, :], ACT.Silu).then_inc(ev, 1)

            @block.vector
            def _(v):
                def shift_taps(us, zs, tile, n, dn):
                    v.wait_ge(z1, n + 1)
                    nc.vector.scalar_tensor_tensor(out=z[:, zs, :], in0=u[:, us, 0:TZ], scalar=shift[:, 0, tile],
                                                   in1=z[:, zs, :], op0=ALU.mult, op1=ALU.add).then_inc(dchain, 1)
                    v.wait_ge(dchain, dn + 1)
                    nc.vector.scalar_tensor_tensor(out=z[:, zs, :], in0=u[:, us, 2:T + 4], scalar=shift[:, 2, tile],
                                                   in1=z[:, zs, :], op0=ALU.mult, op1=ALU.add).then_inc(z_done, 1)

                nc.vector.memset(u[:], 0.0).then_inc(set_up, 1)
                v.wait_ge(c_l, 16 * 5)
                for i in range(2):
                    shift_taps(i, i, slice((O_WD0 // P) + i, (O_WD0 // P) + i + 1), i, i)
                with v.Fori(0, PAIRS) as p:
                    links = 2 + 5 * p
                    for i in range(3):
                        shift_taps(i % 2, zslot(i), bass.ds(p + (0, KD, O_R0 // P)[i], 1), 2 + 3 * p + i, links + i + (2 if i == 2 else 0))
                        if i == 1:
                            v.wait_ge(root, NS * (p + 1))
                            nc.vector.tensor_scalar(rn[:], rn[:], 1e-12, None, ALU.max).then_inc(dchain, 1)
                            v.wait_ge(dchain, links + 3)
                            nc.vector.reciprocal(rn[:], rn[:]).then_inc(dchain, 1)
                            v.wait_ge(dchain, links + 4)
                            v.wait_ge(kk_st, 32 * p)
                            nc.vector.scalar_tensor_tensor(out=kk[:], in0=z[:, 0, :], scalar=k_k[:, bass.ds(p, 1)], in1=rn[:],
                                                           op0=ALU.mult, op1=ALU.mult).then_inc(kk_done, 1)


def rwkv(nc, sem, keep, A, W):
    with ExitStack() as stack:
        core = Core(nc, stack, "rw")
        NBODY = PAIRS * NG
        PER_LOAD = 6
        x4 = [P, 2, NCH, P]
        zin = core.sb("zin", [P, 2, 2, 4, GT])
        wl = core.sb("wl", [P, 2, 2, 2, P])
        lora = core.sb("lora", [P, 2, T])
        par = core.sb("par", [P, PAIRS, 7])
        cur = core.sb("cur", [P, 7])
        tri = core.sb("tri", [P, 2, 2, P])
        level = core.sb("level", [P, 2, 6, P], I32)
        same = core.sb("same", [P, P])
        reset = core.sb("reset", [P, 2, GT])
        flag = core.sb("flag", [P, NBODY])
        ee = core.sb("ee", [P, 2, 2, GT])
        cs, cx, ep, en, ex, t1, kd, b0, q, bv = (core.sb(n, [P, 2, GT]) for n in (
            "cs", "cx", "ep", "en", "ex", "t1", "kd", "b0", "q", "bv"))
        AR = core.sb("AR", [P, 2, NCH, 2, C])
        Kbd, Bbd, Vbd = (core.sb(n, x4) for n in ("Kbd", "Bbd", "Vbd"))
        X, Pm = (core.sb(n, x4) for n in ("X", "Pm"))
        Abd, Rbd = core.sb("Abd", [P, 2, 2, NCH, P]), core.sb("Rbd", [P, 2, 2, NCH, P])
        Kt, Bt, Vt, XT = (core.sb(n, [P, 2, 2, NCH, P]) for n in ("Kt", "Bt", "Vt", "XT"))
        NB_ = core.sb("NB", [P, 2, 2, NCH, 2, P])
        KK_ = core.sb("KK", [P, 2, 2, NCH, 2, P])
        dec = core.sb("dec", [P, 2, 2, NCH])
        S, sd = core.sb("S", [P, 2, P]), core.sb("Sdec", [P, 2, P])
        sd_done = [sem(f"rw_s_decayed{d}") for d in range(2)]
        r1, sa = core.sb("r1", [P, 2, P]), core.sb("sa", [P, 2, P])
        ysb = core.sb("ysb", x4)
        bank = [core.ps(f"bank{i}", [P, 512]) for i in range(8)]

        c_l, t_l, lora_l = sem("rw_consts_loaded"), sem("rw_tables_loaded"), sem("rw_first_lora_loaded")
        in_l = [sem(f"rw_in{i}_loaded") for i in range(2)]
        set_up, blocks_set, par_done = sem("rw_setup"), sem("rw_blocks_setup"), sem("rw_params")
        cur_done, lora_mm, ee_done, cs_done, cx_done = (sem(f"rw_{n}") for n in ("cur", "lora_mm", "ee", "cs", "cx"))
        ep_done, ex_done, ar_done, kb_done = (sem(f"rw_{n}") for n in ("ep_en", "ex", "ar", "kb"))
        bd_done, vbd_done, dec_part, dec_done = (sem(f"rw_{n}") for n in ("ar_per_head", "v_per_head", "dec_parts", "dec"))
        q_done, bon_mm, bv_done, bv_st = (sem(f"rw_{n}") for n in ("q", "bonus_mm", "bv", "bv_stored"))
        dch = sem("rw_dve_chain")
        tr_mm, tr_out = sem("rw_turned"), sem("rw_turned_out")
        sc_mm, sc_out = sem("rw_scores"), sem("rw_scores_out")
        xt_id, x_tr, x_in, p_mm, p_out, qt_mm, xt_up = ([sem(f"rw_{n}{d}") for d in range(2)] for n in (
            "xt_identity", "x_turned", "x_in", "p_mm", "p_out", "qt_mm", "xt_up"))
        r1_mm, r1_out, sa_mm, sa_out, s_mm, s_out, y_mm, y_out, y_st = ([sem(f"rw_{n}{d}") for d in range(2)] for n in (
            "r1_mm", "r1_out", "sa_mm", "sa_out", "s_mm", "s_out", "y_mm", "y_out", "y_stored"))
        settled = [sem(f"rw_settled{i}") for i in range(3)]
        EL = 4
        LEVELS = 6

        def pos(d, c):
            return c if d == 0 else NCH - 1 - c

        def tokens(m, d):
            g = m % NG
            return g * GT if d == 0 else ((NG - g) % NG) * GT

        def span(first, size):
            return slice(first, first + size) if isinstance(first, int) else bass.ds(first, size)

        def inputs_loaded(m, s):
            return (m - s) * 8 * PER_LOAD + 16 * PER_LOAD

        def bodies(fori, one):
            with fori(0, NBODY // 2 - 1) as i:
                one(2 * i, 0, True, True)
                one(2 * i + 1, 1, True, True)
            one(NBODY - 2, 0, True, False)
            one(NBODY - 1, 1, False, False)

        with nc.Block() as block:
            @block.sync
            def _(sp):
                def load(m, s):
                    p = m // NG
                    for d in range(2):
                        src = W["heads"][span(p, 1), :, :, span(tokens(m, d), GT)].rearrange("a c f t -> (a c) f t")
                        sp.dma_start(zin[:, s, d], src).then_inc(in_l[s], 16)
                        for i, name in enumerate(("o_w2", "o_a2")):
                            sp.dma_start(wl[HP * d:HP * d + HP, s, i, d, :], A[name][0, d, :, span(p * P, P)]).then_inc(in_l[s], 16)

                def store_bonus(m):
                    sp.wait_ge(bv_done, m + 1)
                    if not isinstance(m, int):
                        settle(sp, settled[2])
                    for d in range(2):
                        sp.dma_start(W["bv"][d, span((m // NG) * P, P), span(tokens(m, d), GT)], bv[:, d]).then_inc(bv_st, 16)

                def body(n, s, has_load, has_after):
                    if has_load:
                        sp.wait_ge(bv_done, n + 2)
                        sp.wait_ge(ar_done, 2 * n + 4)
                        sp.wait_ge(vbd_done, 2 * n + 4)
                        load(n + 3, 1 - s)
                    if has_after:
                        store_bonus(n + 2)
                    for d in range(2):
                        sp.wait_ge(y_out[d], 4 * n + 4)
                        if not isinstance(n, int):
                            settle(sp, settled[2])
                        for h in range(2):
                            dst = W["y"][d, span(tokens(n, d), GT), span((n // NG) * P + HP * h, HP)]
                            sp.dma_start(dst.rearrange("(c t) v -> t c v", t=C),
                                         ysb[HP * h:HP * h + HP, d, :, C * h:C * h + C]).then_inc(y_st[d], 16)

                sp.dma_start(lora[:, :, 0:GT], W["lora"][:, :, 0:GT].rearrange("i c t -> c i t")).then_inc(lora_l, 16)
                with nc.allow_non_contiguous_dma("short vectors as columns"):
                    for d in range(2):
                        sp.dma_start(par[:, :, d], A["o_w0"][0, d].rearrange("(k p) -> p k", p=P)).then_inc(c_l, 16)
                        sp.dma_start(par[:, :, 2 + d], A["o_a0"][0, d].rearrange("(k p) -> p k", p=P)).then_inc(c_l, 16)
                    sp.dma_start(par[:, :, 4], A["o_k_a"][0].rearrange("(k p) -> p k", p=P)).then_inc(c_l, 16)
                    sp.dma_start(par[:, :, 6], A["o_r_k"][0].rearrange("(k h) c -> (h c) k", h=2)).then_inc(c_l, 16)
                sp.wait_ge(set_up, 1)
                load(0, 0)
                for dst, name in ((reset, "reset"), (same, "same"), (flag, "flag")):
                    sp.dma_start(dst[:], A[name]).then_inc(c_l, 16)
                load(1, 1)
                for dst, name in ((tri, "tri"), (level, "level")):
                    sp.dma_start(dst[:], A[name]).then_inc(t_l, 16)
                sp.dma_start(lora[:, :, GT:], W["lora"][:, :, GT:].rearrange("i c t -> c i t")).then_inc(t_l, 16)
                store_bonus(0)
                sp.wait_ge(ar_done, 2)
                sp.wait_ge(vbd_done, 2)
                load(2, 0)
                store_bonus(1)
                with sp.Fori(0, NBODY // 2 - 2) as i:
                    body(2 * i, 0, True, True)
                    body(2 * i + 1, 1, True, True)
                body(NBODY - 4, 0, True, True)
                body(NBODY - 3, 1, False, True)
                body(NBODY - 2, 0, False, False)
                body(NBODY - 1, 1, False, False)
                sp.wait_ge(bv_st, 32 * NBODY)
                for d in range(2):
                    sp.wait_ge(y_st[d], 32 * NBODY)

            @block.gpsimd
            def _(g):
                def per_head(m, s):
                    g.wait_ge(ar_done, 2 * m + 2)
                    if not (isinstance(m, int) and m == 0):
                        for d in range(2):
                            g.wait_ge(y_mm[d], 4 * m - 4)
                    link = Link(g, bd_done, 4 * m)
                    for x, dst in enumerate((Abd, Rbd)):
                        for h in range(2):
                            rows, cols = slice(HP * h, HP * h + HP), slice(C * h, C * h + C)
                            settle(g, settled[1])
                            link(nc.gpsimd.tensor_copy(dst[rows, s, :, :, cols], AR[rows, :, :, x, :]))

                def operands(m, s):
                    g.wait_ge(cs_done, 2 * m + 2)
                    g.wait_ge(ex_done, m)
                    nc.gpsimd.tensor_tensor(cx[:], cs[:], ee[:, 0], ALU.subtract).then_inc(cx_done, 1)
                    g.wait_ge(cx_done, m + 1)
                    g.wait_ge(in_l[s], inputs_loaded(m, s))
                    g.wait_ge(tr_mm, 6 * m)
                    link = Link(g, vbd_done, 2 * m)
                    for h in range(2):
                        rows, cols = slice(HP * h, HP * h + HP), slice(C * h, C * h + C)
                        settle(g, settled[1])
                        link(nc.gpsimd.tensor_copy(Vbd[rows, :, :, cols], zin[rows, s, :, 3, :].rearrange("p d (c t) -> p d c t", t=C)))

                for x in (NB_, KK_):
                    nc.gpsimd.memset(x[:], 0.0).then_inc(blocks_set, 1)
                    g.wait_ge(blocks_set, 1 if x is NB_ else 2)
                g.wait_ge(set_up, 7)
                operands(0, 0)
                per_head(0, 0)
                operands(1, 1)

                def body(n, s, has_next, has_after):
                    if has_next:
                        per_head(n + 1, 1 - s)
                    if has_after:
                        operands(n + 2, s)

                bodies(g.Fori, body)

            @block.tensor
            def _(pe):
                ident = keep["ident"]

                def low_rank(m, s):
                    pe.wait_ge(in_l[s], inputs_loaded(m, s))
                    if not (isinstance(m, int) and m == 0):
                        for d in range(2):
                            pe.wait_ge(xt_up[d], LEVELS * m - LEVELS)
                    for i in range(2):
                        for d in range(2):
                            last = pe.matmul(bank[6 + i][:, GT * d:GT * (d + 1)], wl[:, s, i, d, :],
                                             lora[:, i, span(tokens(m, d), GT)], start=True, stop=True)
                    last.then_inc(lora_mm, 1)

                def bonus(m):
                    pe.wait_ge(q_done, m + 1)
                    pe.wait_ge(ee_done, m + 1)
                    if not (isinstance(m, int) and m == 0):
                        pe.wait_ge(xt_up[0], LEVELS * m - 1)
                    pe.matmul(bank[6][:], same[:], q[:].rearrange("p d t -> p (d t)"), start=True, stop=True).then_inc(bon_mm, 1)

                def turn(m, i):
                    if i == 0:
                        pe.wait_ge(kb_done, m + 1)
                        for d in range(2):
                            pe.wait_ge(p_out[d], 5 * m)
                    if i == 2:
                        pe.wait_ge(vbd_done, 2 * m + 2)
                    src = (Kbd, Bbd, Vbd)[i]
                    for d in range(2):
                        if i:
                            pe.wait_ge(tr_out, 6 * m + 2 * i + d - 1)
                        for c in range(NCH):
                            last = pe.transpose(bank[4 + d][:, c * P:(c + 1) * P], src[:, d, c, :], ident[:])
                        last.then_inc(tr_mm, 1)

                def scores(m, x, rates_next):
                    for d in range(2):
                        if x == 0:
                            pe.wait_ge(ar_done, 2 * m + 2)
                            if rates_next:
                                pe.wait_ge(ee_done, m + 2)
                            else:
                                pe.wait_ge(xt_up[d], LEVELS * m)
                        else:
                            pe.wait_ge(tr_out, 6 * m + 6)
                        for c in range(NCH):
                            last = pe.matmul(bank[(6, 4)[x] + d][:, c * P:(c + 1) * P], (Bbd, Kbd)[x][:, d, c, :],
                                             AR[:, d, c].rearrange("p a b -> p (a b)"), start=True, stop=True)
                        last.then_inc(sc_mm, 1)

                def first_x(m, t):
                    for d in range(2):
                        pe.wait_ge(xt_up[d], LEVELS * m + 1)
                        for c in range(NCH):
                            last = pe.transpose(bank[6 + d][:, c * P:(c + 1) * P], XT[:, t, d, c, :], ident[:])
                        last.then_inc(x_tr[d], 1)

                def level_p(m, t, k):
                    for d in range(2):
                        if k == 1:
                            pe.wait_ge(sc_out, 8 * m + 6 + 2 * d)
                        pe.wait_ge(x_in[d], 5 * m + k)
                        for c in range(NCH):
                            last = pe.matmul(bank[4 + d][:, c * P:(c + 1) * P], NB_[:, t, d, c, 0, :], X[:, d, c, :], start=True, stop=True)
                        last.then_inc(p_mm[d], 1)

                def level_q(m, t, k, bonus_before=False):
                    for d in range(2):
                        if bonus_before:
                            pe.wait_ge(bv_done, m + 2)
                        pe.wait_ge(p_out[d], 5 * m + k)
                        for c in range(NCH):
                            last = pe.matmul(bank[6 + d][:, c * P:(c + 1) * P], Pm[:, d, c, :], XT[:, t, d, c, :], start=True, stop=True)
                        last.then_inc(qt_mm[d], 1)

                def level_x(m, t, k):
                    for d in range(2):
                        pe.wait_ge(xt_up[d], LEVELS * m + k + 1)
                        for c in range(NCH):
                            last = pe.transpose(bank[4 + d][:, c * P:(c + 1) * P], XT[:, t, d, c, :], ident[:])
                        last.then_inc(x_tr[d], 1)

                def step_begin(n, s, c):
                    for d in range(2):
                        u = pos(d, c)
                        pe.wait_ge(s_out[d], 4 * n + c)
                        if c == 0:
                            pe.wait_ge(bd_done, 4 * n + 4)
                            pe.wait_ge(xt_up[d], LEVELS * n + LEVELS)
                        pe.matmul(bank[d][:, 0:P], Abd[:, s, d, u, :], S[:, d, :], start=True, stop=False)
                        pe.matmul(bank[d][:, 0:P], KK_[:, s, d, u, 0, :], Vt[:, s, d, u, :], start=False, stop=True).then_inc(r1_mm[d], 1)
                    for d in range(2):
                        u = pos(d, c)
                        pe.wait_ge(y_out[d], 4 * n + c)
                        pe.matmul(bank[2 + d][:, 0:P], Rbd[:, s, d, u, :], S[:, d, :], start=True, stop=False, skip_group_check=True)
                        pe.matmul(bank[2 + d][:, 0:P], KK_[:, s, d, u, 1, :], Vt[:, s, d, u, :], start=False, stop=False, skip_group_check=True)
                        pe.matmul(bank[2 + d][:, P:2 * P], Kt[:, s, d, u, :], Vt[:, s, d, u, :], start=False, stop=False, skip_group_check=True)

                def step_sa(n, s, c):
                    for d in range(2):
                        pe.wait_ge(r1_out[d], 4 * n + c + 1)
                        pe.matmul(bank[d][:, P:2 * P], XT[:, s, d, pos(d, c), :], r1[:, d, :], start=True, stop=True).then_inc(sa_mm[d], 1)

                def step_end(n, s, c):
                    for d in range(2):
                        u = pos(d, c)
                        pe.wait_ge(sa_out[d], 4 * n + c + 1)
                        pe.matmul(bank[2 + d][:, P:2 * P], Bt[:, s, d, u, :], sa[:, d, :], start=False, stop=True, skip_group_check=True).then_inc(s_mm[d], 1)
                        pe.matmul(bank[2 + d][:, 0:P], NB_[:, s, d, u, 1, :], sa[:, d, :], start=False, stop=True, skip_group_check=True).then_inc(y_mm[d], 1)

                pe.wait_ge(lora_l, 16)
                low_rank(0, 0)
                pe.wait_ge(c_l, 16 * 9)
                bonus(0)
                turn(0, 0)
                pe.wait_ge(t_l, 16 * 3)
                pe.wait_ge(bv_done, 1)
                low_rank(1, 1)
                turn(0, 1)
                scores(0, 0, True)
                turn(0, 2)
                scores(0, 1, True)
                first_x(0, 0)
                for k in range(1, LEVELS - 1):
                    level_p(0, 0, k)
                    level_q(0, 0, k)
                    level_x(0, 0, k)
                bonus(1)
                level_p(0, 0, 5)
                level_q(0, 0, 5, True)

                def body(n, s, has_next, has_after):
                    m, t = n + 1, 1 - s
                    if has_next:
                        turn(m, 0)
                    if has_after:
                        low_rank(n + 2, s)
                    step_begin(n, s, 0)
                    if has_next:
                        turn(m, 1)
                    step_sa(n, s, 0)
                    if has_next:
                        scores(m, 0, has_after)
                    step_end(n, s, 0)
                    if has_next:
                        turn(m, 2)
                    step_begin(n, s, 1)
                    if has_next:
                        scores(m, 1, has_after)
                    step_sa(n, s, 1)
                    if has_next:
                        first_x(m, t)
                    step_end(n, s, 1)
                    if has_next:
                        level_p(m, t, 1)
                        level_q(m, t, 1)
                    step_begin(n, s, 2)
                    if has_next:
                        level_x(m, t, 1)
                        level_p(m, t, 2)
                        level_q(m, t, 2)
                    step_sa(n, s, 2)
                    if has_next:
                        level_x(m, t, 2)
                        level_p(m, t, 3)
                        level_q(m, t, 3)
                    step_end(n, s, 2)
                    if has_next:
                        level_x(m, t, 3)
                        level_p(m, t, 4)
                        level_q(m, t, 4)
                    step_begin(n, s, 3)
                    if has_next:
                        level_x(m, t, 4)
                    if has_after:
                        bonus(n + 2)
                    step_sa(n, s, 3)
                    if has_next:
                        level_p(m, t, 5)
                    step_end(n, s, 3)
                    if has_next:
                        level_q(m, t, 5, has_after)

                bodies(pe.Fori, body)

            @block.scalar
            def _(a):
                def rates(m):
                    a.wait_ge(lora_mm, m + 1)
                    a.wait_ge(cur_done, m + 1)
                    a.wait_ge(ar_done, 2 * m)
                    a.wait_ge(kb_done, m)
                    a.wait_ge(cx_done, m)
                    for i in range(2):
                        for d in range(2):
                            last = nc.scalar.activation(ee[:, i, d], bank[6 + i][:, GT * d:GT * (d + 1)], ACT.Tanh, scale=0.5,
                                                        bias=cur[:, 2 * i + d:2 * i + d + 1])
                    last.then_inc(ee_done, 1)

                def decays(m):
                    a.wait_ge(cs_done, 2 * m + 2)
                    a.wait_ge(dec_done, m)
                    nc.scalar.activation(ep[:], cs[:], ACT.Exp, scale=-KAPPA)
                    nc.scalar.activation(en[:], cs[:], ACT.Exp, scale=KAPPA).then_inc(ep_done, 1)

                def decay_before(m):
                    a.wait_ge(cx_done, m + 1)
                    nc.scalar.activation(ex[:], cx[:], ACT.Exp, scale=-KAPPA).then_inc(ex_done, 1)

                def turned(m, t, i):
                    dst = (Kt, Bt, Vt)[i]
                    if not (isinstance(m, int) and m == 0):
                        for d in range(2):
                            a.wait_ge(y_mm[d], 4 * m - 4)
                    for d in range(2):
                        a.wait_ge(tr_mm, 6 * m + 2 * i + d + 1)
                        nc.scalar.copy(dst[:, t, d].rearrange("p c t -> p (c t)"), bank[4 + d][:]).then_inc(tr_out, 1)

                def take_x(m, k):
                    for d in range(2):
                        a.wait_ge(x_tr[d], 5 * m + k + 1)
                        nc.scalar.copy(X[:, d].rearrange("p c t -> p (c t)"), bank[(4 if k else 6) + d][:]).then_inc(x_in[d], 1)

                def take_p(m, k):
                    for d in range(2):
                        a.wait_ge(p_mm[d], 5 * m + k)
                        a.wait_ge(qt_mm[d], 5 * m + k - 1)
                        nc.scalar.copy(Pm[:, d].rearrange("p c t -> p (c t)"), bank[4 + d][:]).then_inc(p_out[d], 1)

                def take_r1(n, c):
                    for d in range(2):
                        a.wait_ge(r1_mm[d], 4 * n + c + 1)
                        nc.scalar.copy(r1[:, d, :], bank[d][:, 0:P]).then_inc(r1_out[d], 1)

                def take_sa(n, c):
                    for d in range(2):
                        a.wait_ge(sa_mm[d], 4 * n + c + 1)
                        nc.scalar.copy(sa[:, d, :], bank[d][:, P:2 * P]).then_inc(sa_out[d], 1)

                def take_y(n, c):
                    for d in range(2):
                        a.wait_ge(y_mm[d], 4 * n + c + 1)
                        a.wait_ge(s_out[d], 4 * n + c + 1)
                        if c == 0:
                            a.wait_ge(y_st[d], 32 * n)
                        nc.scalar.copy(ysb[:, d, pos(d, c), :], bank[2 + d][:, 0:P]).then_inc(y_out[d], 1)

                rates(0)
                decays(0)
                decay_before(0)
                turned(0, 0, 0)
                rates(1)
                turned(0, 0, 1)
                turned(0, 0, 2)
                decays(1)
                decay_before(1)
                take_x(0, 0)
                for k in range(1, LEVELS):
                    take_p(0, k)
                    if k < LEVELS - 1:
                        take_x(0, k)

                def body(n, s, has_next, has_after):
                    m, t = n + 1, 1 - s
                    if has_next:
                        turned(m, t, 0)
                    if has_after:
                        rates(n + 2)
                    take_r1(n, 0)
                    if has_next:
                        turned(m, t, 1)
                    take_sa(n, 0)
                    take_y(n, 0)
                    if has_next:
                        turned(m, t, 2)
                    take_r1(n, 1)
                    take_sa(n, 1)
                    if has_next:
                        take_x(m, 0)
                    if has_next:
                        take_p(m, 1)
                    take_y(n, 1)
                    if has_after:
                        decays(n + 2)
                    take_r1(n, 2)
                    if has_next:
                        take_x(m, 1)
                    if has_after:
                        decay_before(n + 2)
                    if has_next:
                        take_p(m, 2)
                    take_sa(n, 2)
                    if has_next:
                        take_x(m, 2)
                        take_p(m, 3)
                        take_x(m, 3)
                    take_y(n, 2)
                    if has_next:
                        take_p(m, 4)
                    take_r1(n, 3)
                    if has_next:
                        take_x(m, 4)
                    take_sa(n, 3)
                    if has_next:
                        take_p(m, 5)
                    take_y(n, 3)

                bodies(a.Fori, body)

            @block.vector
            def _(v):
                one_minus = par[:, :, 5]
                by_chunk = lambda x: x.rearrange("p d (c t) -> p d c t", t=C)

                def decay_of_chunks(m, t):
                    for d in range(2):
                        v.wait_ge(s_out[d], 4 * m - 4 if not isinstance(m, int) else max(4 * m - 4, 0))
                    v.wait_ge(ep_done, m + 1)
                    nc.vector.tensor_copy(dec[:, t, 0, :], ep[:, 0, C - 1::C]).then_inc(dec_part, 1)
                    nc.vector.tensor_copy(dec[:, t, 1, ::-1], ep[:, 1, ::C]).then_inc(dec_part, 1)
                    v.wait_ge(dec_part, 2 * m + 2)
                    nc.vector.tensor_scalar(dec[:, t, :, NCH - 1], dec[:, t, :, NCH - 1], flag[:, span(m, 1)], None, ALU.mult).then_inc(dec_done, 1)

                def parameters(m):
                    v.wait_ge(ee_done, m)
                    v.wait_ge(q_done, m)
                    nc.vector.tensor_copy(cur[:], par[:, span(m // NG, 1), :].rearrange("p a b -> p (a b)")).then_inc(cur_done, 1)

                def sums(m, link):
                    v.wait_ge(ee_done, m + 1)
                    link(nc.vector.tensor_scalar(ee[:], ee[:], 0.5, 0.5, ALU.mult, ALU.add))
                    v.wait_ge(ep_done, m)
                    v.wait_ge(cx_done, m)
                    nc.vector.tensor_tensor_scan(cs[:, 0, :], reset[:, 0, :], ee[:, 0, 0, :], 0.0, ALU.mult, ALU.add).then_inc(cs_done, 1)
                    nc.vector.tensor_tensor_scan(cs[:, 1, ::-1], reset[:, 1, ::-1], ee[:, 0, 1, ::-1], 0.0, ALU.mult, ALU.add).then_inc(cs_done, 1)

                def keys(m, s, link):
                    v.wait_ge(in_l[s], inputs_loaded(m, s))
                    link(nc.vector.tensor_scalar(t1[:], ee[:, 1], cur[:, 4:5], cur[:, 5:6], ALU.mult, ALU.add))
                    link(nc.vector.tensor_tensor(kd[:], t1[:], zin[:, s, :, 0, :], ALU.mult))
                    link(nc.vector.scalar_tensor_tensor(out=b0[:], in0=ee[:, 1], scalar=-1.0, in1=zin[:, s, :, 1, :], op0=ALU.mult, op1=ALU.mult))
                    v.wait_ge(bon_mm, m)
                    nc.vector.scalar_tensor_tensor(out=q[:], in0=zin[:, s, :, 2, :], scalar=cur[:, 6:7], in1=kd[:],
                                                   op0=ALU.mult, op1=ALU.mult).then_inc(q_done, 1)

                def queries(m, s):
                    v.wait_ge(ep_done, m + 1)
                    v.wait_ge(ex_done, m + 1)
                    v.wait_ge(sc_mm, 4 * m)
                    v.wait_ge(bd_done, 4 * m)
                    nc.vector.tensor_tensor(AR[:, :, :, 1, :], by_chunk(ep[:]), by_chunk(zin[:, s, :, 2, :]), ALU.mult).then_inc(ar_done, 1)
                    nc.vector.tensor_tensor(AR[:, :, :, 0, :], by_chunk(ex[:]), by_chunk(zin[:, s, :, 1, :]), ALU.mult).then_inc(ar_done, 1)

                def weights(m):
                    v.wait_ge(sc_mm, 4 * m)
                    for src, dst in ((kd, Kbd), (b0, Bbd)):
                        for h in range(2):
                            rows, cols = slice(HP * h, HP * h + HP), slice(C * h, C * h + C)
                            last = nc.vector.tensor_tensor(dst[rows, :, :, cols], by_chunk(src[rows]), by_chunk(en[rows]), ALU.mult)
                    last.then_inc(kb_done, 1)

                def bonus(m, s):
                    v.wait_ge(bon_mm, m + 1)
                    v.wait_ge(bv_st, 32 * m)
                    nc.vector.tensor_tensor(bv[:], bank[6][:].rearrange("p (d t) -> p d t", d=2), zin[:, s, :, 3, :], ALU.mult).then_inc(bv_done, 1)

                def carry(n, s, c):
                    for d in range(2):
                        v.wait_ge(s_out[d], 4 * n + c)
                        nc.vector.tensor_scalar(sd[:, d, :], S[:, d, :], dec[:, s, d, c:c + 1], None, ALU.mult).then_inc(sd_done[d], 1)
                    for d in range(2):
                        v.wait_ge(sd_done[d], 4 * n + c + 1)
                        v.wait_ge(s_mm[d], 4 * n + c + 1)
                        v.wait_ge(y_mm[d], 4 * n + c + 1)
                        nc.vector.scalar_tensor_tensor(out=S[:, d, :], in0=bank[2 + d][:, P:2 * P], scalar=dec[:, s, d, c:c + 1],
                                                       in1=sd[:, d, :], op0=ALU.mult, op1=ALU.add).then_inc(s_out[d], 1)

                def masks(m, t, x, d):
                    for e in range(2):
                        v.wait_ge(y_mm[e], 4 * m - 4 if not isinstance(m, int) else max(4 * m - 4, 0))
                    v.wait_ge(sc_mm, 4 * m + 2 * x + d + 1)
                    for h in range(2):
                        rows, cols = slice(HP * h, HP * h + HP), slice(C * h, C * h + C)
                        nc.vector.tensor_tensor(
                            (NB_, KK_)[x][rows, t, d, :, :, cols],
                            bank[(6, 4)[x] + d][rows, :].rearrange("p (c a t) -> p c a t", c=NCH, a=2),
                            tri[rows, d, None, :, cols].broadcast_to([HP, NCH, 2, C]), ALU.mult).then_inc(sc_out, 1)

                def start(m, t, d):
                    nc.vector.tensor_copy(XT[:, t, d], keep["ident"][:, None, :].broadcast_to([P, NCH, P])).then_inc(xt_id[d], 1)
                    v.wait_ge(xt_id[d], m + 1)
                    v.wait_ge(sc_out, 8 * m + 2 * d + 2)
                    settle(v, settled[0])
                    nc.vector.copy_predicated(XT[:, t, d], level[:, d, 0, None, :].broadcast_to([P, NCH, P]), NB_[:, t, d, :, 0, :]).then_inc(xt_up[d], 1)

                def double(m, t, k):
                    for d in range(2):
                        v.wait_ge(qt_mm[d], 5 * m + k)
                        v.wait_ge(xt_up[d], LEVELS * m + k)
                        settle(v, settled[0])
                        nc.vector.copy_predicated(XT[:, t, d], level[:, d, k, None, :].broadcast_to([P, NCH, P]),
                                                  bank[6 + d][:].rearrange("p (c t) -> p c t", c=NCH)).then_inc(xt_up[d], 1)

                for x in (wl, Kbd, Bbd, Vbd, S, Abd, Rbd):
                    nc.vector.memset(x[:], 0.0).then_inc(set_up, 1)
                v.wait_ge(set_up, 7)
                v.wait_ge(c_l, 16 * 9)
                nc.vector.tensor_scalar(one_minus, par[:, :, 4], -1.0, 1.0, ALU.mult, ALU.add).then_inc(par_done, 1)
                nc.vector.tensor_scalar(par[:, :, 0:4], par[:, :, 0:4], 0.5, None, ALU.mult).then_inc(par_done, 1)
                v.wait_ge(par_done, 2)

                link = Link(v, dch, 0)
                parameters(0)
                sums(0, link)
                keys(0, 0, link)
                queries(0, 0)
                weights(0)
                bonus(0, 0)
                decay_of_chunks(0, 0)
                link = Link(v, dch, EL)
                parameters(1)
                sums(1, link)
                v.wait_ge(t_l, 16 * 3)
                v.wait_ge(blocks_set, 2)
                for d in range(2):
                    masks(0, 0, 0, d)
                    start(0, 0, d)
                for d in range(2):
                    masks(0, 0, 1, d)
                keys(1, 1, link)
                queries(1, 1)
                weights(1)
                for k in range(1, LEVELS - 1):
                    double(0, 0, k)
                bonus(1, 1)
                double(0, 0, LEVELS - 1)

                def body(n, s, has_next, has_after):
                    m, t = n + 1, 1 - s
                    link = Link(v, dch, EL * (n + 2))
                    if has_next:
                        decay_of_chunks(m, t)
                    if has_after:
                        parameters(n + 2)
                    v.wait_ge(dec_done, n + 1)
                    carry(n, s, 0)
                    if has_next:
                        for d in range(2):
                            masks(m, t, 0, d)
                            start(m, t, d)
                    if has_next:
                        for d in range(2):
                            masks(m, t, 1, d)
                    if has_after:
                        sums(n + 2, link)
                    carry(n, s, 1)
                    if has_after:
                        keys(n + 2, s, link)
                    if has_next:
                        double(m, t, 1)
                        double(m, t, 2)
                    if has_after:
                        queries(n + 2, s)
                    if has_next:
                        double(m, t, 3)
                    carry(n, s, 2)
                    if has_after:
                        weights(n + 2)
                    if has_next:
                        double(m, t, 4)
                    if has_after:
                        bonus(n + 2, s)
                    carry(n, s, 3)
                    if has_next:
                        double(m, t, 5)

                bodies(v.Fori, body)


def merge1(nc, sem, keep, A, W, out):
    with ExitStack() as stack:
        core = Core(nc, stack, "m1")
        NL = SEQ // P
        G = D // C
        w = core.sb("w", [P, KD, D])
        gn = core.sb("gn", [P, 2, KD])
        half = core.sb("half", [P, G])
        yin = core.sb("yin", [P, 2, 2, D])
        bin_ = core.sb("bonus", [P, 2, 2, KD, P])
        gs = core.sb("gs", [P, 2, KD, P])
        xt = core.sb("xt", [P, 2, D])
        ysum, yc, ysq = (core.sb(n, [P, G, C]) for n in ("ysum", "yc", "ysq"))
        mu, nmu, ss, ms, rs = (core.sb(n, [P, G]) for n in ("mu", "nmu", "ss", "ms", "rs"))
        yn = core.sb("yn", [P, 2, D])
        nT, bsum, mT = (core.sb(n, [P, KD, P]) for n in ("nT", "bsum", "mT"))
        oT = core.sb("oT", [P, 2, KD, P])
        gy = core.sb("gy", [P, D])
        xo = core.sb("xo", [P, 2, D])
        bT = [core.ps(f"bT{i}", [P, 512]) for i in range(2)]
        bY = core.ps("bY", [P, 4, 512])
        c_l, w_l = sem("m1_consts_loaded"), sem("m1_w_loaded")
        y_l, b_l, x_l, x_st = ([sem(f"m1_{n}{i}") for i in range(2)] for n in ("y_loaded", "bonus_loaded", "x_loaded", "x_stored"))
        dch, half_set = sem("m1_dve_chain"), sem("m1_half_set")
        y_used, cen, sq, ms_done, rs_done, yn_done = (sem(f"m1_{n}") for n in ("y_used", "centred", "squared", "ms", "rs", "yn"))
        tr_mm, nT_done, bs_done, m_done, o_done = (sem(f"m1_{n}") for n in ("turned", "nT", "bonus_sum", "merged", "oT"))
        y_mm, gy_done, x_done, y_free = sem("m1_y_mm"), sem("m1_gy"), sem("m1_x"), sem("m1_y_free")
        settled = sem("m1_settled")
        ML = 3

        def rows(t, base=0):
            return slice(base + t * P, base + (t + 1) * P) if isinstance(t, int) else bass.ds(t * P + base, P)

        def iterations(fori, one):
            with fori(0, NL // 2 - 1) as i:
                one(2 * i, 0, True, True)
                one(2 * i + 1, 1, True, True)
            one(NL - 2, 0, True, False)
            one(NL - 1, 1, False, False)

        with nc.Block() as block:
            @block.sync
            def _(sp):
                def load_y(t, s):
                    for d in range(2):
                        sp.dma_start(yin[:, s, d, :], W["y"][d, rows(t, CTX), :]).then_inc(y_l[s], 16)

                def load_bonus(t, s):
                    for d in range(2):
                        sp.dma_start(bin_[:, s, d], W["bv"][d, :, rows(t, CTX)].rearrange("(k p) t -> p k t", p=P)).then_inc(b_l[s], 16)
                    sp.dma_start(gs[:, s], W["gsT"][:, :, rows(t)].rearrange("k p t -> p k t")).then_inc(b_l[s], 16)

                def load_x(t, s):
                    sp.dma_start(xt[:, s, :], W["x1"][rows(t, CTX), :]).then_inc(x_l[s], 16)

                with nc.allow_non_contiguous_dma("short vectors as columns"):
                    for i, name in enumerate(("o_gn_w", "o_gn_b")):
                        sp.dma_start(gn[:, i, :], A[name][0].rearrange("(k p) -> p k", p=P)).then_inc(c_l, 16)
                for t in range(2):
                    load_y(t, t)
                    load_bonus(t, t)
                sp.dma_start(w[:], A["o_w_out"][0].rearrange("(k p) n -> p k n", p=P)).then_inc(w_l, 16)
                for t in range(2):
                    load_x(t, t)
                for t in range(2):
                    sp.wait_ge(y_used, t + 1)
                    load_y(t + 2, t)
                sp.wait_ge(o_done, 1)
                load_bonus(2, 0)

                def one(t, s, next1, next2, next3, next4):
                    if next4:
                        sp.wait_ge(y_used, t + 3)
                        load_y(t + 4, s)
                    if next3:
                        sp.wait_ge(o_done, t + 2)
                        settle(sp, settled)
                        load_bonus(t + 3, 1 - s)
                    sp.wait_ge(x_done, t + 1)
                    sp.dma_start(out[0, rows(t), :], xo[:, s, :]).then_inc(x_st[s], 16)
                    if next2:
                        load_x(t + 2, s)

                with sp.Fori(0, NL // 2 - 2) as i:
                    one(2 * i, 0, True, True, True, True)
                    one(2 * i + 1, 1, True, True, True, True)
                one(NL - 4, 0, True, True, True, False)
                one(NL - 3, 1, True, True, False, False)
                one(NL - 2, 0, True, False, False, False)
                one(NL - 1, 1, False, False, False, False)
                for s in range(2):
                    sp.wait_ge(x_st[s], 16 * NL // 2)

            @block.gpsimd
            def _(g):
                def bonus(t, s):
                    g.wait_ge(b_l[s], (t - s) * 24 + 48)
                    g.wait_ge(m_done, t)
                    nc.gpsimd.tensor_tensor(bsum[:], bin_[:, s, 0], bin_[:, s, 1], ALU.add).then_inc(bs_done, 1)
                    g.wait_ge(bs_done, t + 1)

                def rstd(t):
                    g.wait_ge(ms_done, t + 1)
                    g.wait_ge(yn_done, t)
                    nc.gpsimd.tensor_tensor(rs[:], ms[:], half[:], ALU.pow).then_inc(rs_done, 1)
                    g.wait_ge(rs_done, t + 1)

                g.wait_ge(half_set, 1)
                rstd(0)
                rstd(1)
                bonus(0, 0)

                def one(t, s, next1, next2):
                    if next1:
                        bonus(t + 1, 1 - s)
                    if next2:
                        rstd(t + 2)

                iterations(g.Fori, one)

            @block.tensor
            def _(pe):
                def turn(t, s):
                    pe.wait_ge(yn_done, t + 1)
                    pe.wait_ge(nT_done, t)
                    for k in range(KD):
                        last = pe.transpose(bT[k // 4][:, (k % 4) * P:(k % 4 + 1) * P], yn[:, s, k * P:(k + 1) * P], keep["ident"][:])
                    last.then_inc(tr_mm, 1)

                def one(t, s, next1, next2):
                    if next1:
                        turn(t + 1, 1 - s)
                    pe.wait_ge(o_done, t + 1)
                    pe.wait_ge(y_free, t + 1)
                    for j in range(2):
                        for k in range(KD):
                            last = pe.matmul(bY[:, 2 * s + j, :], oT[:, s, k, :], w[:, k, j * 512:(j + 1) * 512],
                                             start=(k == 0), stop=(k == KD - 1))
                        last.then_inc(y_mm, 1)

                turn(0, 0)
                pe.wait_ge(w_l, 16)
                iterations(pe.Fori, one)

            @block.scalar
            def _(a):
                def square(t):
                    a.wait_ge(cen, t + 1)
                    a.wait_ge(ms_done, t)
                    nc.scalar.activation(ysq[:], yc[:], ACT.Square).then_inc(sq, 1)

                def evict(t):
                    a.wait_ge(tr_mm, t + 1)
                    a.wait_ge(m_done, t)
                    for k in range(KD):
                        last = nc.scalar.activation(nT[:, k, :], bT[k // 4][:, (k % 4) * P:(k % 4 + 1) * P], ACT.Identity,
                                                    scale=gn[:, 0, k:k + 1], bias=gn[:, 1, k:k + 1])
                    last.then_inc(nT_done, 1)

                square(0)
                square(1)
                a.wait_ge(c_l, 32)
                evict(0)

                def one(t, s, next1, next2):
                    if next1:
                        evict(t + 1)
                    if next2:
                        square(t + 2)

                iterations(a.Fori, one)

            @block.vector
            def _(v):
                groups = lambda small: small[:, :, None].broadcast_to([P, G, C])

                def centre(t, s, link):
                    v.wait_ge(y_l[s], (t - s) * 16 + 32)
                    nc.vector.tensor_tensor(ysum[:].rearrange("p g c -> p (g c)"), yin[:, s, 0, :], yin[:, s, 1, :], ALU.add).then_inc(y_used, 1)
                    v.wait_ge(y_used, t + 1)
                    link(nc.vector.tensor_reduce(mu[:], ysum[:], AX.X, ALU.add))
                    link(nc.vector.tensor_scalar(nmu[:], mu[:], -1.0 / C, None, ALU.mult))
                    nc.vector.tensor_tensor(yc[:], ysum[:], groups(nmu), ALU.add).then_inc(cen, 1)

                def normalise(t, s, link):
                    v.wait_ge(sq, t + 1)
                    link(nc.vector.tensor_reduce(ss[:], ysq[:], AX.X, ALU.add))
                    v.wait_ge(rs_done, t)
                    nc.vector.tensor_scalar(ms[:], ss[:], 1.0 / C, GN_EPS, ALU.mult, ALU.add).then_inc(ms_done, 1)

                def scale(t, s):
                    v.wait_ge(rs_done, t + 1)
                    v.wait_ge(cen, t + 1)
                    if not (isinstance(t, int) and t < 2):
                        v.wait_ge(tr_mm, t - 1)
                    nc.vector.tensor_tensor(yn[:, s, :].rearrange("p (g c) -> p g c", c=C), yc[:], groups(rs), ALU.mult).then_inc(yn_done, 1)

                def merge(t, s):
                    v.wait_ge(nT_done, t + 1)
                    v.wait_ge(bs_done, t + 1)
                    nc.vector.tensor_tensor(mT[:], nT[:], bsum[:], ALU.add).then_inc(m_done, 1)
                    v.wait_ge(m_done, t + 1)
                    v.wait_ge(b_l[s], (t - s) * 24 + 48)
                    if not (isinstance(t, int) and t < 2):
                        v.wait_ge(y_mm, 2 * t - 2)
                    nc.vector.tensor_tensor(oT[:, s], mT[:], gs[:, s], ALU.mult).then_inc(o_done, 1)

                def residual(t, s):
                    v.wait_ge(x_done, t)
                    for j in range(2):
                        v.wait_ge(y_mm, 2 * t + j + 1)
                        nc.vector.tensor_tensor(gy[:, j * 512:(j + 1) * 512], bY[:, 2 * s + j, :],
                                                keep["gate"][:, 2, j * 512:(j + 1) * 512], ALU.mult).then_inc(gy_done, 1)
                    v.wait_ge(gy_done, 2 * t + 2)
                    v.sem_inc(y_free, 1)
                    v.wait_ge(x_l[s], (t - s) * 8 + 16)
                    v.wait_ge(x_st[s], (t - s) * 8)
                    nc.vector.tensor_tensor(xo[:, s, :], gy[:], xt[:, s, :], ALU.add).then_inc(x_done, 1)

                nc.vector.memset(half[:], -0.5).then_inc(half_set, 1)
                v.sem_inc(y_free, 2)
                for t in range(2):
                    link = Link(v, dch, ML * t)
                    centre(t, t, link)
                    normalise(t, t, link)
                    scale(t, t)
                merge(0, 0)

                def one(t, s, next1, next2):
                    link = Link(v, dch, ML * (t + 2))
                    if next2:
                        centre(t + 2, s, link)
                    if next1:
                        merge(t + 1, 1 - s)
                    if next2:
                        normalise(t + 2, s, link)
                        scale(t + 2, s)
                    residual(t, s)

                iterations(v.Fori, one)


def clear_semaphores(nc, sems):
    with nc.Block() as block:
        @block.sync
        def _(sp):
            for one in sems:
                sp.sem_clear(one)


def program(nc, A, out):
    with ExitStack() as stack:
        first_half, second_half = ExitStack(), stack
        used = []

        def sem_of(owner):
            def sem(name):
                used.append(owner.enter_context(nc.semaphore(name)))
                return used[-1]
            return sem

        sem = sem_of(first_half)

        def keep_sb(name, shape):
            return stack.enter_context(nc.sbuf_tensor(f"keep_{name}", shape, F32))

        def scratch(name, shape):
            return nc.dram_tensor(f"scratch_{name}", shape, F32).ap()

        keep = {
            "ident": keep_sb("ident", [P, P]),
            "scale": keep_sb("scale", [P, 2, KD, 2]),
            "shift": keep_sb("shift", [P, 2, KD, 2]),
            "gate": keep_sb("gate", [P, 3, D]),
        }
        W = {
            "q": scratch("q", (HEADS, T, QK)), "k": scratch("k", (HEADS, T, QK)), "v": scratch("v", (HEADS, T, VH)),
            "gate": scratch("gate", (T, GW)), "fx": scratch("fx", (T, 2 * FW)),
            "mix": scratch("mix", (T, GW)), "z": scratch("z", (2, N2, P, FW)),
            "x1": scratch("x1", (T, D)),
            "heads": scratch("heads", (PAIRS, P, 4, T)), "gsT": scratch("gsT", (PAIRS, P, SEQ)), "lora": scratch("lora", (2, P, T)),
            "bv": scratch("bv", (2, D, T)), "y": scratch("y", (2, T, D)),
        }
        with nc.sbuf_tensor("keep_w_in", [P, KD, EVEN_IN], F32) as w_in:
            keep["w_in"], keep["w_in_loaded"] = w_in, sem("w_in_loaded")
            modulate(nc, sem, keep, A)
            project0(nc, sem, keep, A, W)
        attend(nc, sem, keep, A, W)
        fourier(nc, sem, keep, A, W)
        with nc.sbuf_tensor("keep_hT", [P, KD, T], F32) as hT:
            keep["hT"] = hT
            merge0(nc, sem, keep, A, W)
            project1(nc, sem, keep, A, W)
        clear_semaphores(nc, used)
        first_half.close()
        sem = sem_of(second_half)
        rwkv(nc, sem, keep, A, W)
        merge1(nc, sem, keep, A, W, out)


_INS = ["x", "c", "ctx", "c_ctx", "ada_w", "ada_b", "norm_g", "e_w_in", "e_kv_norm", "e_q_norm", "e_w_uq", "e_w_ukv",
        "e_q_head_norm", "e_k_head_norm", "e_w_fnet", "e_w_out", "o_w_in", "o_shift_w", "o_w0", "o_w2", "o_a0",
        "o_a2", "o_k_k", "o_k_a", "o_r_k", "o_gn_w", "o_gn_b", "o_w_out"]


def kernel(**inputs):
    import numpy as _np
    import concourse.bacc as _bacc
    from concourse import mybir as _mybir
    from concourse.bass_utils import run_bass_kernel_spmd as _run

    nc = _bacc.Bacc("TRN2", target_bir_lowering=False, num_devices=1)
    arrays, A = {}, {}
    tables = constant_tables()
    for name in _INS + list(tables):
        a = _np.ascontiguousarray(tables[name] if name in tables else inputs[name])
        arrays[f"in_{name}_dram"] = a
        A[name] = nc.dram_tensor(f"in_{name}_dram", a.shape, _mybir.dt.from_np(a.dtype), kind="ExternalInput").ap()
    out = nc.dram_tensor("out_0_dram", (1, SEQ, D), _mybir.dt.float32, kind="ExternalOutput").ap()
    program(nc, A, out)
    r = _run(nc, [arrays], core_ids=[0])
    return r.results[0]["out_0_dram"]
```
